# Optimizing a Trainium2 kernel written in Bass

```python
import jax, jax.numpy as jnp
from jax import lax
import numpy as np

'''Hybrid diffusion / flow-matching backbone: DEPTH layers over latent tokens with a context prefix.
Each layer = [sandwich-normed adaLN token-mixing sub-layer: parallel HGRN2 (bidirectional), 2-D Fourier and
chunked spatial-gating branches merged by per-channel sigmoid gates] + [sandwich-normed adaLN expert-choice SwiGLU MoE].
Inputs: x (BATCH, SEQ, D_MODEL) latent tokens; c (BATCH, D_MODEL) conditioning vector; ctx (BATCH, CTX_LEN, D_MODEL)
context tokens; c_ctx (D_MODEL,) constant context modulation vector; per-layer parameters stacked on a leading DEPTH axis.
Output: latent stream (BATCH, SEQ, D_MODEL).
'''

D_MODEL = 1024
BATCH = 1
SEQ = 1024
DEPTH = 1

CTX_LEN = 256
GRID_W = 64
A_HEADS = 4
A_HEAD_DIM = 128
A_WIDTH = A_HEADS * A_HEAD_DIM
A_CHUNK = 64
B_GROUPS = 4
B_GROUP_DIM = 128
B_WIDTH = B_GROUPS * B_GROUP_DIM
C_GROUPS = 4
C_GROUP_DIM = 128
C_WIDTH = C_GROUPS * C_GROUP_DIM
SGU_CHUNK = 128
ROWS_PER_CHUNK = SGU_CHUNK // GRID_W
N_BRANCH = 3
A_IN = 4 * A_WIDTH
IN_COLS = A_IN + A_WIDTH + B_WIDTH + 2 * C_WIDTH + N_BRANCH * D_MODEL
N_EXPERTS = 16
D_EXPERT = 1024
CAPACITY_FACTOR = 2
EPS = 1e-6
LB_FLOOR = 1e-20

kernel_name = 'hybrid_hgrn2_fourier_sgu_ecmoe_diffusion_block'

def rmsnorm(x, w):
    xf = x.astype(jnp.float32)
    y = xf * lax.rsqrt(jnp.mean(xf * xf, axis=-1, keepdims=True) + EPS)
    return (y * w.astype(jnp.float32)).astype(x.dtype)

def adaln(cvec, w, b):
    return jnp.split(jax.nn.silu(cvec) @ w + b, 6, axis=-1)

def modulate(h, shift, scale):
    return h * (1.0 + scale) + shift

def log_forget(z, lb):
    zf = z.astype(jnp.float32)
    return jnp.logaddexp(jnp.log(jnp.maximum(lb, LB_FLOOR)), jnp.log1p(-lb) + jax.nn.log_sigmoid(zf))

def hgrn_scan(q, v, log_f, s0):
    bsz, t_len, heads, _ = q.shape
    n_chunks = t_len // A_CHUNK

    def to_chunks(a):
        a = a.astype(jnp.float32).reshape(bsz, n_chunks, A_CHUNK, heads, a.shape[-1])
        return a.transpose(1, 0, 3, 2, 4)

    tri = jnp.tril(jnp.ones((A_CHUNK, A_CHUNK), dtype=bool))[:, :, None]

    def step(state, inp):
        qc, vc, lfc = inp
        kc = -jnp.expm1(lfc)
        b = jnp.cumsum(lfc, axis=2)
        o_inter = jnp.einsum('bhtk,bhkv->bhtv', qc * jnp.exp(b), state)
        diff = b[:, :, :, None, :] - b[:, :, None, :, :]
        decay = jnp.where(tri, jnp.exp(jnp.where(tri, diff, 0.0)), 0.0)
        scores = jnp.einsum('bhtk,bhsk,bhtsk->bhts', qc, kc, decay)
        o_intra = jnp.einsum('bhts,bhsv->bhtv', scores, vc)
        b_end = b[:, :, -1:, :]
        new_state = jnp.exp(b_end)[:, :, 0, :, None] * state + jnp.einsum('bhsk,bhsv->bhkv', kc * jnp.exp(b_end - b), vc)
        return new_state, o_inter + o_intra

    final_state, o = lax.scan(step, s0, (to_chunks(q), to_chunks(v), to_chunks(log_f)))
    o = o.transpose(1, 0, 3, 2, 4).reshape(bsz, t_len, heads, -1)
    return o, final_state

def hgrn_scan_inputs(z_a, lb_f, lb_b):
    bsz, t_len, _ = z_a.shape
    q, ff, fb, i = jnp.split(z_a, 4, axis=-1)
    heads = lambda a: a.reshape(bsz, t_len, A_HEADS, A_HEAD_DIM)
    return heads(jax.nn.silu(q)), log_forget(heads(ff), lb_f), log_forget(heads(fb), lb_b), heads(i)

def hgrn_bidir(q, lf_f, lf_b, v, s0_f, s0_b):
    flip = lambda a: jnp.flip(a, axis=1)
    o_f, s_f = hgrn_scan(q, v, lf_f, s0_f)
    o_b, s_b = hgrn_scan(flip(q), flip(v), flip(lf_b), s0_b)
    return o_f + flip(o_b), s_f, s_b

def fourier_mix(z):
    bsz, t_len, _ = z.shape
    zg = z.astype(jnp.float32).reshape(bsz, t_len, B_GROUPS, B_GROUP_DIM)
    out = jnp.fft.fft2(zg, axes=(1, 3), norm='ortho').real
    return out.reshape(bsz, t_len, B_WIDTH).astype(z.dtype)

def spatial_gate(u, v, w_s, b_s, norm_w, n_chunks):
    bsz, t_len, _ = u.shape
    u = jax.nn.gelu(u, approximate=False)
    v = rmsnorm(jax.nn.gelu(v, approximate=False).reshape(bsz, t_len, C_GROUPS, C_GROUP_DIM), norm_w)
    vc = v.reshape(bsz, n_chunks, SGU_CHUNK, C_GROUPS, C_GROUP_DIM)
    mixed = jnp.einsum('gpq,bnqgd->bnpgd', w_s, vc) + b_s.T[None, None, :, :, None]
    return u * mixed.reshape(bsz, t_len, C_WIDTH)

def token_mix(h, s0_f, s0_b, n_chunks, w_in, lb_f, lb_b, gnorm_w, sgu_w, sgu_b, sgu_norm_w, w_branch, w_out):
    bsz, t_len, _ = h.shape
    z = h @ w_in
    splits = np.cumsum([A_IN, A_WIDTH, B_WIDTH, C_WIDTH, C_WIDTH]).tolist()
    z_a, g_a, z_b, u, v, gates = jnp.split(z, splits, axis=-1)
    q, lf_f, lf_b, vv = hgrn_scan_inputs(z_a, lb_f, lb_b)
    o_a, s_f, s_b = hgrn_bidir(q, lf_f, lf_b, vv, s0_f, s0_b)
    o_a = rmsnorm(o_a, gnorm_w).reshape(bsz, t_len, A_WIDTH).astype(h.dtype) * jax.nn.silu(g_a)
    o_b = fourier_mix(z_b)
    o_c = spatial_gate(u, v, sgu_w, sgu_b, sgu_norm_w, n_chunks)
    g = jax.nn.sigmoid(gates).reshape(bsz, t_len, N_BRANCH, D_MODEL)
    merged = g[:, :, 0] * (o_a @ w_branch[0]) + g[:, :, 1] * (o_b @ w_branch[1]) + g[:, :, 2] * (o_c @ w_branch[2])
    return merged @ w_out, s_f, s_b

def context_states(h, w_in, lb_f, lb_b, s0):
    q, lf_f, lf_b, vv = hgrn_scan_inputs(h @ w_in[:, :A_IN], lb_f, lb_b)
    _, s_f, s_b = hgrn_bidir(q, lf_f, lf_b, vv, s0, s0)
    return s_f, s_b

def expert_choice_moe(h, router_w, w13, w2):
    bsz, t_len, d = h.shape
    cap = CAPACITY_FACTOR * t_len // N_EXPERTS
    affinity = jax.nn.softmax((h @ router_w).astype(jnp.float32), axis=-1)
    gate, idx = lax.top_k(affinity.transpose(0, 2, 1), cap)
    xe = jax.vmap(lambda hb, ib: hb[ib])(h, idx)
    a, b = jnp.split(jnp.einsum('becd,edf->becf', xe, w13), 2, axis=-1)
    y = jnp.einsum('becf,efd->becd', jax.nn.silu(a) * b, w2) * gate[..., None].astype(h.dtype)
    return jax.vmap(lambda ib, yb: jnp.zeros((t_len, d), yb.dtype).at[ib.reshape(-1)].add(yb.reshape(-1, d)))(idx, y)

def setup_inputs(seed: int = 0) -> dict:
    key = jax.random.key(seed)
    ks = jax.random.split(key, 18)
    nrm = lambda k, shape, s: jax.random.normal(k, shape, jnp.float32) * s
    return {
        'x': nrm(ks[0], (BATCH, SEQ, D_MODEL), 1.0),
        'c': nrm(ks[1], (BATCH, D_MODEL), 1.0),
        'ctx': nrm(ks[2], (BATCH, CTX_LEN, D_MODEL), 1.0),
        'c_ctx': nrm(ks[3], (D_MODEL,), 1.0),
        'ada_w': nrm(ks[4], (DEPTH, D_MODEL, 6 * D_MODEL), 0.5 * D_MODEL ** -0.5),
        'ada_b': nrm(ks[5], (DEPTH, 6 * D_MODEL), 0.02),
        'norm_w': 1.0 + nrm(ks[6], (DEPTH, 4, D_MODEL), 0.05),
        'w_in': nrm(ks[7], (DEPTH, D_MODEL, IN_COLS), D_MODEL ** -0.5),
        'hgrn_lb_raw': nrm(ks[8], (2, DEPTH, A_WIDTH), 0.5),
        'hgrn_gnorm_w': 1.0 + nrm(ks[9], (DEPTH, A_HEAD_DIM), 0.05),
        'sgu_w': nrm(ks[10], (DEPTH, C_GROUPS, SGU_CHUNK, SGU_CHUNK), SGU_CHUNK ** -0.5),
        'sgu_b': 1.0 + nrm(ks[11], (DEPTH, C_GROUPS, SGU_CHUNK), 0.05),
        'sgu_norm_w': 1.0 + nrm(ks[12], (DEPTH, C_GROUPS, C_GROUP_DIM), 0.05),
        'w_branch': nrm(ks[13], (DEPTH, N_BRANCH, A_WIDTH, D_MODEL), A_WIDTH ** -0.5),
        'w_out': nrm(ks[14], (DEPTH, D_MODEL, D_MODEL), D_MODEL ** -0.5),
        'router_w': nrm(ks[15], (DEPTH, D_MODEL, N_EXPERTS), D_MODEL ** -0.5),
        'exp_w13': nrm(ks[16], (DEPTH, N_EXPERTS, D_MODEL, 2 * D_EXPERT), D_MODEL ** -0.5),
        'exp_w2': nrm(ks[17], (DEPTH, N_EXPERTS, D_EXPERT, D_MODEL), D_EXPERT ** -0.5),
    }

def reference(x, c, ctx, c_ctx, ada_w, ada_b, norm_w, w_in, hgrn_lb_raw, hgrn_gnorm_w, sgu_w, sgu_b, sgu_norm_w, w_branch, w_out, router_w, exp_w13, exp_w2):
    rows = x.shape[1] // GRID_W
    lat_chunks = rows // ROWS_PER_CHUNK
    ctx_chunks = ctx.shape[1] // SGU_CHUNK
    p = jax.nn.softmax(hgrn_lb_raw.astype(jnp.float32), axis=1)
    lower_bounds = jnp.cumsum(p, axis=1) - p[:, :1]
    zero_state = jnp.zeros((x.shape[0], A_HEADS, A_HEAD_DIM, A_HEAD_DIM), jnp.float32)
    for l in range(DEPTH):
        last = l == DEPTH - 1
        lb_f = lower_bounds[0, l].reshape(A_HEADS, A_HEAD_DIM)
        lb_b = lower_bounds[1, l].reshape(A_HEADS, A_HEAD_DIM)
        sh1, sc1, g1, sh2, sc2, g2 = adaln(c[:, None, :], ada_w[l], ada_b[l])
        csh1, csc1, cg1, csh2, csc2, cg2 = adaln(c_ctx[None, None, :], ada_w[l], ada_b[l])
        mix_params = (w_in[l], lb_f, lb_b, hgrn_gnorm_w[l], sgu_w[l], sgu_b[l], sgu_norm_w[l], w_branch[l], w_out[l])
        h_ctx = modulate(rmsnorm(ctx, norm_w[l, 0]), csh1, csc1)
        h_lat = modulate(rmsnorm(x, norm_w[l, 0]), sh1, sc1)
        if last:
            s_f, s_b = context_states(h_ctx, w_in[l], lb_f, lb_b, zero_state)
        else:
            y_ctx, s_f, s_b = token_mix(h_ctx, zero_state, zero_state, ctx_chunks, *mix_params)
            ctx_mid = ctx + cg1 * rmsnorm(y_ctx, norm_w[l, 1])
        y_lat, _, _ = token_mix(h_lat, s_f, s_b, lat_chunks, *mix_params)
        x = x + g1 * rmsnorm(y_lat, norm_w[l, 1])
        m_lat = expert_choice_moe(modulate(rmsnorm(x, norm_w[l, 2]), sh2, sc2), router_w[l], exp_w13[l], exp_w2[l])
        x = x + g2 * rmsnorm(m_lat, norm_w[l, 3])
        if not last:
            m_ctx = expert_choice_moe(modulate(rmsnorm(ctx_mid, norm_w[l, 2]), csh2, csc2), router_w[l], exp_w13[l], exp_w2[l])
            ctx = ctx_mid + cg2 * rmsnorm(m_ctx, norm_w[l, 3])
    return x


_drawn_inputs = setup_inputs


def setup_inputs(seed=0):
    import zlib

    import numpy as np

    out = dict(_drawn_inputs(seed))
    spreads = {}
    factors = {'ctx': 64.0, 'c_ctx': 42.942, 'sgu_b': 2.945, 'sgu_norm_w': 2.947, 'hgrn_gnorm_w': 2.765}
    for name, (base, spread) in spreads.items():
        noise = np.random.default_rng([zlib.crc32(name.encode()), seed]).standard_normal(out[name].shape)
        drawn = base * np.exp(spread * noise) if base else spread * noise
        out[name] = __import__('jax').numpy.asarray(drawn.astype(out[name].dtype))
    for name, factor in factors.items():
        out[name] = (out[name] * factor).astype(out[name].dtype)
    return out
```

```python
import math
from contextlib import ExitStack

import numpy as np

import concourse.bass as bass
from concourse import mybir

ALU = mybir.AluOpType
ACT = mybir.ActivationFunctionType
AX = mybir.AxisListType
F32 = mybir.dt.float32
U32 = mybir.dt.uint32
U8 = mybir.dt.uint8

P = 128
D = 1024
T = 1024
TC = 256
H = 4
HD = 128
AW = H * HD
NE = 16
CAP = 2 * T // NE
NK = D // P
NT = T // P
NTC = TC // P
HALF = 512
EPS = 1e-6
FLOOR = 1e-20
LEVELS = 7
COL = dict(q=0, ff=AW, fb=2 * AW, i=3 * AW, ga=4 * AW, zb=5 * AW, u=6 * AW, v=7 * AW, gate=8 * AW)
SLOTS = 3
BLK = NK * HALF


def dft_tables():
    t = np.arange(T // 2)[:, None].astype(np.float64)
    even, odd = np.arange(0, T // 2 + 1, 2), np.arange(1, T // 2, 2)
    w = 2 * np.pi / T
    parts = [np.cos(w * ((t * even) % T)), np.sin(w * ((t * even[1:-1]) % T)),
             np.cos(w * ((t * odd) % T)), np.sin(w * ((t * odd) % T))]
    tokens = np.concatenate(parts, 1)
    d = np.arange(HD)[:, None] * np.arange(HD)[None, :] % HD * (2 * np.pi / HD)
    s = 1.0 / math.sqrt(T * HD)
    channels = np.concatenate([np.cos(d) * s, np.sin(d) * s], 1)
    return tokens.astype(np.float32), channels.astype(np.float32)


def level_masks():
    s, t = np.arange(P)[:, None], np.arange(P)[None, :]
    out = [(s // (2 * m) == t // (2 * m)) & (s // m != t // m) for m in (1 << l for l in range(LEVELS))]
    return np.stack(out, 1).astype(np.float32)


class Psum:

    def __init__(self, banks, full, drained):
        self.banks, self.full, self.sems = banks, full, drained
        self.keys, self.count, self.n = {}, {e: 0 for e in drained}, 0
        self.jobs = []

    def plan(self, key, consumer):
        assert key not in self.keys, key
        self.count[consumer] += 1
        self.keys[key] = self.n
        self.jobs.append((consumer, self.count[consumer]))
        self.n += 1

    def bank(self, key):
        return self.banks[self.keys[key] % len(self.banks)]

    def reuses(self, key):
        return self.keys[key] >= len(self.banks)

    def last_drained(self, key):
        consumer, count = self.jobs[self.keys[key] - len(self.banks)]
        return self.sems[consumer], count

    def filled(self, key):
        return self.full, self.keys[key] + 1

    def freed(self, key):
        return self.sems[self.jobs[self.keys[key]][0]]

    def drained(self, key):
        consumer, count = self.jobs[self.keys[key]]
        return self.sems[consumer], count


def schedule():
    steps = [("small",)]
    steps += [("ada_cols", n) for n in range(4)] + [("ada_turn",)]
    steps += [("norm_x", g) for g in range(3)]
    steps += [("v", t) for t in range(NTC + NT)] + [("ga", t) for t in range(NT)]

    def z_units(h):
        return [("z", h, w, j) for w in ("q", "ff", "fb") for j in range(2 if w == "q" else 3)]

    steps += z_units(0) + [("prepare", 0)]
    for h in range(H):
        fill = z_units(h + 1) if h + 1 < H else [("zb", t) for t in range(NT)]
        steps += [("level", h, 0), ("level", h, 1), fill[0]]
        steps += [("ctx_turn", h), ("level", h, 2), fill[1], ("ctx_state", h)]
        if h:
            steps += [("o_turn", h - 1)]
        steps += [("level", h, 3), fill[2], ("level", h, 4), fill[3], ("level", h, 5), fill[4],
                  ("level", h, 6), fill[5], ("level", h, 7), fill[6], ("k_turn", h), fill[7]]
        if h + 1 < H:
            steps += [("prepare", h + 1)]
        steps += [("kv", h), ("out", h)]
    steps += [("fold",)]
    steps += [("u", t) for t in range(NT)] + [("o_turn", H - 1)] + [("vv", t) for t in range(NT)]
    steps += [("vv_norm",)]
    steps += [("dft", g, par) for g in range(4) for par in range(2)]
    steps += [("dft2", g, par) for g in range(4) for par in range(2)]
    steps += [("mix", g, j) for g in range(4) for j in range(2)]
    steps += [("oc_turn", g, j) for g in range(4) for j in range(2)]
    steps += [("merge", b, n, t) for b in (0, 2, 1) for n in range(2) for t in range(NT)]
    steps += [("ada_rows", n) for n in range(8)]
    steps += [("merged_turn", j, k) for j in range(2) for k in range(NK)]
    for t in range(NT):
        steps += [("y", t)] + ([("h2_turn", t - 1)] if t else [])
    steps += [("h2_turn", NT - 1), ("router",), ("router_turn",), ("choose",), ("choose_turn",)]
    return steps


def weight_blocks():
    blocks = [("ada_cols", n) for n in range(4)] + [("v",), ("ga",)] + [("z", h) for h in range(H)]
    blocks += [("zb",), ("u",), ("vv",)]
    for b in (0, 2, 1):
        for n in range(2):
            blocks += [("gate", b, n), ("branch", b, n)]
    return blocks + [("ada_rows", n) for n in range(8)] + [("out", n) for n in range(2)]


def build(nc, x, c, ctx_in, c_ctx, ada_w, ada_b, norm_w, w_in, hgrn_lb_raw, hgrn_gnorm_w, sgu_w, sgu_b,
          sgu_norm_w, w_branch, w_out, router_w, exp_w13, exp_w2, token_dft, channel_dft, masks_in, out,
          h2_dram, moe_dram):
    STEPS, BLOCKS = schedule(), weight_blocks()
    merge_steps = [st for st in STEPS if st[0] == "merge"]
    merge_index = {st: i for i, st in enumerate(merge_steps)}
    with ExitStack() as stack:
        def sb(name, shape, dt=F32):
            return stack.enter_context(nc.sbuf_tensor(name, shape, dt))

        def sem(name):
            return stack.enter_context(nc.semaphore(name))

        r_h = sb("r_h", [P, NK * T])
        r_w = sb("r_w", [P, SLOTS * BLK])
        r_v = sb("r_v", [P, 2 * NT * AW])
        r_oa = sb("r_oa", [P, H * T])
        r_a = sb("r_a", [P, 8192])
        r_b = sb("r_b", [P, 8192])

        hT = r_h[:].rearrange("p (k t) -> p k t", k=NK)
        r_c = sb("r_c", [P, NK * TC])
        hcT = r_c[:].rearrange("p (k t) -> p k t", k=NK)
        wslot = [r_w[:, s * BLK:(s + 1) * BLK].rearrange("p (k n) -> p k n", k=NK) for s in range(SLOTS)]
        V = r_v[:, 0:NT * AW].rearrange("p (t n) -> p t n", t=NT)
        Gt = r_v[:, NT * AW:].rearrange("p (t n) -> p t n", t=NT)
        oaT = r_oa[:].rearrange("p (h t) -> p h t", h=H)
        U = r_b[:, 7168:8192]
        totals = sb("totals", [P, 2 * NT])
        hb = []
        for r in (r_a, r_b):
            hb.append(dict(X1=r[:, 0:2048].rearrange("p (c a t) -> p c a t", c=NT, a=2),
                           X2=r[:, 2048:4096].rearrange("p (c a t) -> p c a t", c=NT, a=2),
                           F=r[:, 4096:6144],
                           A=r[:, 6144:7168].rearrange("p (c t) -> p c t", c=NT)))
        xbuf = [r_a[:, 0:4096].rearrange("p (t n) -> p t n", t=4), r_b[:, 0:4096].rearrange("p (t n) -> p t n", t=4),
                r_a[:, 4096:8192].rearrange("p (t n) -> p t n", t=4)]
        adar = r_oa[0:2, 0:2048]
        adab = r_oa[0:2, 2048:4096]
        zb = r_a[:, 0:4096].rearrange("p (t n) -> p t n", t=NT)
        tdft = r_a[:, 4096:8192].rearrange("p (t n) -> p t n", t=4)
        zfold = [r_b[:, 0:2048].rearrange("p (t n) -> p t n", t=4),
                 r_b[:, 2048:4096].rearrange("p (t n) -> p t n", t=4)]
        AB = r_b[:, 4096:8192].rearrange("p (g e n) -> p g e n", g=4, e=2)
        obT = r_a[:, 0:4096].rearrange("p (g t) -> p g t", g=4)
        vg = V
        ug = Gt
        ocT = r_a[:, 4096:8192].rearrange("p (g t) -> p g t", g=4)
        merged = r_b[:].rearrange("p (t n) -> p t n", t=NT)
        mT = hT
        rows = r_oa[:].rearrange("p (r n) -> p r n", r=4)
        x1 = r_a[:].rearrange("p (t n) -> p t n", t=NT)
        h2T = r_v[:].rearrange("p (k t) -> p k t", k=NK)
        ybuf = [r_b[:, 4096 + 1024 * i:5120 + 1024 * i] for i in range(2)]
        xre = [r_b[:, 6144 + 1024 * i:7168 + 1024 * i] for i in range(2)]

        ident = sb("ident", [P, P])
        half_pow = sb("half_pow", [P, 32])
        small = sb("small", [20, P])
        cols = sb("cols", [P, 20])
        gate_add = sb("gate_add", [P, 8])
        gate_mul = sb("gate_mul", [P, 8])
        lb = sb("lb", [P, 4, 8])
        craw = sb("craw", [P, 2, NK])
        csilu = sb("csilu", [P, 2, NK])
        scale1 = sb("scale1", [P, NK, 2])
        shift1 = sb("shift1", [P, NK, 2])
        ss = sb("ss", [P, 48])
        rs = sb("rs", [P, 48])
        masks = sb("masks", [P, LEVELS, P], U8)
        gnorm = sb("gnorm", [P, HD])
        Vc = r_oa[:, 3072:4096].rearrange("p (t n) -> p t n", t=NTC)
        Fc = r_oa[:, 2048:3072].rearrange("p (i a t) -> p i a t", i=2, a=2)
        Kc = r_a[:, 7168:7680].rearrange("p (a t) -> p a t", a=2)
        big = r_w[:, 2 * BLK:3 * BLK]
        KT = big[:, 0:2048].rearrange("p (a c k) -> p a c k", a=2, c=NT)
        S = big[:, 2048:4096].rearrange("p (a c k) -> p a c k", a=2, c=NT)
        KcT = big[:, 0:512].rearrange("p (c k) -> p c k", c=4)
        o_sb = sb("o_sb", [P, NT, HD])
        o_sq = big[:, 1024:2048].rearrange("p (c t) -> p c t", c=NT)
        zero = big[:, 1024:2048]
        mask_raw = big[:, 0:LEVELS * P].rearrange("p (l t) -> p l t", t=P)
        wsraw = o_sb[:, 0:4, :]
        wsT = o_sb[:, 4:8, :]
        pq = [r_c[:, 512 * i:512 * (i + 1)] for i in range(2)]
        snorm = r_c[:, 1024:1536]
        cdft = r_c[:, 1536:1792]
        sig = [r_v[:, 512 * i:512 * (i + 1)] for i in range(2)]
        gated = [r_v[:, 1024 + 512 * i:1536 + 512 * i] for i in range(2)]
        cbig = r_c[:, 0:NK * P].rearrange("p (k m) -> p k m", k=NK)
        rowb = r_c[:, NK * P:2 * NK * P]
        roww = r_v[:, 2048:3072]
        rw = r_c[:, 1024:1152].rearrange("p (k e) -> p k e", e=NE)
        prob = r_b[:, 4480:4608].rearrange("p (t e) -> p t e", e=NE)
        pmax = sb("pmax", [P, NT])
        psumm = sb("psumm", [P, NT])
        aff = r_b[0:NE, 6144:7168]
        aff2 = r_b[0:NE, 7168:8192]
        topv, topf = r_b[0:NE, 4096:4096 + CAP], r_b[0:NE, 4096 + CAP:4096 + 2 * CAP]
        topi = r_b[0:NE, 4096 + 2 * CAP:4096 + 3 * CAP].bitcast(U32)
        gates = sb("gates", [P, NE])
        idx = sb("idx", [P, NE], U32)
        mslot = [r_w[:, s * BLK:(s + 1) * BLK] for s in range(3)]
        mslot += [r_h[:, s * BLK:(s + 1) * BLK] for s in range(2)] + [r_b[:, 0:BLK]]
        mslot = [m.rearrange("p (k n) -> p k n", k=NK) for m in mslot]
        xg = r_v[:, 0:1024]
        xeT = r_v[:, 1024:2048].rearrange("p (k t) -> p k t", k=NK)
        hid = r_v[:, 2048:3072]
        hidT = r_v[:, 3072:4096].rearrange("p (k t) -> p k t", k=NK)
        sa = [r_v[:, 4096 + 512 * i:4608 + 512 * i] for i in range(2)]
        yb = r_v[:, 5120:6144]
        gcur = sb("gcur", [P, 1])
        icur = sb("icur", [P, 1], U32)
        icur2 = sb("icur2", [P, 1], U32)
        fin = [r_b[:, 1024 * i:1024 * (i + 1)] for i in range(8)]

        banks = [stack.enter_context(nc.psum_tensor(f"bank{i}", [P, 512], F32)) for i in range(8)]
        G = Psum(banks[0:4], sem("g_full"), dict(act=sem("g_drained_act"), dve=sem("g_drained_dve")))
        L = Psum(banks[4:6], sem("l_full"), dict(act=sem("l_drained_act"), dve=sem("l_drained_dve")))
        S2 = Psum(banks[6:8], sem("s_full"), dict(act=sem("s_drained_act"), dve=sem("s_drained_dve")))

        block_jobs = {}
        for st in STEPS:
            k = st[0]
            if k in ("small", "ada_cols", "ada_turn"):
                G.plan(st, "dve")
            elif k == "norm_x":
                for kk in range(NK):
                    G.plan(st + (kk,), "act" if kk % 2 else "dve")
            elif k in ("v", "ga", "z", "zb", "u", "vv", "oc_turn"):
                G.plan(st, "act")
            elif k == "level":
                for j in range(2):
                    L.plan(st + (j,), "dve" if st[2] else "act")
            elif k in ("ctx_turn", "ctx_state"):
                S2.plan(st, "act")
            elif k == "k_turn":
                for j in range(4):
                    S2.plan(st + (j,), "act")
            elif k == "kv":
                for j in range(4):
                    S2.plan(st + (j,), "dve")
            elif k == "out":
                for j in range(2):
                    S2.plan(st + (j,), "act")
            elif k == "o_turn":
                for j in range(2):
                    S2.plan(st + (j,), "act")
            elif k in ("dft", "dft2"):
                G.plan(st, "act")
            elif k in ("mix", "ada_rows"):
                G.plan(st, "dve")
            elif k == "merge":
                G.plan(("gate",) + st[1:], "act")
                G.plan(("branch",) + st[1:], "dve")
                block_jobs[("gate",) + st[1:3]] = ("gate",) + st[1:]
                block_jobs[("branch",) + st[1:3]] = ("branch",) + st[1:]
            elif k == "merged_turn":
                G.plan(st, "act" if st[2] % 2 else "dve")
            elif k == "y":
                for n in range(2):
                    G.plan(st + (n,), "act")
                    block_jobs[("out", n)] = st + (n,)
            elif k == "h2_turn":
                for j in range(2):
                    G.plan(st + (j,), "act" if j else "dve")
            elif k == "router":
                G.plan(st + (0,), "dve")
            elif k in ("router_turn", "choose_turn"):
                for j in range(2):
                    G.plan(st + (j,), "dve")
            if k in ("ada_cols", "ada_rows"):
                block_jobs[st] = st
            elif k in ("v", "ga", "zb", "u", "vv"):
                block_jobs[(k,)] = st
            elif k == "z":
                block_jobs[("z", st[1])] = st
        first3 = BLOCKS.index(("gate", 0, 0))
        SLOT = {b: i % 2 if i < first3 else (1, 0, 2)[(i - first3) % 3] for i, b in enumerate(BLOCKS)}
        w_full = [sem(f"w_full{s}") for s in range(SLOTS)]
        w_count, last_in, before = {}, {}, {}
        for b in BLOCKS:
            before[b] = last_in.get(SLOT[b])
            w_count[b] = w_count.get(before[b], 0) + (48 if b[0] == "z" else 16)
            last_in[SLOT[b]] = b

        d_small, d_mod, d_row, d_late, d_mask, d_tab, d_ws = (sem(n) for n in ("d_small", "d_mod", "d_row", "d_late", "d_mask", "d_tab", "d_ws"))
        d_x = [sem(f"d_x{g}") for g in range(3)]
        d_rb, d_rw, d_rt, d_xre = sem("d_rb"), sem("d_rw"), sem("d_rt"), [sem("d_xre0"), sem("d_xre1")]
        d_h2, d_zero = [sem("d_h2_0"), sem("d_h2_1")], sem("d_zero")
        ident_ready, pow_ready, zero_ready = sem("ident_ready"), sem("pow_ready"), sem("zero_ready")
        csilu_ready, cbig_ready = sem("csilu_ready"), sem("cbig_ready")
        lb_max, lb_ready = sem("lb_max"), sem("lb_ready")
        x_ss, x_ms, x_rs, x_normed = sem("x_ss"), sem("x_ms"), sem("x_rs"), sem("x_normed")
        ga_gated = sem("ga_gated")
        x_ready = sem("x_ready")
        kc_ready = sem("kc_ready")
        ctx_done = sem("ctx_done")
        s_ready = sem("s_ready")
        o_ms, o_rs, o_gated, o_ready = (sem(n) for n in ("o_ms", "o_rs", "o_gated", "o_ready"))
        fold_done, vv_done = sem("fold_done"), sem("vv_done")
        v_sq, v_ms, v_rs = sem("v_sq"), sem("v_ms"), sem("v_rs")
        ws_t, vv_sq_ready, ob_done = sem("ws_t"), sem("vv_sq_ready"), sem("ob_done")
        merged_done = sem("merged_done")
        rows_done = sem("rows_done")
        y_ss, y_ms, y_rs, x1_done, x1_ss, x1_ms, x1_rs, h2_done = (sem(n) for n in (
            "y_ss", "y_ms", "y_rs", "x1_done", "x1_ss", "x1_ms", "x1_rs", "h2_done"))
        yg = sem("yg")
        r_sub, r_exp, r_prob, chosen = (sem(n) for n in ("r_sub", "r_exp", "r_prob", "chosen"))
        vstep, pstep, tick = sem("dve_step"), sem("pool_step"), sem("pool_tick")
        added = sem("added")
        m_full = [sem(f"m_full{s}") for s in range(6)]
        ab_full, a_drained, b_drained, tx_full, tx_drained = (sem(n) for n in ("ab_full", "a_drained", "b_drained", "tx_full", "tx_drained"))
        th_full, th_drained, y_full, y_drained = (sem(n) for n in ("th_full", "th_drained", "y_full", "y_drained"))
        cur_done, xg_full, sc_done, cur_g = sem("cur_done"), sem("xg_full"), sem("sc_done"), sem("cur_g")
        f_ss, f_ms, f_rs, f_out, d_out = (sem(n) for n in ("f_ss", "f_ms", "f_rs", "f_out", "d_out"))
        d_fins = [sem(f"d_fin{t}") for t in range(NT)]

        def x_at(h, l):
            return 8 * h + l + 1

        def wcol(b):
            def cut(a, c0, n=HALF):
                return a[:, c0:c0 + n].rearrange("(k p) n -> p k n", p=P)
            k = b[0]
            if k == "ada_cols":
                return ada_w[0, :, b[1] * HALF:(b[1] + 1) * HALF].rearrange("(p k) n -> p k n", k=NK)
            if k == "ada_rows":
                c0 = 2048 + b[1] * HALF
                return ada_w[0, :, c0:c0 + HALF].rearrange("(p k) n -> p k n", k=NK)
            if k == "gate":
                return cut(w_in[0], COL["gate"] + b[1] * D + b[2] * HALF)
            if k == "branch":
                return cut(w_branch[0, b[1]], b[2] * HALF)
            if k == "out":
                return cut(w_out[0], b[1] * HALF)
            return cut(w_in[0], COL[{"v": "i", "ga": "ga", "zb": "zb", "u": "u", "vv": "v"}[k]])

        block = stack.enter_context(nc.Block())

        @block.sync
        def _(sp):
            sp.dma_start(small[0:8, :], norm_w[0, 0, :].rearrange("(r n) -> r n", r=8)).then_inc(d_small, 16)
            sp.dma_start(small[8:12, :], sgu_b[0]).then_inc(d_small, 16)
            sp.dma_start(small[12:20, :], hgrn_lb_raw.rearrange("a d (h n) -> (a d h) n", h=H)).then_inc(d_small, 16)
            sp.dma_start(craw[:, 0, :], c[0].rearrange("(p k) -> p k", k=NK)).then_inc(d_mod, 16)
            sp.dma_start(craw[:, 1, :], c_ctx.rearrange("(p k) -> p k", k=NK)).then_inc(d_mod, 16)
            sp.dma_start(adab[:, :], ada_b[0:1, 0:2048].to_broadcast([2, 2048])).then_inc(d_mod, 16)
            n_block = [0]

            def load_block():
                i = n_block[0]
                b = BLOCKS[i]
                n_block[0] += 1
                if before[b]:
                    sp.wait_ge(*G.filled(block_jobs[before[b]]))
                elif SLOT[b] == 2:
                    sp.wait_ge(v_sq, 4)
                w = wslot[SLOT[b]]
                if b[0] == "z":
                    for j, name in enumerate(("q", "ff", "fb")):
                        c0 = COL[name] + b[1] * HD
                        sp.dma_start(w[:, :, j * HD:(j + 1) * HD],
                                     w_in[0, :, c0:c0 + HD].rearrange("(k p) n -> p k n", p=P)).then_inc(w_full[SLOT[b]], 16)
                elif b[0] == "branch":
                    sp.dma_start(w[:, 0:4, :], wcol(b)).then_inc(w_full[SLOT[b]], 16)
                else:
                    sp.dma_start(w, wcol(b)).then_inc(w_full[SLOT[b]], 16)

            load_block()
            load_block()
            for t in range(NTC):
                sp.dma_start(xbuf[0][:, t, :], ctx_in[0, t * P:(t + 1) * P, :]).then_inc(d_x[0], 16)
            for g in (1, 2):
                for t in range(4):
                    i = 4 * (g - 1) + t
                    sp.dma_start(xbuf[g][:, t, :], x[0, i * P:(i + 1) * P, :]).then_inc(d_x[g], 16)
            sp.dma_start(mask_raw, masks_in).then_inc(d_mask, 16)
            sp.dma_start(gnorm[:], hgrn_gnorm_w[0:1, :].to_broadcast([P, HD])).then_inc(d_row, 16)
            sp.wait_ge(zero_ready, 1)
            for t in range(NT):
                sp.dma_start(moe_dram[t * P:(t + 1) * P, :], zero).then_inc(d_zero, 16)
            while n_block[0] < BLOCKS.index(("zb",)) + 1:
                load_block()
            sp.wait_ge(*S2.filled(("ctx_turn", H - 1)))
            sp.wait_ge(*G.filled(("z", H - 1, "fb", 2)))
            sp.dma_start(snorm, sgu_norm_w.rearrange("a g n -> a (g n)").to_broadcast([P, 4 * P])).then_inc(d_late, 16)
            sp.dma_start(cdft, channel_dft).then_inc(d_late, 16)
            sp.dma_start(tdft, token_dft.rearrange("(t p) n -> p t n", p=P)).then_inc(d_tab, 16)
            for _ in range(4):
                load_block()
            sp.wait_ge(o_ready, 4)
            sp.wait_ge(*S2.filled(("o_turn", H - 1, 1)))
            sp.dma_start(wsraw, sgu_w[0].rearrange("g p q -> p g q")).then_inc(d_ws, 16)
            for n in range(8):
                while n_block[0] < BLOCKS.index(("ada_rows", n)) + 1:
                    load_block()
                seg, j = n // 2, n % 2
                if j == 0:
                    if seg == 0:
                        sp.wait_ge(merged_done, 4 * NT)
                    else:
                        sp.wait_ge(rows_done, 2 * seg)
                    c0 = 2048 + seg * D
                    sp.dma_start(rowb, ada_b[0:1, c0:c0 + D].to_broadcast([P, D])).then_inc(d_rb, 16)
                    nw = {0: 1, 1: 1, 2: 2, 3: 3}[seg]
                    sp.dma_start(roww, norm_w[0, nw:nw + 1, :].to_broadcast([P, D])).then_inc(d_rb, 16)
            while n_block[0] < len(BLOCKS):
                load_block()
            sp.wait_ge(rows_done, 8)
            sp.dma_start(rw, router_w[0].rearrange("(k p) e -> p k e", p=P)).then_inc(d_row, 16)
            sp.wait_ge(*G.filled(("merged_turn", 1, NK - 1)))
            for t in range(NT):
                if t >= 2:
                    sp.wait_ge(x1_done, t - 1)
                sp.dma_start(xre[t % 2], x[0, t * P:(t + 1) * P, :]).then_inc(d_xre[t % 2], 16)
                if t >= 1:
                    sp.wait_ge(h2_done, t)
                    sp.dma_start(h2_dram[(t - 1) * P:t * P, :], ybuf[(t - 1) % 2]).then_inc(d_h2[(t - 1) % 2], 16)
            sp.wait_ge(h2_done, NT)
            sp.dma_start(h2_dram[(NT - 1) * P:NT * P, :], ybuf[(NT - 1) % 2]).then_inc(d_h2[(NT - 1) % 2], 16)

            def expert_weights(e, s):
                if s < 4:
                    c0 = (s % 2) * D + (s // 2) * HALF
                    src = exp_w13[0, e, :, c0:c0 + HALF]
                else:
                    src = exp_w2[0, e, :, (s - 4) * HALF:(s - 3) * HALF]
                sp.dma_start(mslot[s], src.rearrange("(k p) n -> p k n", p=P)).then_inc(m_full[s], 16)

            sp.wait_ge(*G.filled(("y", NT - 1, 1)))
            for s in range(6):
                expert_weights(0, s)
            with sp.Fori(0, NE - 1) as e:
                for s in range(4):
                    sp.wait_ge(ab_full, e * 4 + (s + 1))
                    expert_weights(e + 1, s)
                for s in range(4, 6):
                    sp.wait_ge(y_full, e * 2 + (s - 3))
                    expert_weights(e + 1, s)
            sp.wait_ge(sc_done, 16 * NE)
            sp.wait_ge(y_full, 2 * NE)
            for t in range(NT):
                sp.dma_start(fin[t], moe_dram[t * P:(t + 1) * P, :]).then_inc(d_fins[t], 16)
            for t in range(NT):
                sp.wait_ge(f_out, t + 1)
                sp.dma_start(out[0, t * P:(t + 1) * P, :], fin[t]).then_inc(d_out, 16)
            sp.wait_ge(d_out, 16 * NT)
            sp.wait_ge(d_zero, 16 * NT)
            for j in range(2):
                sp.wait_ge(d_h2[j], 8 * NT)

        @block.tensor
        def _(pe):
            def claim(stream, key):
                if stream.reuses(key):
                    pe.wait_ge(*stream.last_drained(key))
                return stream.bank(key)

            def weights(b):
                pe.wait_ge(w_full[SLOT[b]], w_count[b])
                return wslot[SLOT[b]]

            def turn(dst, src, n=P):
                return nc.tensor.transpose(dst, src, ident[0:n, 0:n])

            def tokens_by_cols(bank, w, lhs, t, nk=NK):
                for k in range(nk):
                    mm = nc.tensor.matmul(bank[:], lhs[:, k, t * P:(t + 1) * P], w[:, k, :],
                                          start=(k == 0), stop=(k == nk - 1))
                return mm

            pe.wait_ge(ident_ready, 2)
            for st in STEPS:
                kind = st[0]
                if kind == "small":
                    bank = claim(G, st)
                    pe.wait_ge(d_small, 48)
                    turn(bank[:, 0:20], small[:], 20).then_inc(G.full, 1)
                elif kind == "ada_cols":
                    w = weights(st)
                    bank = claim(G, st)
                    pe.wait_ge(csilu_ready, 2)
                    for k in range(NK):
                        mm = nc.tensor.matmul(bank[0:2, :], csilu[:, :, k], w[:, k, :], start=(k == 0), stop=(k == NK - 1))
                    mm.then_inc(G.full, 1)
                elif kind == "ada_turn":
                    bank = claim(G, st)
                    pe.wait_ge(*G.drained(("ada_cols", 3)))
                    for m in range(16):
                        mm = turn(bank[:, 2 * m:2 * m + 2], adar[:, m * P:(m + 1) * P], 2)
                    mm.then_inc(G.full, 1)
                elif kind == "norm_x":
                    g = st[1]
                    nt = NTC if g == 0 else 4
                    pe.wait_ge(x_normed, g + 1)
                    for k in range(NK):
                        bank = claim(G, st + (k,))
                        for t in range(nt):
                            mm = turn(bank[:, t * P:(t + 1) * P], xbuf[g][:, t, k * P:(k + 1) * P])
                        mm.then_inc(G.full, 1)
                elif kind == "v":
                    w = weights(("v",))
                    bank = claim(G, st)
                    if st[1] == 0:
                        pe.wait_ge(*G.drained(("norm_x", 2, NK - 1)))
                        pe.wait_ge(*G.drained(("norm_x", 2, NK - 2)))
                    if st[1] < NTC:
                        tokens_by_cols(bank, w, hcT, st[1]).then_inc(G.full, 1)
                    else:
                        tokens_by_cols(bank, w, hT, st[1] - NTC).then_inc(G.full, 1)
                elif kind in ("ga", "zb", "u", "vv"):
                    w = weights((kind,))
                    bank = claim(G, st)
                    tokens_by_cols(bank, w, hT, st[1]).then_inc(G.full, 1)
                elif kind == "z":
                    _, h, name, j = st
                    w = weights(("z", h))
                    bank = claim(G, st)
                    c0 = ("q", "ff", "fb").index(name) * HD
                    for k in range(NK):
                        rhs = hT[:, k, j * HALF:(j + 1) * HALF] if j < 2 else hcT[:, k, :]
                        o = bank[:] if j < 2 else bank[:, 0:TC]
                        mm = nc.tensor.matmul(o, w[:, k, c0:c0 + HD], rhs, start=(k == 0), stop=(k == NK - 1))
                    mm.then_inc(G.full, 1)
                elif kind == "level":
                    _, h, l = st
                    B = hb[h % 2]
                    pe.wait_ge(x_ready, x_at(h, max(l - 1, 0)))
                    for j in range(2):
                        bank = claim(L, st + (j,))
                        for cc in range(4):
                            ch = 4 * j + cc
                            if l == 0:
                                mm = nc.tensor.matmul(bank[:, cc * P:(cc + 1) * P], U[:, ch * P:(ch + 1) * P],
                                                      B["A"][:, ch, :], start=True, stop=True)
                                continue
                            m = 1 << (l - 1)
                            o = bank[:, cc * P:(cc + 1) * P].rearrange("p (b two m) -> p b two m", two=2, m=m)
                            qf = B["X1"][:, ch, 0, :].rearrange("p (b two m) -> p b two m", two=2, m=m)
                            qb = B["X2"][:, ch, 1, :].rearrange("p (b two m) -> p b two m", two=2, m=m)
                            nc.tensor.matmul(o[:, :, 1, :], B["X2"][:, ch, 0, :], qf[:, :, 1, :], start=True, stop=True)
                            mm = nc.tensor.matmul(o[:, :, 0, :], B["X1"][:, ch, 1, :], qb[:, :, 0, :], start=True, stop=True)
                        mm.then_inc(L.full, 1)
                elif kind == "ctx_turn":
                    bank = claim(S2, st)
                    pe.wait_ge(ctx_done, st[1] + 1)
                    for a in range(2):
                        for t in range(NTC):
                            mm = turn(bank[:, (2 * a + t) * P:(2 * a + t + 1) * P], Kc[:, a, t * P:(t + 1) * P])
                    mm.then_inc(S2.full, 1)
                elif kind == "ctx_state":
                    h = st[1]
                    bank = claim(S2, st)
                    pe.wait_ge(*S2.drained(("ctx_turn", h)))
                    for a in range(2):
                        for t in range(NTC):
                            mm = nc.tensor.matmul(bank[:, a * P:(a + 1) * P], KcT[:, 2 * a + t, :],
                                                  Vc[:, t, h * HD:(h + 1) * HD], start=(t == 0), stop=(t == NTC - 1))
                    mm.then_inc(S2.full, 1)
                elif kind == "k_turn":
                    h = st[1]
                    B = hb[h % 2]
                    pe.wait_ge(x_ready, x_at(h, LEVELS))
                    for j in range(4):
                        bank = claim(S2, st + (j,))
                        src = B["X2"] if j < 2 else B["X1"]
                        for cc in range(4):
                            mm = turn(bank[:, cc * P:(cc + 1) * P], src[:, 4 * (j % 2) + cc, j // 2, :])
                        mm.then_inc(S2.full, 1)
                elif kind == "kv":
                    h = st[1]
                    for j in range(4):
                        bank = claim(S2, st + (j,))
                        if j == 0:
                            pe.wait_ge(*S2.drained(("k_turn", h, 3)))
                        a = j % 2
                        for i in range(4 if j < 2 else 3):
                            ch = 4 * (j // 2) + i if a == 0 else 7 - 4 * (j // 2) - i
                            mm = nc.tensor.matmul(bank[:, i * P:(i + 1) * P], KT[:, a, ch, :],
                                                  V[:, ch, h * HD:(h + 1) * HD], start=True, stop=True)
                        mm.then_inc(S2.full, 1)
                elif kind == "out":
                    h = st[1]
                    B = hb[h % 2]
                    pe.wait_ge(s_ready, h + 1)
                    for j in range(2):
                        bank = claim(S2, st + (j,))
                        for cc in range(4):
                            ch = 4 * j + cc
                            o = bank[:, cc * P:(cc + 1) * P]
                            nc.tensor.matmul(o, B["A"][:, ch, :], V[:, ch, h * HD:(h + 1) * HD], start=True, stop=False)
                            nc.tensor.matmul(o, B["X1"][:, ch, 0, :], S[:, 0, ch, :], start=False, stop=False)
                            mm = nc.tensor.matmul(o, B["X2"][:, ch, 1, :], S[:, 1, ch, :], start=False, stop=True)
                        mm.then_inc(S2.full, 1)
                elif kind == "o_turn":
                    h = st[1]
                    pe.wait_ge(o_ready, h + 1)
                    for j in range(2):
                        bank = claim(S2, st + (j,))
                        for cc in range(4):
                            mm = turn(bank[:, cc * P:(cc + 1) * P], o_sb[:, 4 * j + cc, :])
                        mm.then_inc(S2.full, 1)
                elif kind == "dft":
                    _, g, par = st
                    bank = claim(G, st)
                    if (g, par) == (0, 0):
                        pe.wait_ge(fold_done, 2)
                        pe.wait_ge(d_tab, 16)
                    for t in range(4):
                        mm = nc.tensor.matmul(bank[:], zfold[par][:, t, g * P:(g + 1) * P],
                                              tdft[:, t, par * HALF:(par + 1) * HALF], start=(t == 0), stop=(t == 3))
                    mm.then_inc(G.full, 1)
                elif kind == "dft2":
                    _, g, par = st
                    bank = claim(G, st)
                    pe.wait_ge(*G.drained(("dft", g, par)))
                    n = 257 - par
                    pe.wait_ge(d_late, 32)
                    nc.tensor.matmul(bank[:, 0:n], cdft[:, 0:HD], AB[:, g, par, 0:n], start=True, stop=True)
                    nc.tensor.matmul(bank[:, n:HALF], cdft[:, HD:], AB[:, g, par, n:HALF], start=True,
                                     stop=True).then_inc(G.full, 1)
                elif kind == "mix":
                    _, g, j = st
                    if (g, j) == (0, 0):
                        pe.wait_ge(d_ws, 16)
                        pe.wait_ge(L.sems["dve"], L.count["dve"])
                        for gg in range(4):
                            mm = turn(banks[4][:, gg * P:(gg + 1) * P], wsraw[:, gg, :])
                        mm.then_inc(ws_t, 1)
                        pe.wait_ge(vv_done, 1)
                        pe.wait_ge(ws_t, 2)
                    bank = claim(G, st)
                    nc.tensor.matmul(bank[:].rearrange("p (t n) -> p t n", t=4), wsT[:, g, :],
                                     vg[:, 4 * j:4 * j + 4, g * P:(g + 1) * P], start=True, stop=True).then_inc(G.full, 1)
                elif kind == "oc_turn":
                    _, g, j = st
                    bank = claim(G, st)
                    pe.wait_ge(*G.drained(("mix", 3, 1)))
                    for t in range(4):
                        mm = turn(bank[:, t * P:(t + 1) * P], ug[:, 4 * j + t, g * P:(g + 1) * P])
                    mm.then_inc(G.full, 1)
                elif kind == "merge":
                    _, b, n, t = st
                    w = weights(("gate", b, n))
                    tokens_by_cols(claim(G, ("gate",) + st[1:]), w, hT, t).then_inc(G.full, 1)
                    w = weights(("branch", b, n))
                    bank = claim(G, ("branch",) + st[1:])
                    if n == 0 and t == 0:
                        if b == 0:
                            pe.wait_ge(*S2.drained(("o_turn", H - 1, 1)))
                        elif b == 2:
                            pe.wait_ge(*G.drained(("oc_turn", 3, 1)))
                        else:
                            pe.wait_ge(ob_done, 8)
                    tokens_by_cols(bank, w, (oaT, obT, ocT)[b], t, 4).then_inc(G.full, 1)
                elif kind == "ada_rows":
                    w = weights(st)
                    bank = claim(G, st)
                    pe.wait_ge(cbig_ready, 1)
                    for k in range(NK):
                        mm = nc.tensor.matmul(bank[:], cbig[:, k, :], w[:, k, :], start=(k == 0), stop=(k == NK - 1))
                    mm.then_inc(G.full, 1)
                elif kind == "merged_turn":
                    _, j, k = st
                    bank = claim(G, st)
                    pe.wait_ge(merged_done, 4 * NT)
                    for t in range(4):
                        mm = turn(bank[:, t * P:(t + 1) * P], merged[:, 4 * j + t, k * P:(k + 1) * P])
                    mm.then_inc(G.full, 1)
                elif kind == "y":
                    t = st[1]
                    if t == 0:
                        pe.wait_ge(*G.drained(("merged_turn", 1, NK - 1)))
                        pe.wait_ge(*G.drained(("merged_turn", 1, NK - 2)))
                    for n in range(2):
                        w = weights(("out", n))
                        tokens_by_cols(claim(G, st + (n,)), w, mT, t).then_inc(G.full, 1)
                elif kind == "h2_turn":
                    t = st[1]
                    pe.wait_ge(h2_done, t + 1)
                    for j in range(2):
                        bank = claim(G, st + (j,))
                        for k in range(4):
                            mm = turn(bank[:, k * P:(k + 1) * P], ybuf[t % 2][:, (4 * j + k) * P:(4 * j + k + 1) * P])
                        mm.then_inc(G.full, 1)
                elif kind == "router":
                    bank = claim(G, st + (0,))
                    for j in range(2):
                        pe.wait_ge(*G.drained(("h2_turn", NT - 1, j)))
                    pe.wait_ge(d_row, 32)
                    for t in range(NT):
                        for k in range(NK):
                            mm = nc.tensor.matmul(bank[:, t * NE:(t + 1) * NE], h2T[:, k, t * P:(t + 1) * P], rw[:, k, :],
                                                  start=(k == 0), stop=(k == NK - 1))
                    mm.then_inc(G.full, 1)
                elif kind == "router_turn":
                    pe.wait_ge(r_prob, 1)
                    for j in range(2):
                        bank = claim(G, st + (j,))
                        for t in range(4):
                            mm = turn(bank[0:NE, t * P:(t + 1) * P], prob[:, 4 * j + t, :])
                        mm.then_inc(G.full, 1)
                elif kind == "choose_turn":
                    pe.wait_ge(chosen, 1)
                    for j, src in enumerate((topv, topf)):
                        bank = claim(G, st + (j,))
                        turn(bank[:, 0:NE], src, NE).then_inc(G.full, 1)

            def turn_gathered(n):
                pe.wait_ge(xg_full, n * 16 + 16)
                for j in range(2):
                    for k in range(4):
                        mm = turn(banks[4 + j][:, k * P:(k + 1) * P], xg[:, (4 * j + k) * P:(4 * j + k + 1) * P])
                    mm.then_inc(tx_full, 1)

            def expert(e, last):
                pe.wait_ge(tx_drained, e * 2 + 2)
                pe.wait_ge(y_drained, e * 2 + 2)
                for s in range(4):
                    if s == 2:
                        pe.wait_ge(b_drained, e * 2 + 2)
                    pe.wait_ge(m_full[s], e * 16 + 16)
                    for k in range(NK):
                        mm = nc.tensor.matmul(banks[s][:], xeT[:, k, :], mslot[s][:, k, :], start=(k == 0), stop=(k == NK - 1))
                    mm.then_inc(ab_full, 1)
                if not last:
                    turn_gathered(e + 1)
                pe.wait_ge(th_drained, e * 2 + 2)
                for j in range(2):
                    pe.wait_ge(b_drained, e * 2 + (j + 3))
                    for k in range(4):
                        mm = turn(banks[6 + j][:, k * P:(k + 1) * P], hid[:, (4 * j + k) * P:(4 * j + k + 1) * P])
                    mm.then_inc(th_full, 1)
                for s in range(4, 6):
                    pe.wait_ge(m_full[s], e * 16 + 16)
                    for k in range(NK):
                        if s == 4 and k % 4 == 0:
                            pe.wait_ge(th_drained, e * 2 + (k // 4 + 3))
                        mm = nc.tensor.matmul(banks[s - 4][:], hidT[:, k, :], mslot[s][:, k, :], start=(k == 0), stop=(k == NK - 1))
                    mm.then_inc(y_full, 1)

            turn_gathered(0)
            with pe.Fori(0, NE - 1) as e:
                expert(e, False)
            expert(NE - 1, True)

        @block.scalar
        def _(act):
            def take(stream, key):
                act.wait_ge(*stream.filled(key))
                return stream.bank(key)

            act.wait_ge(d_mod, 48)
            for j in range(2):
                nc.scalar.activation(csilu[:, j, :], craw[:, j, :], ACT.Silu).then_inc(csilu_ready, 1)
            for st in STEPS:
                kind = st[0]
                if kind == "small":
                    act.wait_ge(lb_max, 1)
                    nc.scalar.activation(lb[:, 1, :], lb[:, 0, :], ACT.Exp).then_inc(lb_ready, 1)
                elif kind == "norm_x":
                    g = st[1]
                    nt = NTC if g == 0 else 4
                    act.wait_ge(d_x[g], 16 * nt)
                    for t in range(nt):
                        nc.scalar.activation(o_sb[:].rearrange("p a b -> p (a b)"), xbuf[g][:, t, :], ACT.Square,
                                             scale=1.0 / math.sqrt(D), accum_out=ss[:, 4 * g + t:4 * g + t + 1]).then_inc(x_ss, 1)
                        act.wait_ge(x_ss, (0, 2, 6)[g] + t + 1)
                    act.wait_ge(*G.drained(("ada_turn",)))
                    for k in range(1, NK, 2):
                        bank = take(G, st + (k,))
                        dst = hcT[:, k, :] if g == 0 else hT[:, k, (g - 1) * HALF:g * HALF]
                        w = TC if g == 0 else HALF
                        j = 1 if g == 0 else 0
                        nc.scalar.activation(dst, bank[:, 0:w], ACT.Identity, bias=shift1[:, k, j:j + 1],
                                             scale=scale1[:, k, j:j + 1]).then_inc(G.freed(st + (k,)), 1)
                elif kind == "v":
                    bank = take(G, st)
                    dst = Vc[:, st[1], :] if st[1] < NTC else V[:, st[1] - NTC, :]
                    nc.scalar.copy(dst, bank[:]).then_inc(G.freed(st), 1)
                elif kind == "ga":
                    bank = take(G, st)
                    nc.scalar.activation(Gt[:, st[1], :], bank[:], ACT.Silu).then_inc(G.freed(st), 1)
                elif kind == "z":
                    _, h, name, j = st
                    B = hb[h % 2]
                    bank = take(G, st)
                    src = bank[:].rearrange("p (c t) -> p c t", c=4)
                    if name == "q":
                        nc.scalar.activation(B["A"][:, 4 * j:4 * j + 4, :], src, ACT.Silu).then_inc(G.freed(st), 1)
                        continue
                    a = 0 if name == "ff" else 1
                    if j < 2:
                        f = B["F"].rearrange("p (c a t) -> p c a t", c=NT, a=2)[:, 4 * j:4 * j + 4, a, :]
                        kk = (B["X2"], B["X1"])[a][:, 4 * j:4 * j + 4, a, :]
                    else:
                        src, f, kk = bank[:, 0:TC], Fc[:, 0, a, :], Kc[:, a, :]
                        if h:
                            act.wait_ge(*S2.filled(("ctx_turn", h - 1)))
                    nc.scalar.activation(f, src, ACT.Sigmoid)
                    nc.scalar.activation(kk, src, ACT.Sigmoid, scale=-1.0).then_inc(G.freed(st), 1)
                elif kind == "level" and st[2] == 0:
                    for j in range(2):
                        bank = take(L, st + (j,))
                        nc.scalar.copy(hb[st[1] % 2]["A"][:, 4 * j:4 * j + 4, :],
                                       bank[:].rearrange("p (c t) -> p c t", c=4)).then_inc(L.freed(st + (j,)), 1)
                elif kind == "ctx_turn":
                    bank = take(S2, st)
                    nc.scalar.copy(KcT, bank[:].rearrange("p (c t) -> p c t", c=4)).then_inc(S2.freed(st), 1)
                elif kind == "ctx_state":
                    h = st[1]
                    bank = take(S2, st)
                    nc.scalar.copy(S[:, 0, 0, :], bank[:, 0:P])
                    nc.scalar.copy(S[:, 1, NT - 1, :], bank[:, P:2 * P]).then_inc(S2.freed(st), 1)
                elif kind == "k_turn":
                    if st[1] == 0:
                        act.wait_ge(d_zero, 16 * NT)
                    for j in range(4):
                        bank = take(S2, st + (j,))
                        nc.scalar.copy(KT[:, j // 2, 4 * (j % 2):4 * (j % 2) + 4, :],
                                       bank[:].rearrange("p (c t) -> p c t", c=4)).then_inc(S2.freed(st + (j,)), 1)
                elif kind == "out":
                    h = st[1]
                    for j in range(2):
                        bank = take(S2, st + (j,))
                        src = bank[:].rearrange("p (c t) -> p c t", c=4)
                        if j == 0 and h:
                            act.wait_ge(*S2.filled(("o_turn", h - 1, 1)))
                        nc.scalar.copy(o_sb[:, 4 * j:4 * j + 4, :], src)
                        nc.scalar.activation(o_sq[:, 4 * j:4 * j + 4, :], src, ACT.Square,
                                             scale=1.0 / math.sqrt(HD)).then_inc(S2.freed(st + (j,)), 1)
                elif kind == "o_turn":
                    h = st[1]
                    for j in range(2):
                        bank = take(S2, st + (j,))
                        nc.scalar.copy(oaT[:, h, j * HALF:(j + 1) * HALF], bank[:]).then_inc(S2.freed(st + (j,)), 1)
                elif kind == "zb":
                    bank = take(G, st)
                    nc.scalar.copy(zb[:, st[1], :], bank[:]).then_inc(G.freed(st), 1)
                elif kind in ("u", "vv"):
                    bank = take(G, st)
                    if st == ("u", 0):
                        act.wait_ge(o_gated, H)
                    nc.scalar.activation((ug if kind == "u" else vg)[:, st[1], :], bank[:], ACT.Gelu).then_inc(G.freed(st), 1)
                elif kind == "vv_norm":
                    act.wait_ge(*G.drained(("vv", NT - 1)))
                    for j in range(4):
                        if j >= 2:
                            act.wait_ge(v_sq, j - 1)
                        sq = big[:, 1024 * (j % 2):1024 * (j % 2 + 1)].rearrange("p (t n) -> p t n", t=2)
                        nc.scalar.activation(sq, vg[:, 2 * j:2 * j + 2, :], ACT.Square,
                                             scale=1.0 / math.sqrt(P)).then_inc(vv_sq_ready, 1)
                elif kind == "dft":
                    _, g, par = st
                    bank = take(G, st)
                    nc.scalar.copy(AB[:, g, par, :], bank[:]).then_inc(G.freed(st), 1)
                elif kind == "dft2":
                    _, g, par = st
                    n = 2 * g + par
                    bank = take(G, st)
                    if n >= 2:
                        act.wait_ge(ob_done, n - 1)
                    nc.scalar.copy(pq[n % 2], bank[:]).then_inc(G.freed(st), 1)
                elif kind == "mix" and st[1:] == (0, 0):
                    act.wait_ge(ws_t, 1)
                    nc.scalar.copy(wsT, banks[4][:].rearrange("p (c t) -> p c t", c=4)).then_inc(ws_t, 1)
                elif kind == "oc_turn":
                    _, g, j = st
                    bank = take(G, st)
                    nc.scalar.copy(ocT[:, g, j * HALF:(j + 1) * HALF], bank[:]).then_inc(G.freed(st), 1)
                elif kind == "merge":
                    key = ("gate",) + st[1:]
                    i = merge_index[st]
                    bank = take(G, key)
                    if i >= 2:
                        act.wait_ge(*G.drained(("branch",) + merge_steps[i - 2][1:]))
                    nc.scalar.activation(sig[i % 2], bank[:], ACT.Sigmoid).then_inc(G.freed(key), 1)
                elif kind == "merged_turn" and st[2] % 2:
                    _, j, k = st
                    bank = take(G, st)
                    nc.scalar.copy(mT[:, k, j * HALF:(j + 1) * HALF], bank[:]).then_inc(G.freed(st), 1)
                elif kind == "y":
                    t = st[1]
                    for n in range(2):
                        bank = take(G, st + (n,))
                        if t == 0 and n == 0:
                            act.wait_ge(*G.filled(("merged_turn", 1, NK - 1)))
                        if t >= 2 and n == 0:
                            act.wait_ge(d_h2[t % 2], 16 * (t // 2))
                            act.wait_ge(*G.filled(("h2_turn", t - 2, 1)))
                        nc.scalar.copy(ybuf[t % 2][:, n * HALF:(n + 1) * HALF], bank[:]).then_inc(G.freed(st + (n,)), 1)
                    act.wait_ge(*G.drained(st + (1,)))
                    nc.scalar.activation(o_sb[:].rearrange("p a b -> p (a b)"), ybuf[t % 2], ACT.Square, scale=1.0 / math.sqrt(D),
                                         accum_out=ss[:, t:t + 1]).then_inc(y_ss, 1)
                    act.wait_ge(x1_done, t + 1)
                    act.wait_ge(y_ss, t + 1)
                    nc.scalar.activation(o_sb[:].rearrange("p a b -> p (a b)"), x1[:, t, :], ACT.Square, scale=1.0 / math.sqrt(D),
                                         accum_out=ss[:, 8 + t:9 + t]).then_inc(x1_ss, 1)
                    act.wait_ge(x1_ss, t + 1)
                elif kind == "h2_turn":
                    t = st[1]
                    bank = take(G, st + (1,))
                    nc.scalar.copy(h2T[:, 4:8, t * P:(t + 1) * P], bank[:].rearrange("p (k t) -> p k t", k=4)).then_inc(G.freed(st + (1,)), 1)
                elif kind == "router":
                    act.wait_ge(r_sub, 1)
                    nc.scalar.activation(prob, prob, ACT.Exp).then_inc(r_exp, 1)

            act.wait_ge(r_exp, 1)
            act.wait_ge(G.sems["act"], G.count["act"])
            act.wait_ge(G.sems["dve"], G.count["dve"])
            for s, n in ((y_drained, 2), (a_drained, 2)):
                act.sem_inc(s, n)

            def drain_gathered(n):
                for j in range(2):
                    act.wait_ge(tx_full, n * 2 + (j + 1))
                    nc.scalar.copy(xeT[:, 4 * j:4 * j + 4, :], banks[4 + j][:].rearrange("p (k t) -> p k t", k=4)).then_inc(tx_drained, 1)

            def expert(e, last):
                for j in range(2):
                    act.wait_ge(ab_full, e * 4 + (2 * j + 1))
                    act.wait_ge(b_drained, e * 2 + (j + 1))
                    nc.scalar.activation(sa[j], banks[2 * j][:], ACT.Silu).then_inc(a_drained, 1)
                if not last:
                    drain_gathered(e + 1)
                act.wait_ge(cur_g, e + 1)
                for j in range(2):
                    act.wait_ge(y_full, e * 2 + (j + 1))
                    if j == 0:
                        act.wait_ge(added, e + 1)
                    nc.scalar.activation(yb[:, j * HALF:(j + 1) * HALF], banks[j][:], ACT.Identity, scale=gcur[:, 0:1]).then_inc(y_drained, 1)

            drain_gathered(0)
            with act.Fori(0, NE - 1) as e:
                expert(e, False)
            expert(NE - 1, True)
            for t in range(NT):
                act.wait_ge(d_fins[t], 16)
                nc.scalar.activation(o_sb[:].rearrange("p a b -> p (a b)"), fin[t], ACT.Square, scale=1.0 / math.sqrt(D),
                                     accum_out=ss[:, 16 + t:17 + t]).then_inc(f_ss, 1)
                act.wait_ge(f_ss, t + 1)

        @block.vector
        def _(dve):
            def take(stream, key):
                dve.wait_ge(*stream.filled(key))
                return stream.bank(key)

            n = [0]

            def step(ins):
                ins.then_inc(vstep, 1)
                n[0] += 1
                dve.wait_ge(vstep, n[0])

            nc.vector.memset(zero, 0.0).then_inc(zero_ready, 1)
            for st in STEPS:
                kind = st[0]
                if kind == "small":
                    step(nc.vector.tensor_copy(cols[:], take(G, st)[:, 0:20]))
                    nc.vector.tensor_copy(lb[:, 3, :], cols[:, 12:20]).then_inc(G.freed(st), 1)
                    dve.wait_ge(G.sems["dve"], 1)
                    nc.vector.tensor_tensor(lb[:, 0, :], lb[:, 3, :], lb[:, 3, :], ALU.subtract).then_inc(lb_max, 1)
                    dve.wait_ge(lb_ready, 1)
                    step(nc.vector.reciprocal(lb[:, 2, :], lb[:, 1, :]))
                    step(nc.vector.tensor_tensor(lb[:, 2, :], lb[:, 2, :], lb[:, 1, :], ALU.mult))
                    step(nc.vector.tensor_tensor(lb[:, 0, :], lb[:, 2, :], lb[:, 2, :], ALU.subtract))
                    nc.vector.tensor_scalar(gate_add[:], lb[:, 0, :], FLOOR, None, ALU.max)
                    step(nc.vector.tensor_scalar(gate_mul[:], lb[:, 0, :], -1.0, 1.0, ALU.mult, ALU.add))
                elif kind == "ada_cols":
                    nn = st[1]
                    bank = take(G, st)
                    dve.wait_ge(d_mod, 48)
                    nc.vector.tensor_tensor(adar[:, nn * HALF:(nn + 1) * HALF], bank[0:2, :],
                                            adab[:, nn * HALF:(nn + 1) * HALF], ALU.add).then_inc(G.freed(st), 1)
                elif kind == "ada_turn":
                    bank = take(G, st)
                    nc.vector.tensor_copy(shift1[:], bank[:, 0:16].rearrange("p (k j) -> p k j", j=2))
                    nc.vector.scalar_tensor_tensor(scale1[:], bank[:, 16:32].rearrange("p (k j) -> p k j", j=2), 1.0,
                                                   cols[:, 0:8].rearrange("p (k o) -> p k o", o=1).to_broadcast([P, NK, 2]), ALU.add, ALU.mult).then_inc(G.freed(st), 1)
                    dve.wait_ge(*G.drained(st))
                elif kind == "norm_x":
                    g = st[1]
                    nt = NTC if g == 0 else 4
                    dve.wait_ge(x_ss, (2, 6, 10)[g])
                    nc.vector.tensor_scalar(ss[:, 16 + 4 * g:16 + 4 * g + nt], ss[:, 4 * g:4 * g + nt], EPS, None, ALU.add).then_inc(x_ms, 1)
                    dve.wait_ge(x_rs, g + 1)
                    for t in range(nt):
                        ins = nc.vector.tensor_scalar(xbuf[g][:, t, :], xbuf[g][:, t, :], rs[:, 4 * g + t:4 * g + t + 1], None, ALU.mult)
                    ins.then_inc(x_normed, 1)
                    for k in range(0, NK, 2):
                        bank = take(G, st + (k,))
                        dst = hcT[:, k, :] if g == 0 else hT[:, k, (g - 1) * HALF:g * HALF]
                        w = TC if g == 0 else HALF
                        j = 1 if g == 0 else 0
                        nc.vector.tensor_scalar(dst, bank[:, 0:w], scale1[:, k, j:j + 1], shift1[:, k, j:j + 1],
                                                ALU.mult, ALU.add).then_inc(G.freed(st + (k,)), 1)
                elif kind == "prepare":
                    h = st[1]
                    B = hb[h % 2]
                    if h == 0:
                        dve.wait_ge(d_mask, 16)
                        step(nc.vector.tensor_copy(masks[:], mask_raw))
                    dve.wait_ge(*G.drained(("z", h, "fb", 2)))
                    for a in range(2):
                        mul, add = gate_mul[:, 4 * a + h:4 * a + h + 1], gate_add[:, 4 * a + h:4 * a + h + 1]
                        f = B["F"].rearrange("p (c a t) -> p c a t", c=NT, a=2)[:, :, a, :]
                        kk = (B["X2"], B["X1"])[a][:, :, a, :]
                        nc.vector.tensor_scalar(Fc[:, 0, a, :], Fc[:, 0, a, :], mul, add, ALU.mult, ALU.add)
                        nc.vector.tensor_scalar(Kc[:, a, :], Kc[:, a, :], mul, None, ALU.mult).then_inc(kc_ready, 1)
                        nc.vector.tensor_scalar(f, f, mul, add, ALU.mult, ALU.add)
                        ins = nc.vector.tensor_scalar(kk, kk, mul, None, ALU.mult)
                    step(ins)
                    F4 = B["F"].rearrange("p (c a t) -> p c a t", c=NT, a=2)
                    nc.vector.tensor_tensor(B["X1"][:, :, 0, :], B["A"], F4[:, :, 0, :], ALU.mult)
                    nc.vector.tensor_tensor(B["X2"][:, :, 1, :], B["A"], F4[:, :, 1, :], ALU.mult)
                    nc.vector.tensor_tensor(U.rearrange("p (c t) -> p c t", c=NT), B["X2"][:, :, 0, :],
                                            B["X1"][:, :, 1, :], ALU.add).then_inc(x_ready, 1)
                elif kind == "level" and st[2]:
                    _, h, l = st
                    B = hb[h % 2]
                    m = 1 << (l - 1)
                    if l == 1:
                        dve.wait_ge(L.freed(("level", h, 0, 1)), 2 * (h + 1))
                    else:
                        dve.wait_ge(x_ready, x_at(h, l - 1))
                    for j in range(2):
                        bank = take(L, st + (j,))
                        nc.vector.copy_predicated(B["A"][:, 4 * j:4 * j + 4, :], masks[:, l - 1:l, :].to_broadcast([P, 4, P]),
                                                  bank[:].rearrange("p (c t) -> p c t", c=4)).then_inc(L.freed(st + (j,)), 1)
                    nb = 2 * NT * P // (2 * m)
                    src, dst = (B["F"], U) if l % 2 else (U, B["F"])
                    if l == LEVELS:
                        dst = totals
                    pair = src[:, 0:2 * nb].rearrange("p (b two) -> p b two", two=2)
                    X1 = B["X1"].rearrange("p c a t -> p (c a t)").rearrange("p (b two m) -> p b two m", two=2, m=m)
                    X2 = B["X2"].rearrange("p c a t -> p (c a t)").rearrange("p (b two m) -> p b two m", two=2, m=m)
                    nc.vector.tensor_tensor(dst[:, 0:nb], pair[:, :, 0], pair[:, :, 1], ALU.mult)
                    nc.vector.tensor_tensor(X1[:, :, 1, :], X1[:, :, 1, :], pair[:, :, 0:1].to_broadcast([P, nb, m]), ALU.mult)
                    nc.vector.tensor_tensor(X2[:, :, 0, :], X2[:, :, 0, :], pair[:, :, 1:2].to_broadcast([P, nb, m]),
                                            ALU.mult).then_inc(x_ready, 1)
                elif kind == "kv":
                    h = st[1]
                    B = hb[h % 2]
                    tot = totals[:].rearrange("p (c a) -> p c a", a=2)
                    dve.wait_ge(x_ready, x_at(h, LEVELS))
                    dve.wait_ge(*S2.drained(("ctx_state", h)))
                    for half in range(2):
                        banks2 = [take(S2, st + (2 * half + a,)) for a in range(2)]
                        for i in range(4 - half):
                            for a in range(2):
                                ch = 4 * half + i if a == 0 else 7 - 4 * half - i
                                nx = ch + 1 if a == 0 else ch - 1
                                ins = nc.vector.scalar_tensor_tensor(S[:, a, nx, :], S[:, a, ch, :], tot[:, ch, a:a + 1],
                                                                     banks2[a][:, i * P:(i + 1) * P], ALU.mult, ALU.add)
                            step(ins)
                        for a in range(2):
                            dve.sem_inc(S2.freed(st + (2 * half + a,)), 1)
                    dve.sem_inc(s_ready, 1)
                elif kind == "out":
                    h = st[1]
                    dve.wait_ge(*S2.drained(("out", h, 1)))
                    step(nc.vector.tensor_reduce(ss[:, 32:40], o_sq, AX.X, ALU.add))
                    nc.vector.tensor_scalar(ss[:, 40:48], ss[:, 32:40], EPS, None, ALU.add).then_inc(o_ms, 1)
                    dve.wait_ge(o_rs, h + 1)
                    dve.wait_ge(o_gated, h + 1)
                    nc.vector.tensor_tensor(o_sb[:], o_sb[:], rs[:, 32:40].rearrange("p (c o) -> p c o", o=1).to_broadcast([P, NT, HD]),
                                            ALU.mult).then_inc(o_ready, 1)
                elif kind == "fold":
                    dve.wait_ge(*S2.filled(("out", H - 1, 1)))
                    dve.wait_ge(*G.drained(("zb", NT - 1)))
                    nc.vector.tensor_tensor(zfold[0], zb[:, 0:4, :], zb[:, 4:8, :], ALU.add).then_inc(fold_done, 1)
                    nc.vector.tensor_tensor(zfold[1], zb[:, 0:4, :], zb[:, 4:8, :], ALU.subtract).then_inc(fold_done, 1)
                elif kind == "vv_norm":
                    for j in range(4):
                        dve.wait_ge(vv_sq_ready, j + 1)
                        sq = big[:, 1024 * (j % 2):1024 * (j % 2 + 1)].rearrange("p (c t) -> p c t", t=P)
                        nc.vector.tensor_reduce(ss[:, 8 * j:8 * j + 8], sq, AX.X, ALU.add).then_inc(v_sq, 1)
                    dve.wait_ge(v_sq, 4)
                    nc.vector.tensor_scalar(ss[:, 0:32], ss[:, 0:32], EPS, None, ALU.add).then_inc(v_ms, 1)
                    dve.wait_ge(v_rs, 1)
                    v4 = vg.rearrange("p t (g n) -> p (t g) n", g=4)
                    step(nc.vector.tensor_tensor(v4, v4, rs[:, 0:32].rearrange("p (c o) -> p c o", o=1).to_broadcast([P, 32, P]), ALU.mult))
                    dve.wait_ge(d_late, 32)
                    nc.vector.tensor_tensor(vg, vg, snorm.rearrange("p (o n) -> p o n", o=1).to_broadcast([P, NT, 4 * P]), ALU.mult).then_inc(vv_done, 1)
                elif kind == "dft2":
                    _, g, par = st
                    i = 2 * g + par
                    dve.wait_ge(*G.drained(st))
                    b = pq[i % 2]
                    if par == 0:
                        nc.vector.tensor_tensor(obT[:, g, 2:HALF:2], b[:, 1:256], b[:, 257:512], ALU.subtract)
                        nc.vector.tensor_tensor(obT[:, g, T - 2:HALF:-2], b[:, 1:256], b[:, 257:512], ALU.add)
                        nc.vector.tensor_copy(obT[:, g, 0:HALF + 1:HALF], b[:, 0:257:256]).then_inc(ob_done, 1)
                    else:
                        nc.vector.tensor_tensor(obT[:, g, 1:HALF:2], b[:, 0:256], b[:, 256:512], ALU.subtract)
                        nc.vector.tensor_tensor(obT[:, g, T - 1:HALF:-2], b[:, 0:256], b[:, 256:512], ALU.add).then_inc(ob_done, 1)
                elif kind == "mix":
                    _, g, j = st
                    bank = take(G, st)
                    uu = ug[:, 4 * j:4 * j + 4, g * P:(g + 1) * P]
                    nc.vector.scalar_tensor_tensor(uu, bank[:].rearrange("p (t n) -> p t n", t=4), cols[:, 8 + g:9 + g], uu,
                                                   ALU.add, ALU.mult).then_inc(G.freed(st), 1)
                elif kind == "merge":
                    _, b, nn, t = st
                    i = merge_index[st]
                    key = ("branch",) + st[1:]
                    bank = take(G, key)
                    dve.wait_ge(*G.drained(("gate",) + st[1:]))
                    if b == 0:
                        nc.vector.tensor_tensor(merged[:, t, nn * HALF:(nn + 1) * HALF], bank[:], sig[i % 2], ALU.mult).then_inc(G.freed(key), 1)
                    else:
                        if i - 2 >= 2 * NT:
                            dve.wait_ge(merged_done, i - 1 - 2 * NT)
                        nc.vector.tensor_tensor(gated[i % 2], bank[:], sig[i % 2], ALU.mult).then_inc(G.freed(key), 1)
                elif kind == "ada_rows":
                    nn = st[1]
                    seg, j = nn // 2, nn % 2
                    bank = take(G, st)
                    dve.wait_ge(d_rb, 32 * (seg + 1))
                    dst = rows[:, seg, j * HALF:(j + 1) * HALF]
                    step(nc.vector.tensor_tensor(dst, bank[:], rowb[:, j * HALF:(j + 1) * HALF], ALU.add))
                    dve.sem_inc(G.freed(st), 1)
                    w = roww[:, j * HALF:(j + 1) * HALF]
                    if seg == 1:
                        dve.sem_inc(rows_done, 1)
                    elif seg == 2:
                        nc.vector.scalar_tensor_tensor(dst, dst, 1.0, w, ALU.add, ALU.mult).then_inc(rows_done, 1)
                    else:
                        nc.vector.tensor_tensor(dst, dst, w, ALU.mult).then_inc(rows_done, 1)
                elif kind == "merged_turn" and st[2] % 2 == 0:
                    _, j, k = st
                    bank = take(G, st)
                    nc.vector.tensor_copy(mT[:, k, j * HALF:(j + 1) * HALF], bank[:]).then_inc(G.freed(st), 1)
                elif kind == "y":
                    t = st[1]
                    y = ybuf[t % 2]
                    dve.wait_ge(y_ss, t + 1)
                    nc.vector.tensor_scalar(ss[:, 16 + t:17 + t], ss[:, t:t + 1], EPS, None, ALU.add).then_inc(y_ms, 1)
                    dve.wait_ge(rows_done, 8)
                    dve.wait_ge(y_rs, t + 1)
                    nc.vector.scalar_tensor_tensor(y, y, rs[:, t:t + 1], rows[:, 0, :], ALU.mult, ALU.mult).then_inc(yg, 1)
                    dve.wait_ge(d_xre[t % 2], 16 * (t // 2 + 1))
                    dve.wait_ge(yg, t + 1)
                    nc.vector.tensor_tensor(x1[:, t, :], y, xre[t % 2], ALU.add).then_inc(x1_done, 1)
                    dve.wait_ge(x1_ss, t + 1)
                    nc.vector.tensor_scalar(ss[:, 24 + t:25 + t], ss[:, 8 + t:9 + t], EPS, None, ALU.add).then_inc(x1_ms, 1)
                    dve.wait_ge(x1_rs, t + 1)
                    step(nc.vector.scalar_tensor_tensor(y, x1[:, t, :], rs[:, 8 + t:9 + t], rows[:, 2, :], ALU.mult, ALU.mult))
                    nc.vector.tensor_tensor(y, y, rows[:, 1, :], ALU.add).then_inc(h2_done, 1)
                elif kind == "h2_turn":
                    t = st[1]
                    bank = take(G, st + (0,))
                    nc.vector.tensor_copy(h2T[:, 0:4, t * P:(t + 1) * P], bank[:].rearrange("p (k t) -> p k t", k=4)).then_inc(G.freed(st + (0,)), 1)
                elif kind == "router":
                    bank = take(G, st + (0,))
                    dve.wait_ge(d_h2[0], 8 * NT)
                    logits = bank[:, 0:NT * NE].rearrange("p (t e) -> p t e", e=NE)
                    step(nc.vector.tensor_reduce(pmax[:], logits, AX.X, ALU.max))
                    step(nc.vector.tensor_tensor(prob, logits, pmax[:].rearrange("p (t o) -> p t o", o=1).to_broadcast([P, NT, NE]), ALU.subtract))
                    dve.sem_inc(G.freed(st + (0,)), 1)
                    dve.sem_inc(r_sub, 1)
                    dve.wait_ge(r_exp, 1)
                    step(nc.vector.tensor_reduce(psumm[:], prob, AX.X, ALU.add))
                    step(nc.vector.reciprocal(psumm[:], psumm[:]))
                    nc.vector.tensor_tensor(prob, prob, psumm[:].rearrange("p (t o) -> p t o", o=1).to_broadcast([P, NT, NE]),
                                            ALU.mult).then_inc(r_prob, 1)
                elif kind == "router_turn":
                    for j in range(2):
                        bank = take(G, st + (j,))
                        nc.vector.tensor_copy(aff[:, j * HALF:(j + 1) * HALF], bank[0:NE, :]).then_inc(G.freed(st + (j,)), 1)
                    dve.wait_ge(*G.drained(st + (1,)))
                elif kind == "choose":
                    a, b = aff, aff2
                    for r in range(CAP // 8):
                        v8, i8 = topv[:, 8 * r:8 * r + 8], topi[:, 8 * r:8 * r + 8]
                        step(nc.vector.max(v8, a))
                        nc.vector.max_index(i8, v8, a)
                        step(nc.vector.match_replace(b, v8, a, -1.0))
                        a, b = b, a
                    nc.vector.tensor_copy(topf, topi).then_inc(chosen, 1)
                elif kind == "choose_turn":
                    nc.vector.tensor_copy(gates[:], take(G, st + (0,))[:, 0:NE]).then_inc(G.freed(st + (0,)), 1)
                    nc.vector.tensor_copy(idx[:], take(G, st + (1,))[:, 0:NE]).then_inc(G.freed(st + (1,)), 1)

            dve.wait_ge(G.sems["dve"], G.count["dve"])
            dve.sem_inc(b_drained, 2)
            dve.sem_inc(th_drained, 2)

            def expert(e):
                for j in range(2):
                    dve.wait_ge(a_drained, e * 2 + (j + 3))
                    dve.wait_ge(ab_full, e * 4 + (2 * j + 2))
                    nc.vector.tensor_tensor(hid[:, j * HALF:(j + 1) * HALF], banks[2 * j + 1][:], sa[j], ALU.mult).then_inc(b_drained, 1)
                for j in range(2):
                    dve.wait_ge(th_full, e * 2 + (j + 1))
                    nc.vector.tensor_copy(hidT[:, 4 * j:4 * j + 4, :], banks[6 + j][:].rearrange("p (k t) -> p k t", k=4)).then_inc(th_drained, 1)

            with dve.Fori(0, NE) as e:
                expert(e)
            for t in range(NT):
                dve.wait_ge(f_ss, t + 1)
                nc.vector.tensor_scalar(ss[:, 24 + t:25 + t], ss[:, 16 + t:17 + t], EPS, None, ALU.add).then_inc(f_ms, 1)
                dve.wait_ge(f_rs, t + 1)
                step(nc.vector.scalar_tensor_tensor(fin[t], fin[t], rs[:, 16 + t:17 + t], rows[:, 3, :], ALU.mult, ALU.mult))
                nc.vector.tensor_tensor(fin[t], fin[t], x1[:, t, :], ALU.add).then_inc(f_out, 1)

        @block.gpsimd
        def _(pool):
            def root(dst, src, w):
                return nc.gpsimd.tensor_tensor(dst, src, half_pow[:, 0:w], ALU.pow)

            nc.gpsimd.memset(ident[:], 0.0).then_inc(ident_ready, 1)
            nc.gpsimd.memset(half_pow[:], -0.5).then_inc(pow_ready, 1)
            pool.wait_ge(ident_ready, 1)
            nc.gpsimd.affine_select(out=ident[:], in_=ident[:], compare_op=ALU.not_equal, fill=1.0, base=0,
                                    pattern=[[-1, P]], channel_multiplier=1).then_inc(ident_ready, 1)
            pool.wait_ge(pow_ready, 1)
            n = [0]
            for st in STEPS:
                kind = st[0]
                if kind == "norm_x":
                    g = st[1]
                    nt = NTC if g == 0 else 4
                    pool.wait_ge(x_ms, g + 1)
                    root(rs[:, 4 * g:4 * g + nt], ss[:, 16 + 4 * g:16 + 4 * g + nt], nt).then_inc(x_rs, 1)
                elif kind == "ga":
                    t = st[1]
                    if t == 0:
                        pool.wait_ge(d_row, 16)
                    pool.wait_ge(*G.drained(st))
                    g4 = Gt[:, t, :].rearrange("p (h n) -> p h n", h=H)
                    nc.gpsimd.tensor_tensor(g4, g4, gnorm[:].rearrange("p (o n) -> p o n", o=1).to_broadcast([P, H, HD]), ALU.mult).then_inc(ga_gated, 1)
                elif kind == "prepare":
                    h = st[1]
                    pool.wait_ge(kc_ready, 2 * (h + 1))
                    for l in range(8):
                        m = 1 << l
                        nb = TC // (2 * m)
                        src, dst = Fc[:, l % 2], Fc[:, 1 - l % 2]
                        pair = src[:, :, 0:2 * nb].rearrange("p a (b two) -> p a b two", two=2)
                        kf = Kc[:, 0, :].rearrange("p (b two m) -> p b two m", two=2, m=m)
                        kb = Kc[:, 1, :].rearrange("p (b two m) -> p b two m", two=2, m=m)
                        nc.gpsimd.tensor_tensor(kf[:, :, 0, :], kf[:, :, 0, :], pair[:, 0, :, 1:2].to_broadcast([P, nb, m]), ALU.mult)
                        ins = nc.gpsimd.tensor_tensor(kb[:, :, 1, :], kb[:, :, 1, :], pair[:, 1, :, 0:1].to_broadcast([P, nb, m]), ALU.mult)
                        if l < 7:
                            ins = nc.gpsimd.tensor_tensor(dst[:, :, 0:nb], pair[:, :, :, 0], pair[:, :, :, 1], ALU.mult)
                            ins.then_inc(pstep, 1)
                            n[0] += 1
                            pool.wait_ge(pstep, n[0])
                        else:
                            ins.then_inc(ctx_done, 1)
                elif kind == "out":
                    h = st[1]
                    pool.wait_ge(o_ms, h + 1)
                    root(rs[:, 32:40], ss[:, 40:48], 8).then_inc(o_rs, 1)
                    if h == 0:
                        pool.wait_ge(ga_gated, NT)
                    pool.wait_ge(*S2.drained(("out", h, 1)))
                    nc.gpsimd.tensor_tensor(o_sb[:], o_sb[:], Gt[:, :, h * HD:(h + 1) * HD], ALU.mult).then_inc(o_gated, 1)
                elif kind == "vv_norm":
                    pool.wait_ge(v_ms, 1)
                    root(rs[:, 0:32], ss[:, 0:32], 32).then_inc(v_rs, 1)
                elif kind == "merge" and st[1] != 0:
                    _, b, nn, t = st
                    i = merge_index[st]
                    pool.wait_ge(*G.drained(("branch",) + st[1:]))
                    mm = merged[:, t, nn * HALF:(nn + 1) * HALF]
                    nc.gpsimd.tensor_tensor(mm, mm, gated[i % 2], ALU.add).then_inc(merged_done, 1)
                elif kind == "ada_rows" and st[1] == 0:
                    pool.wait_ge(ob_done, 8)
                    nc.gpsimd.tensor_copy(cbig, csilu[:, 0, :].rearrange("p (k o) -> p k o", o=1).to_broadcast([P, NK, P])).then_inc(cbig_ready, 1)
                elif kind == "y":
                    t = st[1]
                    pool.wait_ge(y_ms, t + 1)
                    root(rs[:, t:t + 1], ss[:, 16 + t:17 + t], 1).then_inc(y_rs, 1)
                    pool.wait_ge(x1_ms, t + 1)
                    root(rs[:, 8 + t:9 + t], ss[:, 24 + t:25 + t], 1).then_inc(x1_rs, 1)

            pool.wait_ge(G.sems["dve"], G.count["dve"])
            for j in range(2):
                pool.wait_ge(d_h2[j], 8 * NT)
            pool.wait_ge(d_zero, 16 * NT)
            pool.sem_inc(added, 1)

            def wait(semaphore, value):
                pool.wait_ge(semaphore, value)
                pool.sem_inc(tick, 1)

            def gather(e):
                nc.gpsimd.tensor_copy(icur[:, :], idx[:, bass.ds(e, 1)]).then_inc(cur_done, 1)
                wait(cur_done, e + 1)
                pool.indirect_dma_start(xg, None, h2_dram[:, :], bass.IndirectOffsetOnAxis(ap=icur[:, 0:1], axis=0),
                                        bounds_check=T - 1).then_inc(xg_full, 16)

            def scatter(e):
                wait(y_drained, e * 2 + 4)
                pool.indirect_dma_start(moe_dram[:, :], bass.IndirectOffsetOnAxis(ap=icur2[:, 0:1], axis=0), yb, None,
                                        compute_op=ALU.add, bounds_check=T - 1).then_inc(sc_done, 16)

            gather(0)
            def expert(e, last):
                if True:
                    nc.gpsimd.tensor_copy(icur2[:, :], idx[:, bass.ds(e, 1)])
                    nc.gpsimd.tensor_copy(gcur[:, :], gates[:, bass.ds(e, 1)]).then_inc(cur_g, 1)
                if not last:
                    wait(tx_full, e * 2 + 2)
                    gather(e + 1)
                wait(cur_g, e + 1)
                scatter(e)
                wait(sc_done, e * 16 + 16)
                pool.sem_inc(added, 1)
            with pool.Fori(0, NE - 1) as e:
                expert(e, False)
            expert(NE - 1, True)
            for t in range(NT):
                pool.wait_ge(f_ms, t + 1)
                root(rs[:, 16 + t:17 + t], ss[:, 24 + t:25 + t], 1).then_inc(f_rs, 1)


_INS = ["x", "c", "ctx", "c_ctx", "ada_w", "ada_b", "norm_w", "w_in", "hgrn_lb_raw", "hgrn_gnorm_w", "sgu_w", "sgu_b",
        "sgu_norm_w", "w_branch", "w_out", "router_w", "exp_w13", "exp_w2"]


def kernel(**inputs):
    import concourse.bacc as bacc
    from concourse.bass_utils import run_bass_kernel_spmd

    nc = bacc.Bacc("TRN2", target_bir_lowering=False, num_devices=1)
    arrays, args = {}, []
    tokens, channels = dft_tables()
    extra = dict(token_dft=tokens, channel_dft=channels, level_masks=level_masks())
    for name in _INS + list(extra):
        a = np.ascontiguousarray(inputs[name] if name in inputs else extra[name])
        arrays[f"in_{name}"] = a
        args.append(nc.dram_tensor(f"in_{name}", a.shape, mybir.dt.from_np(a.dtype), kind="ExternalInput").ap())
    out = nc.dram_tensor("out", (1, T, D), F32, kind="ExternalOutput").ap()
    h2 = nc.dram_tensor("h2", (T, D), F32, kind="Internal").ap()
    moe = nc.dram_tensor("moe", (T, D), F32, kind="Internal").ap()
    build(nc, *args, out, h2, moe)
    r = run_bass_kernel_spmd(nc, [arrays], core_ids=[0])
    return r.results[0]["out"]
```

```python
import math
from contextlib import ExitStack

import numpy as np

import concourse.bass as bass
from concourse import mybir

ALU = mybir.AluOpType
ACT = mybir.ActivationFunctionType
AX = mybir.AxisListType
F32 = mybir.dt.float32
F32R = mybir.dt.float32r
U32 = mybir.dt.uint32
U8 = mybir.dt.uint8

P = 128
D = 1024
T = 1024
TC = 256
H = 4
HD = 128
AW = H * HD
NE = 16
CAP = 2 * T // NE
NK = D // P
NT = T // P
NTC = TC // P
HALF = 512
EPS = 1e-6
FLOOR = 1e-20
LEVELS = 7
COL = dict(q=0, ff=AW, fb=2 * AW, i=3 * AW, ga=4 * AW, zb=5 * AW, u=6 * AW, v=7 * AW, gate=8 * AW)
SLOTS = 4
BLK = NK * HALF
UNIT = 4 * HALF
UNITS = 12
RAW = 6
PAIRS = 6
BY_POOL = (1, 4, 7, 10)
MERGE = [(b, j) for b in (0, 2, 1) for j in range(NK)]
PART = 4 * P
MERGE_UNITS = 3 * len(MERGE)
RING = 4
ADA_AT = {NK - 1 + i: i for i in range(16)}


def dft_tables():
    t = np.arange(T // 2)[:, None].astype(np.float64)
    even, odd = np.arange(0, T // 2 + 1, 2), np.arange(1, T // 2, 2)
    w = 2 * np.pi / T
    parts = [np.cos(w * ((t * even) % T)), np.sin(w * ((t * even[1:-1]) % T)),
             np.cos(w * ((t * odd) % T)), np.sin(w * ((t * odd) % T))]
    tokens = np.concatenate(parts, 1)
    d = np.arange(HD)[:, None] * np.arange(HD)[None, :] % HD * (2 * np.pi / HD)
    s = 1.0 / math.sqrt(T * HD)
    channels = np.concatenate([np.cos(d) * s, np.sin(d) * s], 1)
    return tokens.astype(np.float32), channels.astype(np.float32)


def level_masks():
    s, t = np.arange(P)[:, None], np.arange(P)[None, :]
    out = [(s // (2 * m) == t // (2 * m)) & (s // m != t // m) for m in (1 << l for l in range(LEVELS))]
    return np.stack(out, 1).astype(np.float32)


class Psum:

    def __init__(self, banks, full, drained):
        self.banks, self.full, self.sems = banks, full, drained
        self.keys, self.count, self.n = {}, {e: 0 for e in drained}, 0
        self.jobs = []

    def plan(self, key, consumer):
        assert key not in self.keys, key
        self.count[consumer] += 1
        self.keys[key] = self.n
        self.jobs.append((consumer, self.count[consumer]))
        self.n += 1

    def bank(self, key):
        return self.banks[self.keys[key] % len(self.banks)]

    def reuses(self, key):
        return self.keys[key] >= len(self.banks)

    def last_drained(self, key):
        consumer, count = self.jobs[self.keys[key] - len(self.banks)]
        return self.sems[consumer], count

    def filled(self, key):
        return self.full, self.keys[key] + 1

    def freed(self, key):
        return self.sems[self.jobs[self.keys[key]][0]]

    def drained(self, key):
        consumer, count = self.jobs[self.keys[key]]
        return self.sems[consumer], count


def schedule():
    steps = [("small",)]
    steps += [("ada_cols", n) for n in range(4)] + [("ada_turn",)]
    steps += [("norm_s", 0), ("norm_s", 1), ("norm_x", 0), ("norm_s", 2), ("norm_x", 1), ("norm_x", 2)]
    steps += [("v", t) for t in range(NTC + NT)] + [("ga", t) for t in range(NT)]

    def z_units(h):
        return [("z", h, w, j) for w in ("ff", "fb", "q") for j in range(2 if w == "q" else 3)]

    steps += z_units(0) + [("prepare", 0, part) for part in range(3)]
    for h in range(H):
        fill = z_units(h + 1) if h + 1 < H else [("zb", t) for t in range(NT)]
        steps += [("level", h, 0), ("level", h, 1), fill[0]]
        steps += [("ctx_turn", h), ("level", h, 2), fill[1], ("ctx_state", h)]
        if h:
            steps += [("o_turn", h - 1)]
        steps += [("level", h, 3), fill[2], ("level", h, 4), fill[3]]
        if h + 1 < H:
            steps += [("prepare", h + 1, 0)]
        steps += [("level", h, 5), fill[4], ("level", h, 6), fill[5], ("level", h, 7), fill[6], ("k_turn", h)]
        if h + 1 < H:
            steps += [("prepare", h + 1, 1)]
        steps += [fill[7], ("kv", h)]
        if h + 1 < H:
            steps += [("prepare", h + 1, 2)]
        steps += [("out", h)]
    steps += [("fold",)]
    steps += [("u", t) for t in range(NT)] + [("o_turn", H - 1)] + [("vv", t) for t in range(NT)]
    steps += [("vv_norm",)]
    for g in range(4):
        for par in range(2):
            steps += [("dft", g, par), ("h_split", 2 * g + par)]
    for g in range(4):
        steps += [("dft2", g, 0), ("dft2", g, 1), ("o_split", 0, g)]
    steps += [("mix", g, j) for g in range(4) for j in range(2)]
    steps += [("oc_turn", g, j) for g in range(4) for j in range(2)]
    for q, (b, j) in enumerate(MERGE):
        if j == 0 and q:
            steps += [("o_split", b, g) for g in range(4)]
        if q == len(MERGE) - 1:
            steps += [("out_split", 0)]
        steps += [("merge", q)]
        if ADA_AT.get(q - 1, 0) % 2:
            steps += [("ada_rows", ADA_AT[q - 1] // 2)]
        if q in ADA_AT:
            steps += [("ada_sum", ADA_AT[q])]
    steps += [("out_split", 1), ("m_split", 0), ("out_split", 2), ("m_split", 1), ("out_split", 3)]
    for t in range(NT):
        steps += [("y", t)] + ([("m_split", t + 2)] if t + 2 < NT else []) + [("y_norm", t)]
        steps += [("h2_turn", t - 1)] if t else []
    steps += [("h2_turn", NT - 1), ("router",), ("router_turn",), ("choose",), ("choose_turn",)]
    return steps


def weight_blocks():
    blocks = [("ada_cols", n) for n in range(4)] + [("v",), ("ga",)] + [("z", h) for h in range(H)]
    return blocks + [("zb",), ("u",), ("vv",)]


def build(nc, x, c, ctx_in, c_ctx, ada_w, ada_b, norm_w, w_in, hgrn_lb_raw, hgrn_gnorm_w, sgu_w, sgu_b,
          sgu_norm_w, w_branch, w_out, router_w, exp_w13, exp_w2, token_dft, channel_dft, masks_in, out,
          h2_dram, moe_dram, x1_dram):
    STEPS, BLOCKS = schedule(), weight_blocks()
    with ExitStack() as stack:
        def sb(name, shape, dt=F32):
            return stack.enter_context(nc.sbuf_tensor(name, shape, dt))

        def sem(name):
            return stack.enter_context(nc.semaphore(name))

        space = -(-nc.sbuf_base // 32) * 32
        sb("fence", [P, 49152])
        AT_H, AT_W, AT_V, AT_OA, AT_A, AT_B = 0, 8192, 20480, 28672, 32768, 40960

        def place(name, at, n, dt=F32):
            return nc.alloc_sbuf_tensor_at(name, [P, n], dt, offset=space + 4 * at)

        r_h = place("r_h", AT_H, NK * T)
        r_w = place("r_w", AT_W, 3 * BLK)
        r_v = place("r_v", AT_V, 2 * NT * AW)
        r_oa = place("r_oa", AT_OA, H * T)
        r_a = place("r_a", AT_A, 8192)
        r_b = place("r_b", AT_B, 8192)

        r_c = sb("r_c", [P, NK * TC])
        hT = r_h[:].rearrange("p (k t) -> p k t", k=NK)
        hcT = r_c[:].rearrange("p (k t) -> p k t", k=NK)
        wslot = [r[:, s * BLK:(s + 1) * BLK].rearrange("p (k n) -> p k n", k=NK) for r in (r_w, r_v) for s in range(2)]
        V = r_v[:, 0:NT * AW].rearrange("p (t n) -> p t n", t=NT)
        Gt = r_v[:, NT * AW:].rearrange("p (t n) -> p t n", t=NT)
        oaT = r_oa[:].rearrange("p (h t) -> p h t", h=H)
        U = r_b[:, 7168:8192]
        totals = sb("totals", [P, 2 * NT])
        hb = []
        for r in (r_a, r_b):
            hb.append(dict(X1=r[:, 0:2048].rearrange("p (c a t) -> p c a t", c=NT, a=2),
                           X2=r[:, 2048:4096].rearrange("p (c a t) -> p c a t", c=NT, a=2),
                           F=r[:, 4096:6144],
                           A=r[:, 6144:7168].rearrange("p (c t) -> p c t", c=NT)))
        xbuf = [r_a[:, 0:4096].rearrange("p (t n) -> p t n", t=4), r_b[:, 0:4096].rearrange("p (t n) -> p t n", t=4),
                r_a[:, 4096:8192].rearrange("p (t n) -> p t n", t=4)]
        adar = r_oa[0:2, 0:2048]
        adab = r_oa[0:2, 2048:4096]
        zb = r_a[:, 0:4096].rearrange("p (t n) -> p t n", t=NT)
        tdft = r_a[:, 4096:8192].rearrange("p (t n) -> p t n", t=4)
        zfold = [r_b[:, 0:2048].rearrange("p (t n) -> p t n", t=4),
                 r_b[:, 2048:4096].rearrange("p (t n) -> p t n", t=4)]
        AB = r_b[:, 4096:8192].rearrange("p (g e n) -> p g e n", g=4, e=2)
        obT = r_a[:, 0:4096].rearrange("p (g t) -> p g t", g=4)
        vg = V
        ug = Gt
        ocT = r_a[:, 4096:8192].rearrange("p (g t) -> p g t", g=4)
        mT = r_b[:].rearrange("p (k t) -> p k t", k=NK)
        rows = r_oa[:].rearrange("p (r n) -> p r n", r=4)
        x1 = r_a[:].rearrange("p (t n) -> p t n", t=NT)
        h2T = mT
        ybuf = [r_v[:, 6144 + 1024 * i:7168 + 1024 * i] for i in range(2)]
        xre = [r_v[:, 4096 + 1024 * i:5120 + 1024 * i] for i in range(2)]
        h_hi = place("h_hi", AT_W, NK * T, F32R)[:].rearrange("p (k t) -> p k t", k=NK)
        h_lo = place("h_lo", AT_H, NK * T, F32R)[:].rearrange("p (k t) -> p k t", k=NK)
        o_hi = place("o_hi", AT_W + 2 * BLK, H * T, F32R)[:].rearrange("p (k t) -> p k t", k=H)
        o_lo = [place(f"o_lo{b}", at, H * T, F32R)[:].rearrange("p (k t) -> p k t", k=H)
                for b, at in enumerate((AT_OA, AT_A, AT_A + 4096))]
        raw_m = [r_v[:, u * PART:(u + 1) * PART].rearrange("p (k n) -> p k n", k=4) for u in range(RING)]
        wm = place("wm", AT_V + RING * PART, 2 * RING * PART, F32R)
        wm_hi = [wm[:, 2 * u * PART:(2 * u + 1) * PART].rearrange("p (k n) -> p k n", k=4) for u in range(RING)]
        wm_lo = [wm[:, (2 * u + 1) * PART:(2 * u + 2) * PART].rearrange("p (k n) -> p k n", k=4) for u in range(RING)]
        out_raw = [x.rearrange("p (k n) -> p k n", k=4) for x in (
            r_a[:, 4096:6144], r_a[:, 6144:8192], r_c[:], r_w[:, 2 * BLK:2 * BLK + 2048])]
        out_hi = place("out_hi", AT_W, 2 * BLK, F32R)[:].rearrange("p (n k c) -> p n k c", n=2, k=NK)
        out_lo = place("out_lo", AT_H, 2 * BLK, F32R)[:].rearrange("p (n k c) -> p n k c", n=2, k=NK)
        mt_hi = place("mt_hi", AT_V, 2 * D, F32R)[:].rearrange("p (s k t) -> p s k t", s=2, k=NK)
        mt_lo = place("mt_lo", AT_V + 2 * D, 2 * D, F32R)[:].rearrange("p (s k t) -> p s k t", s=2, k=NK)

        ident = sb("ident", [P, P])
        half_pow = sb("half_pow", [P, 32])
        small = sb("small", [20, P])
        cols = sb("cols", [P, 20])
        gate_add = sb("gate_add", [P, 8])
        gate_mul = sb("gate_mul", [P, 8])
        lb = sb("lb", [P, 4, 8])
        craw = sb("craw", [P, 2, NK])
        csilu = sb("csilu", [P, 2, NK])
        scale1 = sb("scale1", [P, NK, 2])
        shift1 = sb("shift1", [P, NK, 2])
        ss = sb("ss", [P, 48])
        rs = sb("rs", [P, 48])
        masks = sb("masks", [P, LEVELS, P], U8)
        gnorm = sb("gnorm", [P, HD])
        Vc = r_oa[:, 3072:4096].rearrange("p (t n) -> p t n", t=NTC)
        Fc = r_oa[:, 2048:3072].rearrange("p (i a t) -> p i a t", i=2, a=2)
        Kc = r_a[:, 7168:7680].rearrange("p (a t) -> p a t", a=2)
        big = r_w[:, 2 * BLK:3 * BLK]
        KT = big[:, 0:2048].rearrange("p (a c k) -> p a c k", a=2, c=NT)
        S = big[:, 2048:4096].rearrange("p (a c k) -> p a c k", a=2, c=NT)
        KcT = big[:, 0:512].rearrange("p (c k) -> p c k", c=4)
        o_sb = sb("o_sb", [P, NT, HD])
        o_sq = big[:, 1024:2048].rearrange("p (c t) -> p c t", c=NT)
        zero = big[:, 1024:2048]
        mask_raw = big[:, 0:LEVELS * P].rearrange("p (l t) -> p l t", t=P)
        wsraw = o_sb[:, 0:4, :]
        wsT = o_sb[:, 4:8, :]
        pq = [r_c[:, 512 * i:512 * (i + 1)] for i in range(2)]
        snorm = r_c[:, 1024:1536]
        cdft = r_c[:, 1536:1792]
        sig = [r_v[:, 6144 + 512 * i:6656 + 512 * i] for i in range(2)]
        gated = [r_v[:, 7168 + 512 * i:7680 + 512 * i] for i in range(2)]
        ada_part = r_c[:].rearrange("p (k n) -> p k n", k=4)
        flat = o_sb[:].rearrange("p a b -> p (a b)")
        ada_bias, norm_row = flat[:, 0:HALF], flat[:, HALF:]
        ones = gnorm
        rw = gnorm[:].rearrange("p (k e) -> p k e", e=NE)
        prob = r_v[:, 2816:2944].rearrange("p (t e) -> p t e", e=NE)
        pmax = sb("pmax", [P, NT])
        psumm = sb("psumm", [P, NT])
        aff, aff2 = r_v[0:NE, 0:1024], r_v[0:NE, 1024:2048]
        topv, topf = r_v[0:NE, 2048:2048 + CAP], r_v[0:NE, 2048 + CAP:2048 + 2 * CAP]
        topi = r_v[0:NE, 2048 + 2 * CAP:2048 + 3 * CAP].bitcast(U32)
        gates = sb("gates", [P, NE])
        idx = sb("idx", [P, NE], U32)
        raw = [r_w[:, u * UNIT:(u + 1) * UNIT].rearrange("p (k n) -> p k n", k=4) for u in range(RAW)]
        def pairs(name, at, n):
            t = place(name, at, n * UNIT, F32R)
            return [t[:, u * UNIT:(u + 1) * UNIT].rearrange("p (k n) -> p k n", k=4) for u in range(n)]

        whi = pairs("w_hi0", AT_H, 4) + pairs("w_hi1", AT_A, 2)
        wlo = pairs("w_lo0", AT_B, 4) + pairs("w_lo1", AT_A + 4096, 2)
        x1_again = r_w[:, 0:NT * D].rearrange("p (t n) -> p t n", t=NT)
        xg = r_v[:, 0:1024]
        hid = r_v[:, 1024:2048]
        sa = [r_v[:, 2048 + 512 * i:2560 + 512 * i] for i in range(2)]
        yb = r_v[:, 3072:4096]
        m_x = place("m_x", AT_V + 4096, 2048, F32R)
        m_t = place("m_t", AT_V + 6144, 2048, F32R)
        xe_hi, xe_lo = (m_x[:, 1024 * i:1024 * (i + 1)].rearrange("p (k t) -> p k t", k=NK) for i in range(2))
        ht_hi, ht_lo = (m_t[:, 1024 * i:1024 * (i + 1)].rearrange("p (k t) -> p k t", k=NK) for i in range(2))
        gcur = sb("gcur", [P, 1])
        icur = sb("icur", [P, 1], U32)
        icur2 = sb("icur2", [P, 1], U32)
        fin = [r_b[:, 1024 * i:1024 * (i + 1)] for i in range(8)]

        banks = [stack.enter_context(nc.psum_tensor(f"bank{i}", [P, 512], F32)) for i in range(8)]
        G = Psum(banks[0:4], sem("g_full"), dict(act=sem("g_drained_act"), dve=sem("g_drained_dve")))
        L = Psum(banks[4:6], sem("l_full"), dict(act=sem("l_drained_act"), dve=sem("l_drained_dve")))
        S2 = Psum(banks[6:8], sem("s_full"), dict(act=sem("s_drained_act"), dve=sem("s_drained_dve")))

        block_jobs = {}
        for st in STEPS:
            k = st[0]
            if k in ("small", "ada_cols", "ada_turn"):
                G.plan(st, "dve")
            elif k == "norm_x":
                for kk in range(NK):
                    G.plan(st + (kk,), "act" if kk % 2 else "dve")
            elif k in ("v", "ga", "z", "zb", "u", "vv", "oc_turn"):
                G.plan(st, "act")
            elif k == "level":
                for j in range(2):
                    L.plan(st + (j,), "dve" if st[2] else "act")
            elif k in ("ctx_turn", "ctx_state"):
                S2.plan(st, "act")
            elif k == "k_turn":
                for j in range(4):
                    S2.plan(st + (j,), "act")
            elif k == "kv":
                for j in range(4):
                    S2.plan(st + (j,), "dve")
            elif k == "out":
                for j in range(2):
                    S2.plan(st + (j,), "act")
            elif k == "o_turn":
                for j in range(2):
                    S2.plan(st + (j,), "act")
            elif k in ("dft", "dft2"):
                G.plan(st, "act")
            elif k in ("mix", "ada_rows"):
                G.plan(st, "dve")
            elif k == "merge":
                for j in range(2):
                    G.plan(("gate",) + st[1:] + (j,), "act")
                for j in range(2):
                    G.plan(("branch",) + st[1:] + (j,), "dve")
            elif k == "y":
                for n in range(2):
                    G.plan(st + (n,), "act")
            elif k == "h2_turn":
                for j in range(2):
                    G.plan(st + (j,), "act" if j else "dve")
            elif k == "router":
                G.plan(st + (0,), "dve")
            elif k in ("router_turn", "choose_turn"):
                for j in range(2):
                    G.plan(st + (j,), "dve")
            if k == "ada_cols":
                block_jobs[st] = st
            elif k in ("v", "ga", "zb", "u", "vv"):
                block_jobs[(k,)] = st
            elif k == "z":
                block_jobs[("z", st[1])] = st
        SLOT = {b: i if i < SLOTS else i % 2 for i, b in enumerate(BLOCKS)}
        w_full = [sem(f"w_full{s}") for s in range(SLOTS)]
        w_count, last_in, before = {}, {}, {}
        for b in BLOCKS:
            before[b] = last_in.get(SLOT[b])
            w_count[b] = w_count.get(before[b], 0) + (48 if b[0] == "z" else 16)
            last_in[SLOT[b]] = b

        d_small, d_mod, d_row, d_late, d_mask, d_tab, d_ws = (sem(n) for n in ("d_small", "d_mod", "d_row", "d_late", "d_mask", "d_tab", "d_ws"))
        d_x = [sem(f"d_x{g}") for g in range(3)]
        d_xre = [sem("d_xre0"), sem("d_xre1")]
        d_h2, d_zero = [sem("d_h2_0"), sem("d_h2_1")], sem("d_zero")
        ident_ready, pow_ready, zero_ready = sem("ident_ready"), sem("pow_ready"), sem("zero_ready")
        csilu_ready = sem("csilu_ready")
        lb_max, lb_ready = sem("lb_max"), sem("lb_ready")
        x_ss, x_ms, x_rs, x_normed = sem("x_ss"), sem("x_ms"), sem("x_rs"), sem("x_normed")
        ga_gated = sem("ga_gated")
        x_ready = sem("x_ready")
        kc_ready = sem("kc_ready")
        ctx_done = sem("ctx_done")
        s_ready = sem("s_ready")
        o_ms, o_rs, o_gated, o_ready = (sem(n) for n in ("o_ms", "o_rs", "o_gated", "o_ready"))
        fold_done, vv_done = sem("fold_done"), sem("vv_done")
        v_sq, v_ms, v_rs = sem("v_sq"), sem("v_ms"), sem("v_rs")
        ws_t, vv_sq_ready, ob_done = sem("ws_t"), sem("vv_sq_ready"), sem("ob_done")
        merged_done = sem("merged_done")
        rows_done = sem("rows_done")
        h_hi_done, h_lo_done, o_hi_done, o_lo_done = sem("h_hi_done"), sem("h_lo_done"), sem("o_hi_done"), sem("o_lo_done")
        m_full = [sem(f"m_full{s}") for s in range(RING)]
        m_hi_done, m_lo_done, m_used = sem("m_hi_done"), sem("m_lo_done"), sem("m_used")
        d_ada, d_rows, ones_ready, ada_summed, ada_added = (sem(n) for n in ("d_ada", "d_rows", "ones_ready", "ada_summed", "ada_added"))
        d_out_w = [sem(f"d_out_w{s}") for s in range(4)]
        out_hi_done, out_lo_done, mt_hi_done, mt_lo_done = (sem(n) for n in ("out_hi_done", "out_lo_done", "mt_hi_done", "mt_lo_done"))
        y_ss, y_ms, y_rs, x1_done, x1_ss, x1_ms, x1_rs, h2_done = (sem(n) for n in (
            "y_ss", "y_ms", "y_rs", "x1_done", "x1_ss", "x1_ms", "x1_rs", "h2_done"))
        yg = sem("yg")
        r_sub, r_exp, r_prob, chosen = (sem(n) for n in ("r_sub", "r_exp", "r_prob", "chosen"))
        vstep, pstep, tick = sem("dve_step"), sem("pool_step"), sem("pool_tick")
        added = sem("added")
        raw_full = [sem(f"raw_full{s}") for s in range(RAW)]
        hi_done, used = sem("hi_done"), sem("used")
        lo_dve, lo_pool = sem("lo_dve"), sem("lo_pool")
        x1_stored, x1_back = sem("x1_stored"), sem("x1_back")
        a_drained, b_drained = sem("a_drained"), sem("b_drained")
        tx_full, tx_hi, tx_lo, th_full, th_hi, th_lo = (sem(n) for n in ("tx_full", "tx_hi", "tx_lo", "th_full", "th_hi", "th_lo"))
        y_drained = sem("y_drained")
        cur_done, xg_full, sc_done, cur_g = sem("cur_done"), sem("xg_full"), sem("sc_done"), sem("cur_g")
        f_ss, f_ms, f_rs, f_scaled, d_out = (sem(n) for n in ("f_ss", "f_ms", "f_rs", "f_scaled", "d_out"))
        f_out = [sem("f_out_pool"), sem("f_out_dve")]
        d_fins = [sem(f"d_fin{t}") for t in range(NT)]

        def lo_done(e, u):
            before = sum(v in BY_POOL for v in range(u))
            if u in BY_POOL:
                return lo_pool, e * len(BY_POOL) + (before + 1)
            return lo_dve, e * (UNITS - len(BY_POOL)) + (u - before + 1)

        def x_at(h, l):
            return 8 * h + l + 1

        def wcol(b):
            def cut(a, c0, n=HALF):
                return a[:, c0:c0 + n].rearrange("(k p) n -> p k n", p=P)
            k = b[0]
            if k == "ada_cols":
                return ada_w[0, :, b[1] * HALF:(b[1] + 1) * HALF].rearrange("(p k) n -> p k n", k=NK)
            return cut(w_in[0], COL[{"v": "i", "ga": "ga", "zb": "zb", "u": "u", "vv": "v"}[k]])

        def merge_unit(i):
            b, j = MERGE[i // 3]
            if i % 3 < 2:
                c0, r0 = COL["gate"] + b * D + j * P, i % 3 * HALF
                src = w_in[0, r0:r0 + HALF, c0:c0 + P]
            else:
                src = w_branch[0, b, :, j * P:(j + 1) * P]
            return src.rearrange("(k p) n -> p k n", p=P)

        def unit_used(i):
            if i % 3 == 0:
                return m_used, i // 3 + 1
            return G.filled((("gate", "branch")[i % 3 - 1], i // 3, 1))

        block = stack.enter_context(nc.Block())

        @block.sync
        def _(sp):
            sp.dma_start(small[0:8, :], norm_w[0, 0, :].rearrange("(r n) -> r n", r=8)).then_inc(d_small, 16)
            sp.dma_start(small[8:12, :], sgu_b[0]).then_inc(d_small, 16)
            sp.dma_start(small[12:20, :], hgrn_lb_raw.rearrange("a d (h n) -> (a d h) n", h=H)).then_inc(d_small, 16)
            sp.dma_start(craw[:, 0, :], c[0].rearrange("(p k) -> p k", k=NK)).then_inc(d_mod, 16)
            sp.dma_start(craw[:, 1, :], c_ctx.rearrange("(p k) -> p k", k=NK)).then_inc(d_mod, 16)
            sp.dma_start(adab[:, :], ada_b[0:1, 0:2048].to_broadcast([2, 2048])).then_inc(d_mod, 16)
            n_block = [0]

            def load_block():
                i = n_block[0]
                b = BLOCKS[i]
                n_block[0] += 1
                if before[b]:
                    sp.wait_ge(*G.filled(block_jobs[before[b]]))
                w = wslot[SLOT[b]]
                if b[0] == "z":
                    for j, name in enumerate(("q", "ff", "fb")):
                        c0 = COL[name] + b[1] * HD
                        sp.dma_start(w[:, :, j * HD:(j + 1) * HD],
                                     w_in[0, :, c0:c0 + HD].rearrange("(k p) n -> p k n", p=P)).then_inc(w_full[SLOT[b]], 16)
                else:
                    sp.dma_start(w, wcol(b)).then_inc(w_full[SLOT[b]], 16)

            for _ in range(SLOTS):
                load_block()
            for t in range(NTC):
                sp.dma_start(xbuf[0][:, t, :], ctx_in[0, t * P:(t + 1) * P, :]).then_inc(d_x[0], 16)
            for g in (1, 2):
                for t in range(4):
                    i = 4 * (g - 1) + t
                    sp.dma_start(xbuf[g][:, t, :], x[0, i * P:(i + 1) * P, :]).then_inc(d_x[g], 16)
            load_block()
            load_block()
            sp.dma_start(mask_raw, masks_in).then_inc(d_mask, 16)
            sp.dma_start(gnorm[:], hgrn_gnorm_w[0:1, :].to_broadcast([P, HD])).then_inc(d_row, 16)
            sp.wait_ge(zero_ready, 1)
            for t in range(NT):
                sp.dma_start(moe_dram[t * P:(t + 1) * P, :], zero).then_inc(d_zero, 16)
            while n_block[0] < BLOCKS.index(("zb",)) + 1:
                load_block()
            sp.wait_ge(*S2.filled(("ctx_turn", H - 1)))
            sp.wait_ge(*G.filled(("z", H - 1, "q", 1)))
            sp.dma_start(snorm, sgu_norm_w.rearrange("a g n -> a (g n)").to_broadcast([P, 4 * P])).then_inc(d_late, 16)
            sp.dma_start(cdft, channel_dft).then_inc(d_late, 16)
            sp.dma_start(tdft, token_dft.rearrange("(t p) n -> p t n", p=P)).then_inc(d_tab, 16)
            while n_block[0] < len(BLOCKS):
                load_block()
            sp.wait_ge(o_ready, 4)
            sp.wait_ge(*S2.filled(("o_turn", H - 1, 1)))
            sp.dma_start(wsraw, sgu_w[0].rearrange("g p q -> p g q")).then_inc(d_ws, 16)
            sp.wait_ge(*G.filled(("mix", 3, 1)))
            for i in range(MERGE_UNITS):
                if i >= RING:
                    sp.wait_ge(m_lo_done, i - RING + 1)
                sp.dma_start(raw_m[i % RING], merge_unit(i)).then_inc(m_full[i % RING], 16)
                if i % 3 or i // 3 - 1 not in ADA_AT:
                    continue
                part = ADA_AT[i // 3 - 1]
                if part:
                    sp.wait_ge(ada_added, part)
                else:
                    sp.wait_ge(ob_done, 8)
                n, kh = part // 2, part % 2
                c0 = 2048 + n * HALF
                src = ada_w[0, :, c0:c0 + HALF].rearrange("(p k) n -> p k n", k=NK)
                sp.dma_start(ada_part, src[:, 4 * kh:4 * kh + 4, :]).then_inc(d_ada, 16)
                if kh:
                    if n:
                        sp.wait_ge(rows_done, n)
                    nw, r0 = (1, 1, 2, 3)[n // 2], n % 2 * HALF
                    sp.dma_start(ada_bias, ada_b[0:1, c0:c0 + HALF].to_broadcast([P, HALF])).then_inc(d_rows, 16)
                    sp.dma_start(norm_row, norm_w[0, nw:nw + 1, r0:r0 + HALF].to_broadcast([P, HALF])).then_inc(d_rows, 16)
            for u in range(4):
                if u == 0:
                    sp.wait_ge(*G.filled(("branch", 2 * NK - 1, 1)))
                elif u == 2:
                    sp.wait_ge(ada_added, 16)
                elif u == 3:
                    sp.wait_ge(*G.filled(("branch", len(MERGE) - 1, 1)))
                n, kh = u // 2, u % 2
                sp.dma_start(out_raw[u], w_out[0, kh * HALF:(kh + 1) * HALF, n * HALF:(n + 1) * HALF].rearrange(
                    "(k p) n -> p k n", p=P)).then_inc(d_out_w[u], 16)
            sp.wait_ge(*G.filled(("ada_rows", 7)))
            sp.dma_start(rw, router_w[0].rearrange("(k p) e -> p k e", p=P)).then_inc(d_row, 16)
            for t in range(NT):
                if t >= 2:
                    sp.wait_ge(x1_done, t - 1)
                sp.dma_start(xre[t % 2], x[0, t * P:(t + 1) * P, :]).then_inc(d_xre[t % 2], 16)
                if t >= 1:
                    sp.wait_ge(h2_done, t)
                    sp.dma_start(x1_dram[(t - 1) * P:t * P, :], x1[:, t - 1, :]).then_inc(x1_stored, 16)
                    sp.dma_start(h2_dram[(t - 1) * P:t * P, :], ybuf[(t - 1) % 2]).then_inc(d_h2[(t - 1) % 2], 16)
            sp.wait_ge(h2_done, NT)
            sp.dma_start(x1_dram[(NT - 1) * P:NT * P, :], x1[:, NT - 1, :]).then_inc(x1_stored, 16)
            sp.dma_start(h2_dram[(NT - 1) * P:NT * P, :], ybuf[(NT - 1) % 2]).then_inc(d_h2[(NT - 1) % 2], 16)

            def expert_unit(e, u):
                if u < 8:
                    c0 = (u // 2 % 2) * D + (u // 4) * HALF
                    src, k0 = exp_w13[0, e, :, c0:c0 + HALF], u % 2 * 4
                else:
                    c0 = u % 2 * HALF
                    src, k0 = exp_w2[0, e, :, c0:c0 + HALF], (u - 8) // 2 * 4
                sp.dma_start(raw[u % RAW], src[k0 * P:(k0 + 4) * P, :].rearrange("(k p) n -> p k n", p=P)).then_inc(raw_full[u % RAW], 16)

            sp.wait_ge(*G.filled(("y", NT - 1, 1)))
            for u in range(UNITS):
                if u >= RAW:
                    sp.wait_ge(*lo_done(0, u - RAW))
                expert_unit(0, u)
            with sp.Fori(0, NE - 1) as e:
                for u in range(UNITS):
                    sp.wait_ge(*(lo_done(e, u + UNITS - RAW) if u < RAW else lo_done(e + 1, u - RAW)))
                    expert_unit(e + 1, u)
            for u in range(UNITS - RAW, UNITS):
                sp.wait_ge(*lo_done(NE - 1, u))
            sp.wait_ge(x1_stored, 16 * NT)
            sp.dma_start(x1_again, x1_dram.rearrange("(t p) n -> p t n", p=P)).then_inc(x1_back, 16)
            sp.wait_ge(sc_done, 16 * NE)
            for t in range(NT):
                sp.dma_start(fin[t], moe_dram[t * P:(t + 1) * P, :]).then_inc(d_fins[t], 16)
            for t in range(NT):
                sp.wait_ge(f_out[t % 2], t // 2 + 1)
                sp.dma_start(out[0, t * P:(t + 1) * P, :], fin[t]).then_inc(d_out, 16)
            sp.wait_ge(d_out, 16 * NT)
            sp.wait_ge(d_zero, 16 * NT)
            for j in range(2):
                sp.wait_ge(d_h2[j], 8 * NT)

        @block.tensor
        def _(pe):
            def claim(stream, key):
                if stream.reuses(key):
                    pe.wait_ge(*stream.last_drained(key))
                return stream.bank(key)

            def weights(b):
                pe.wait_ge(w_full[SLOT[b]], w_count[b])
                return wslot[SLOT[b]]

            def turn(dst, src, n=P):
                return nc.tensor.transpose(dst, src, ident[0:n, 0:n])

            def tokens_by_cols(bank, w, lhs, t, nk=NK):
                for k in range(nk):
                    mm = nc.tensor.matmul(bank[:], lhs[:, k, t * P:(t + 1) * P], w[:, k, :],
                                          start=(k == 0), stop=(k == nk - 1))
                return mm

            pe.wait_ge(ident_ready, 2)
            for st in STEPS:
                kind = st[0]
                if kind == "small":
                    bank = claim(G, st)
                    pe.wait_ge(d_small, 48)
                    turn(bank[:, 0:20], small[:], 20).then_inc(G.full, 1)
                elif kind == "ada_cols":
                    w = weights(st)
                    bank = claim(G, st)
                    pe.wait_ge(csilu_ready, 2)
                    for k in range(NK):
                        mm = nc.tensor.matmul(bank[0:2, :], csilu[:, :, k], w[:, k, :], start=(k == 0), stop=(k == NK - 1))
                    mm.then_inc(G.full, 1)
                elif kind == "ada_turn":
                    bank = claim(G, st)
                    pe.wait_ge(*G.drained(("ada_cols", 3)))
                    for m in range(16):
                        mm = turn(bank[:, 2 * m:2 * m + 2], adar[:, m * P:(m + 1) * P], 2)
                    mm.then_inc(G.full, 1)
                elif kind == "norm_x":
                    g = st[1]
                    nt = NTC if g == 0 else 4
                    pe.wait_ge(x_normed, g + 1)
                    for k in range(NK):
                        bank = claim(G, st + (k,))
                        for t in range(nt):
                            mm = turn(bank[:, t * P:(t + 1) * P], xbuf[g][:, t, k * P:(k + 1) * P])
                        mm.then_inc(G.full, 1)
                elif kind == "v":
                    w = weights(("v",))
                    bank = claim(G, st)
                    if st[1] == 0:
                        pe.wait_ge(*G.drained(("norm_x", 2, NK - 1)))
                        pe.wait_ge(*G.drained(("norm_x", 2, NK - 2)))
                    if st[1] < NTC:
                        tokens_by_cols(bank, w, hcT, st[1]).then_inc(G.full, 1)
                    else:
                        tokens_by_cols(bank, w, hT, st[1] - NTC).then_inc(G.full, 1)
                elif kind in ("ga", "zb", "u", "vv"):
                    w = weights((kind,))
                    bank = claim(G, st)
                    tokens_by_cols(bank, w, hT, st[1]).then_inc(G.full, 1)
                elif kind == "z":
                    _, h, name, j = st
                    w = weights(("z", h))
                    bank = claim(G, st)
                    c0 = ("q", "ff", "fb").index(name) * HD
                    for k in range(NK):
                        rhs = hT[:, k, j * HALF:(j + 1) * HALF] if j < 2 else hcT[:, k, :]
                        o = bank[:] if j < 2 else bank[:, 0:TC]
                        mm = nc.tensor.matmul(o, w[:, k, c0:c0 + HD], rhs, start=(k == 0), stop=(k == NK - 1))
                    mm.then_inc(G.full, 1)
                elif kind == "level":
                    _, h, l = st
                    B = hb[h % 2]
                    pe.wait_ge(x_ready, x_at(h, max(l - 1, 0)))
                    for j in range(2):
                        bank = claim(L, st + (j,))
                        for cc in range(4):
                            ch = 4 * j + cc
                            if l == 0:
                                mm = nc.tensor.matmul(bank[:, cc * P:(cc + 1) * P], U[:, ch * P:(ch + 1) * P],
                                                      B["A"][:, ch, :], start=True, stop=True)
                                continue
                            m = 1 << (l - 1)
                            o = bank[:, cc * P:(cc + 1) * P].rearrange("p (b two m) -> p b two m", two=2, m=m)
                            qf = B["X1"][:, ch, 0, :].rearrange("p (b two m) -> p b two m", two=2, m=m)
                            qb = B["X2"][:, ch, 1, :].rearrange("p (b two m) -> p b two m", two=2, m=m)
                            nc.tensor.matmul(o[:, :, 1, :], B["X2"][:, ch, 0, :], qf[:, :, 1, :], start=True, stop=True)
                            mm = nc.tensor.matmul(o[:, :, 0, :], B["X1"][:, ch, 1, :], qb[:, :, 0, :], start=True, stop=True)
                        mm.then_inc(L.full, 1)
                elif kind == "ctx_turn":
                    bank = claim(S2, st)
                    pe.wait_ge(ctx_done, st[1] + 1)
                    for a in range(2):
                        for t in range(NTC):
                            mm = turn(bank[:, (2 * a + t) * P:(2 * a + t + 1) * P], Kc[:, a, t * P:(t + 1) * P])
                    mm.then_inc(S2.full, 1)
                elif kind == "ctx_state":
                    h = st[1]
                    bank = claim(S2, st)
                    pe.wait_ge(*S2.drained(("ctx_turn", h)))
                    for a in range(2):
                        for t in range(NTC):
                            mm = nc.tensor.matmul(bank[:, a * P:(a + 1) * P], KcT[:, 2 * a + t, :],
                                                  Vc[:, t, h * HD:(h + 1) * HD], start=(t == 0), stop=(t == NTC - 1))
                    mm.then_inc(S2.full, 1)
                elif kind == "k_turn":
                    h = st[1]
                    B = hb[h % 2]
                    pe.wait_ge(x_ready, x_at(h, LEVELS))
                    for j in range(4):
                        bank = claim(S2, st + (j,))
                        src = B["X2"] if j < 2 else B["X1"]
                        for cc in range(4):
                            mm = turn(bank[:, cc * P:(cc + 1) * P], src[:, 4 * (j % 2) + cc, j // 2, :])
                        mm.then_inc(S2.full, 1)
                elif kind == "kv":
                    h = st[1]
                    for j in range(4):
                        bank = claim(S2, st + (j,))
                        if j == 0:
                            pe.wait_ge(*S2.drained(("k_turn", h, 3)))
                        a = j % 2
                        for i in range(4 if j < 2 else 3):
                            ch = 4 * (j // 2) + i if a == 0 else 7 - 4 * (j // 2) - i
                            mm = nc.tensor.matmul(bank[:, i * P:(i + 1) * P], KT[:, a, ch, :],
                                                  V[:, ch, h * HD:(h + 1) * HD], start=True, stop=True)
                        mm.then_inc(S2.full, 1)
                elif kind == "out":
                    h = st[1]
                    B = hb[h % 2]
                    pe.wait_ge(s_ready, h + 1)
                    for j in range(2):
                        bank = claim(S2, st + (j,))
                        for cc in range(4):
                            ch = 4 * j + cc
                            o = bank[:, cc * P:(cc + 1) * P]
                            nc.tensor.matmul(o, B["A"][:, ch, :], V[:, ch, h * HD:(h + 1) * HD], start=True, stop=False)
                            nc.tensor.matmul(o, B["X1"][:, ch, 0, :], S[:, 0, ch, :], start=False, stop=False)
                            mm = nc.tensor.matmul(o, B["X2"][:, ch, 1, :], S[:, 1, ch, :], start=False, stop=True)
                        mm.then_inc(S2.full, 1)
                elif kind == "o_turn":
                    h = st[1]
                    pe.wait_ge(o_ready, h + 1)
                    for j in range(2):
                        bank = claim(S2, st + (j,))
                        for cc in range(4):
                            mm = turn(bank[:, cc * P:(cc + 1) * P], o_sb[:, 4 * j + cc, :])
                        mm.then_inc(S2.full, 1)
                elif kind == "dft":
                    _, g, par = st
                    bank = claim(G, st)
                    if (g, par) == (0, 0):
                        pe.wait_ge(fold_done, 2)
                        pe.wait_ge(d_tab, 16)
                    for t in range(4):
                        mm = nc.tensor.matmul(bank[:], zfold[par][:, t, g * P:(g + 1) * P],
                                              tdft[:, t, par * HALF:(par + 1) * HALF], start=(t == 0), stop=(t == 3))
                    mm.then_inc(G.full, 1)
                elif kind == "dft2":
                    _, g, par = st
                    bank = claim(G, st)
                    pe.wait_ge(*G.drained(("dft", g, par)))
                    n = 257 - par
                    pe.wait_ge(d_late, 32)
                    nc.tensor.matmul(bank[:, 0:n], cdft[:, 0:HD], AB[:, g, par, 0:n], start=True, stop=True)
                    nc.tensor.matmul(bank[:, n:HALF], cdft[:, HD:], AB[:, g, par, n:HALF], start=True,
                                     stop=True).then_inc(G.full, 1)
                elif kind == "mix":
                    _, g, j = st
                    if (g, j) == (0, 0):
                        pe.wait_ge(d_ws, 16)
                        pe.wait_ge(L.sems["dve"], L.count["dve"])
                        for gg in range(4):
                            mm = turn(banks[4][:, gg * P:(gg + 1) * P], wsraw[:, gg, :])
                        mm.then_inc(ws_t, 1)
                        pe.wait_ge(vv_done, 1)
                        pe.wait_ge(ws_t, 2)
                    bank = claim(G, st)
                    nc.tensor.matmul(bank[:].rearrange("p (t n) -> p t n", t=4), wsT[:, g, :],
                                     vg[:, 4 * j:4 * j + 4, g * P:(g + 1) * P], start=True, stop=True).then_inc(G.full, 1)
                elif kind == "oc_turn":
                    _, g, j = st
                    bank = claim(G, st)
                    pe.wait_ge(*G.drained(("mix", 3, 1)))
                    for t in range(4):
                        mm = turn(bank[:, t * P:(t + 1) * P], ug[:, 4 * j + t, g * P:(g + 1) * P])
                    mm.then_inc(G.full, 1)
                elif kind == "merge":
                    q = st[1]
                    b = MERGE[q][0]
                    for part in range(3):
                        i = 3 * q + part
                        if i == 0:
                            pe.wait_ge(h_lo_done, NK)
                        if part == 2 and MERGE[q][1] == 0:
                            pe.wait_ge(o_lo_done, 4 * (q // NK + 1))
                        pe.wait_ge(m_lo_done, i + 1)
                        for j in range(2):
                            key = ("branch" if part == 2 else "gate", q, j)
                            bank = G.bank(key) if part == 1 else claim(G, key)
                            xh, xl = (h_hi, h_lo) if part < 2 else (o_hi, o_lo[b])
                            for k in range(4):
                                kx = 4 * part + k if part < 2 else k
                                first, last = part != 1 and k == 0, part and k == 3
                                cut = slice(j * HALF, (j + 1) * HALF)
                                wh, wl = wm_hi[i % RING][:, k, :], wm_lo[i % RING][:, k, :]
                                nc.tensor.matmul(bank[:], wh, xh[:, kx, cut], start=first, stop=False)
                                nc.tensor.matmul(bank[:], wh, xl[:, kx, cut], start=False, stop=False)
                                mm = nc.tensor.matmul(bank[:], wl, xh[:, kx, cut], start=False, stop=bool(last))
                            if part:
                                mm.then_inc(G.full, 1)
                            elif j:
                                mm.then_inc(m_used, 1)
                elif kind == "ada_rows":
                    n = st[1]
                    bank = claim(G, st)
                    pe.wait_ge(ones_ready, 1)
                    pe.wait_ge(ada_summed, n + 1)
                    nc.tensor.matmul(bank[:], ones[:], rows[:, n // 2, n % 2 * HALF:(n % 2 + 1) * HALF],
                                     start=True, stop=True).then_inc(G.full, 1)
                elif kind == "y":
                    t = st[1]
                    pe.wait_ge(mt_lo_done, t + 1)
                    for n in range(2):
                        bank = claim(G, st + (n,))
                        for k in range(NK):
                            if t == 0 and k % 4 == 0:
                                pe.wait_ge(out_lo_done, 2 * n + k // 4 + 1)
                            hi, lo = mt_hi[:, t % 2, k, :], mt_lo[:, t % 2, k, :]
                            nc.tensor.matmul(bank[:], hi, out_hi[:, n, k, :], start=(k == 0), stop=False)
                            nc.tensor.matmul(bank[:], hi, out_lo[:, n, k, :], start=False, stop=False)
                            mm = nc.tensor.matmul(bank[:], lo, out_hi[:, n, k, :], start=False, stop=(k == NK - 1))
                        mm.then_inc(G.full, 1)
                elif kind == "h2_turn":
                    t = st[1]
                    pe.wait_ge(h2_done, t + 1)
                    for j in range(2):
                        bank = claim(G, st + (j,))
                        for k in range(4):
                            mm = turn(bank[:, k * P:(k + 1) * P], ybuf[t % 2][:, (4 * j + k) * P:(4 * j + k + 1) * P])
                        mm.then_inc(G.full, 1)
                elif kind == "router":
                    bank = claim(G, st + (0,))
                    for j in range(2):
                        pe.wait_ge(*G.drained(("h2_turn", NT - 1, j)))
                    pe.wait_ge(d_row, 32)
                    for t in range(NT):
                        for k in range(NK):
                            mm = nc.tensor.matmul(bank[:, t * NE:(t + 1) * NE], h2T[:, k, t * P:(t + 1) * P], rw[:, k, :],
                                                  start=(k == 0), stop=(k == NK - 1))
                    mm.then_inc(G.full, 1)
                elif kind == "router_turn":
                    pe.wait_ge(r_prob, 1)
                    for j in range(2):
                        bank = claim(G, st + (j,))
                        for t in range(4):
                            mm = turn(bank[0:NE, t * P:(t + 1) * P], prob[:, 4 * j + t, :])
                        mm.then_inc(G.full, 1)
                elif kind == "choose_turn":
                    pe.wait_ge(chosen, 1)
                    for j, src in enumerate((topv, topf)):
                        bank = claim(G, st + (j,))
                        turn(bank[:, 0:NE], src, NE).then_inc(G.full, 1)

            pe.wait_ge(*S2.drained(("o_turn", H - 1, 1)))

            def turn_gathered(n, j):
                if j == 0:
                    pe.wait_ge(xg_full, n * 16 + 16)
                else:
                    pe.wait_ge(tx_hi, n * 2 + 1)
                    pe.wait_ge(tx_lo, n * 2 + 1)
                for k in range(4):
                    mm = turn(banks[4][:, k * P:(k + 1) * P], xg[:, (4 * j + k) * P:(4 * j + k + 1) * P])
                mm.then_inc(tx_full, 1)

            def turn_hidden(e, j):
                pe.wait_ge(b_drained, e * 2 + (j + 1))
                if j:
                    pe.wait_ge(th_hi, e * 2 + 1)
                    pe.wait_ge(th_lo, e * 2 + 1)
                for k in range(4):
                    mm = turn(banks[6][:, k * P:(k + 1) * P], hid[:, (4 * j + k) * P:(4 * j + k + 1) * P])
                mm.then_inc(th_full, 1)

            def unit(e, u):
                if u < 8:
                    bank, k0, stop_at, hi, lo = banks[u // 2], u % 2 * 4, 1, xe_hi, xe_lo
                    if u < 2:
                        pe.wait_ge(tx_hi, e * 2 + (u + 1))
                        pe.wait_ge(tx_lo, e * 2 + (u + 1))
                else:
                    bank, k0, hi, lo = banks[7 if u % 2 == 0 else 5], (u - 8) // 2 * 4, ht_hi, ht_lo
                    if u in (8, 10):
                        pe.wait_ge(th_hi, e * 2 + (u // 2 - 3))
                        pe.wait_ge(th_lo, e * 2 + (u // 2 - 3))
                    if u in (8, 9):
                        pe.wait_ge(y_drained, e * 2 + 2)
                pe.wait_ge(*lo_done(e, u))
                for k in range(4):
                    first, last = k0 == 0 and k == 0, k0 == 4 and k == 3
                    nc.tensor.matmul(bank[:], hi[:, k0 + k, :], whi[u % PAIRS][:, k, :], start=first, stop=False)
                    nc.tensor.matmul(bank[:], hi[:, k0 + k, :], wlo[u % PAIRS][:, k, :], start=False, stop=False)
                    mm = nc.tensor.matmul(bank[:], lo[:, k0 + k, :], whi[u % PAIRS][:, k, :], start=False, stop=last)
                mm.then_inc(used, 1)

            def expert(e, last):
                for u in range(6):
                    unit(e, u)
                turn_hidden(e, 0)
                for u in (6, 7, 8):
                    unit(e, u)
                if not last:
                    turn_gathered(e + 1, 0)
                turn_hidden(e, 1)
                unit(e, 9)
                if not last:
                    turn_gathered(e + 1, 1)
                unit(e, 10)
                unit(e, 11)

            turn_gathered(0, 0)
            turn_gathered(0, 1)
            with pe.Fori(0, NE - 1) as e:
                expert(e, False)
            expert(NE - 1, True)

        @block.scalar
        def _(act):
            def take(stream, key):
                act.wait_ge(*stream.filled(key))
                return stream.bank(key)

            def split_unit(i):
                if i < MERGE_UNITS:
                    act.wait_ge(m_full[i % RING], 16 * (i // RING + 1))
                    if i >= RING:
                        act.wait_ge(*unit_used(i - RING))
                    nc.scalar.copy(wm_hi[i % RING], raw_m[i % RING]).then_inc(m_hi_done, 1)

            act.wait_ge(d_mod, 48)
            for j in range(2):
                nc.scalar.activation(csilu[:, j, :], craw[:, j, :], ACT.Silu).then_inc(csilu_ready, 1)
            for st in STEPS:
                kind = st[0]
                if kind == "small":
                    act.wait_ge(lb_max, 1)
                    nc.scalar.activation(lb[:, 1, :], lb[:, 0, :], ACT.Exp).then_inc(lb_ready, 1)
                elif kind == "norm_s":
                    g = st[1]
                    nt = NTC if g == 0 else 4
                    act.wait_ge(d_x[g], 16 * nt)
                    for t in range(nt):
                        nc.scalar.activation(o_sb[:].rearrange("p a b -> p (a b)"), xbuf[g][:, t, :], ACT.Square,
                                             scale=1.0 / math.sqrt(D), accum_out=ss[:, 4 * g + t:4 * g + t + 1]).then_inc(x_ss, 1)
                        act.wait_ge(x_ss, (0, 2, 6)[g] + t + 1)
                elif kind == "norm_x":
                    g = st[1]
                    act.wait_ge(*G.drained(("ada_turn",)))
                    for k in range(1, NK, 2):
                        bank = take(G, st + (k,))
                        dst = hcT[:, k, :] if g == 0 else hT[:, k, (g - 1) * HALF:g * HALF]
                        w = TC if g == 0 else HALF
                        j = 1 if g == 0 else 0
                        nc.scalar.activation(dst, bank[:, 0:w], ACT.Identity, bias=shift1[:, k, j:j + 1],
                                             scale=scale1[:, k, j:j + 1]).then_inc(G.freed(st + (k,)), 1)
                elif kind == "v":
                    bank = take(G, st)
                    dst = Vc[:, st[1], :] if st[1] < NTC else V[:, st[1] - NTC, :]
                    nc.scalar.copy(dst, bank[:]).then_inc(G.freed(st), 1)
                elif kind == "ga":
                    bank = take(G, st)
                    nc.scalar.activation(Gt[:, st[1], :], bank[:], ACT.Silu).then_inc(G.freed(st), 1)
                elif kind == "z":
                    _, h, name, j = st
                    B = hb[h % 2]
                    bank = take(G, st)
                    src = bank[:].rearrange("p (c t) -> p c t", c=4)
                    if name == "q":
                        nc.scalar.activation(B["A"][:, 4 * j:4 * j + 4, :], src, ACT.Silu).then_inc(G.freed(st), 1)
                        continue
                    a = 0 if name == "ff" else 1
                    if j < 2:
                        f = B["F"].rearrange("p (c a t) -> p c a t", c=NT, a=2)[:, 4 * j:4 * j + 4, a, :]
                        kk = (B["X2"], B["X1"])[a][:, 4 * j:4 * j + 4, a, :]
                    else:
                        src, f, kk = bank[:, 0:TC], Fc[:, 0, a, :], Kc[:, a, :]
                        if h:
                            act.wait_ge(*S2.filled(("ctx_turn", h - 1)))
                    nc.scalar.activation(f, src, ACT.Sigmoid)
                    nc.scalar.activation(kk, src, ACT.Sigmoid, scale=-1.0).then_inc(G.freed(st), 1)
                elif kind == "level" and st[2] == 0:
                    for j in range(2):
                        bank = take(L, st + (j,))
                        nc.scalar.copy(hb[st[1] % 2]["A"][:, 4 * j:4 * j + 4, :],
                                       bank[:].rearrange("p (c t) -> p c t", c=4)).then_inc(L.freed(st + (j,)), 1)
                elif kind == "ctx_turn":
                    bank = take(S2, st)
                    nc.scalar.copy(KcT, bank[:].rearrange("p (c t) -> p c t", c=4)).then_inc(S2.freed(st), 1)
                elif kind == "ctx_state":
                    h = st[1]
                    bank = take(S2, st)
                    nc.scalar.copy(S[:, 0, 0, :], bank[:, 0:P])
                    nc.scalar.copy(S[:, 1, NT - 1, :], bank[:, P:2 * P]).then_inc(S2.freed(st), 1)
                elif kind == "k_turn":
                    if st[1] == 0:
                        act.wait_ge(d_zero, 16 * NT)
                    for j in range(4):
                        bank = take(S2, st + (j,))
                        nc.scalar.copy(KT[:, j // 2, 4 * (j % 2):4 * (j % 2) + 4, :],
                                       bank[:].rearrange("p (c t) -> p c t", c=4)).then_inc(S2.freed(st + (j,)), 1)
                elif kind == "out":
                    h = st[1]
                    for j in range(2):
                        bank = take(S2, st + (j,))
                        src = bank[:].rearrange("p (c t) -> p c t", c=4)
                        if j == 0 and h:
                            act.wait_ge(*S2.filled(("o_turn", h - 1, 1)))
                        nc.scalar.copy(o_sb[:, 4 * j:4 * j + 4, :], src)
                        nc.scalar.activation(o_sq[:, 4 * j:4 * j + 4, :], src, ACT.Square,
                                             scale=1.0 / math.sqrt(HD)).then_inc(S2.freed(st + (j,)), 1)
                elif kind == "o_turn":
                    h = st[1]
                    for j in range(2):
                        bank = take(S2, st + (j,))
                        nc.scalar.copy(oaT[:, h, j * HALF:(j + 1) * HALF], bank[:]).then_inc(S2.freed(st + (j,)), 1)
                elif kind == "zb":
                    bank = take(G, st)
                    nc.scalar.copy(zb[:, st[1], :], bank[:]).then_inc(G.freed(st), 1)
                elif kind in ("u", "vv"):
                    bank = take(G, st)
                    if st == ("u", 0):
                        act.wait_ge(o_gated, H)
                    nc.scalar.activation((ug if kind == "u" else vg)[:, st[1], :], bank[:], ACT.Gelu).then_inc(G.freed(st), 1)
                elif kind == "vv_norm":
                    act.wait_ge(*G.drained(("vv", NT - 1)))
                    for j in range(4):
                        if j >= 2:
                            act.wait_ge(v_sq, j - 1)
                        sq = big[:, 1024 * (j % 2):1024 * (j % 2 + 1)].rearrange("p (t n) -> p t n", t=2)
                        nc.scalar.activation(sq, vg[:, 2 * j:2 * j + 2, :], ACT.Square,
                                             scale=1.0 / math.sqrt(P)).then_inc(vv_sq_ready, 1)
                elif kind == "dft":
                    _, g, par = st
                    bank = take(G, st)
                    nc.scalar.copy(AB[:, g, par, :], bank[:]).then_inc(G.freed(st), 1)
                elif kind == "dft2":
                    _, g, par = st
                    n = 2 * g + par
                    bank = take(G, st)
                    if n >= 2:
                        act.wait_ge(ob_done, n - 1)
                    nc.scalar.copy(pq[n % 2], bank[:]).then_inc(G.freed(st), 1)
                elif kind == "mix" and st[1:] == (0, 0):
                    act.wait_ge(ws_t, 1)
                    nc.scalar.copy(wsT, banks[4][:].rearrange("p (c t) -> p c t", c=4)).then_inc(ws_t, 1)
                elif kind == "oc_turn":
                    _, g, j = st
                    bank = take(G, st)
                    nc.scalar.copy(ocT[:, g, j * HALF:(j + 1) * HALF], bank[:]).then_inc(G.freed(st), 1)
                elif kind == "h_split":
                    k = st[1]
                    if k == 0:
                        act.wait_ge(*G.filled(("vv", NT - 1)))
                    nc.scalar.copy(h_hi[:, k, :], hT[:, k, :]).then_inc(h_hi_done, 1)
                elif kind == "o_split":
                    _, b, g = st
                    if b == 0 and g == 0:
                        act.wait_ge(v_sq, 4)
                        act.wait_ge(*S2.drained(("o_turn", H - 1, 1)))
                    elif g == 0:
                        act.wait_ge(*G.filled(("branch", (NK if b == 2 else 2 * NK) - 1, 1)))
                        if b == 1:
                            act.wait_ge(ob_done, 8)
                        else:
                            act.wait_ge(*G.drained(("oc_turn", 3, 1)))
                    nc.scalar.copy(o_hi[:, g, :], (oaT, obT, ocT)[b][:, g, :]).then_inc(o_hi_done, 1)
                elif kind == "merge":
                    q = st[1]
                    if q == 0:
                        act.wait_ge(*G.filled(("oc_turn", 3, 1)))
                        for i in range(4):
                            split_unit(i)
                    split_unit(3 * q + 4)
                    for j in range(2):
                        key = ("gate", q, j)
                        bank = take(G, key)
                        if q:
                            act.wait_ge(*G.drained(("branch", q - 1, j)))
                        nc.scalar.activation(sig[j], bank[:], ACT.Sigmoid).then_inc(G.freed(key), 1)
                    split_unit(3 * q + 5)
                    split_unit(3 * q + 6)
                elif kind == "out_split":
                    u = st[1]
                    act.wait_ge(d_out_w[u], 16)
                    if u == 0:
                        act.wait_ge(*G.filled(("gate", len(MERGE) - 1, 1)))
                    nc.scalar.copy(out_hi[:, u // 2, u % 2 * 4:u % 2 * 4 + 4, :], out_raw[u]).then_inc(out_hi_done, 1)
                elif kind == "m_split":
                    t = st[1]
                    if t == 0:
                        act.wait_ge(merged_done, 4 * NK)
                        act.wait_ge(*G.filled(("branch", len(MERGE) - 1, 1)))
                    elif t >= 2:
                        act.wait_ge(*G.filled(("y", t - 2, 1)))
                    nc.scalar.copy(mt_hi[:, t % 2], mT[:, :, t * P:(t + 1) * P]).then_inc(mt_hi_done, 1)
                elif kind == "y_norm":
                    t = st[1]
                    for n in range(2):
                        key = ("y", t, n)
                        bank = take(G, key)
                        if t >= 2 and n == 0:
                            act.wait_ge(d_h2[t % 2], 16 * (t // 2))
                            act.wait_ge(*G.filled(("h2_turn", t - 2, 1)))
                        nc.scalar.copy(ybuf[t % 2][:, n * HALF:(n + 1) * HALF], bank[:]).then_inc(G.freed(key), 1)
                    act.wait_ge(*G.drained(("y", t, 1)))
                    nc.scalar.activation(flat, ybuf[t % 2], ACT.Square, scale=1.0 / math.sqrt(D),
                                         accum_out=ss[:, t:t + 1]).then_inc(y_ss, 1)
                    act.wait_ge(x1_done, t + 1)
                    act.wait_ge(y_ss, t + 1)
                    nc.scalar.activation(flat, x1[:, t, :], ACT.Square, scale=1.0 / math.sqrt(D),
                                         accum_out=ss[:, 8 + t:9 + t]).then_inc(x1_ss, 1)
                    act.wait_ge(x1_ss, t + 1)
                elif kind == "h2_turn":
                    t = st[1]
                    bank = take(G, st + (1,))
                    nc.scalar.copy(h2T[:, 4:8, t * P:(t + 1) * P], bank[:].rearrange("p (k t) -> p k t", k=4)).then_inc(G.freed(st + (1,)), 1)
                elif kind == "router":
                    act.wait_ge(r_sub, 1)
                    nc.scalar.activation(prob, prob, ACT.Exp).then_inc(r_exp, 1)


            def split(e, u):
                act.wait_ge(raw_full[u % RAW], e * (16 * UNITS // RAW) + 16 * (u // RAW + 1))
                if not (isinstance(e, int) and e == 0 and u < PAIRS):
                    act.wait_ge(used, e * UNITS + (u - PAIRS + 1))
                nc.scalar.copy(whi[u % PAIRS], raw[u % RAW]).then_inc(hi_done, 1)

            def gathered(n, j):
                act.wait_ge(tx_full, n * 2 + (j + 1))
                nc.scalar.copy(xe_hi[:, 4 * j:4 * j + 4, :], banks[4][:].rearrange("p (k t) -> p k t", k=4)).then_inc(tx_hi, 1)

            def hidden(e, j):
                act.wait_ge(th_full, e * 2 + (j + 1))
                nc.scalar.copy(ht_hi[:, 4 * j:4 * j + 4, :], banks[6][:].rearrange("p (k t) -> p k t", k=4)).then_inc(th_hi, 1)

            def silu_a(e, j):
                act.wait_ge(used, e * UNITS + (4 * j + 2))
                nc.scalar.activation(sa[j], banks[2 * j][:], ACT.Silu).then_inc(a_drained, 1)

            def result(e, j):
                if j == 0:
                    act.wait_ge(cur_g, e + 1)
                    act.wait_ge(added, e + 1)
                act.wait_ge(used, e * UNITS + (11 + j))
                nc.scalar.activation(yb[:, j * HALF:(j + 1) * HALF], banks[7 - 2 * j][:], ACT.Identity,
                                     scale=gcur[:, 0:1]).then_inc(y_drained, 1)

            def expert(e, before):
                if before is not None:
                    split(e, 0)
                    split(e, 1)
                    gathered(e, 0)
                    hidden(before, 1)
                    split(e, 2)
                    gathered(e, 1)
                    split(e, 3)
                    split(e, 4)
                    result(before, 0)
                    split(e, 5)
                    result(before, 1)
                split(e, 6)
                silu_a(e, 0)
                for u in (7, 8, 9, 10):
                    split(e, u)
                silu_a(e, 1)
                hidden(e, 0)
                split(e, 11)

            act.wait_ge(x1_stored, 16 * NT)
            for u in range(PAIRS):
                split(0, u)
            act.wait_ge(G.sems["act"], G.count["act"])
            act.wait_ge(G.sems["dve"], G.count["dve"])
            act.sem_inc(y_drained, 2)
            gathered(0, 0)
            gathered(0, 1)
            expert(0, None)
            with act.Fori(0, NE - 1) as i:
                expert(i + 1, i)
            hidden(NE - 1, 1)
            result(NE - 1, 0)
            result(NE - 1, 1)
            for t in range(NT):
                act.wait_ge(d_fins[t], 16)
                nc.scalar.activation(o_sb[:].rearrange("p a b -> p (a b)"), fin[t], ACT.Square, scale=1.0 / math.sqrt(D),
                                     accum_out=ss[:, 16 + t:17 + t]).then_inc(f_ss, 1)
                act.wait_ge(f_ss, t + 1)

        @block.vector
        def _(dve):
            def take(stream, key):
                dve.wait_ge(*stream.filled(key))
                return stream.bank(key)

            n = [0]

            def step(ins):
                ins.then_inc(vstep, 1)
                n[0] += 1
                dve.wait_ge(vstep, n[0])

            def split_unit(i):
                if i < MERGE_UNITS:
                    dve.wait_ge(m_hi_done, i + 1)
                    nc.vector.tensor_tensor(wm_lo[i % RING], raw_m[i % RING], wm_hi[i % RING].bitcast(F32),
                                            ALU.subtract).then_inc(m_lo_done, 1)

            nc.vector.memset(zero, 0.0).then_inc(zero_ready, 1)
            for st in STEPS:
                kind = st[0]
                if kind == "small":
                    step(nc.vector.tensor_copy(cols[:], take(G, st)[:, 0:20]))
                    nc.vector.tensor_copy(lb[:, 3, :], cols[:, 12:20]).then_inc(G.freed(st), 1)
                    dve.wait_ge(G.sems["dve"], 1)
                    nc.vector.tensor_tensor(lb[:, 0, :], lb[:, 3, :], lb[:, 3, :], ALU.subtract).then_inc(lb_max, 1)
                    dve.wait_ge(lb_ready, 1)
                    step(nc.vector.reciprocal(lb[:, 2, :], lb[:, 1, :]))
                    step(nc.vector.tensor_tensor(lb[:, 2, :], lb[:, 2, :], lb[:, 1, :], ALU.mult))
                    step(nc.vector.tensor_tensor(lb[:, 0, :], lb[:, 2, :], lb[:, 2, :], ALU.subtract))
                    nc.vector.tensor_scalar(gate_add[:], lb[:, 0, :], FLOOR, None, ALU.max)
                    step(nc.vector.tensor_scalar(gate_mul[:], lb[:, 0, :], -1.0, 1.0, ALU.mult, ALU.add))
                elif kind == "ada_cols":
                    nn = st[1]
                    bank = take(G, st)
                    dve.wait_ge(d_mod, 48)
                    nc.vector.tensor_tensor(adar[:, nn * HALF:(nn + 1) * HALF], bank[0:2, :],
                                            adab[:, nn * HALF:(nn + 1) * HALF], ALU.add).then_inc(G.freed(st), 1)
                elif kind == "ada_turn":
                    bank = take(G, st)
                    nc.vector.tensor_copy(shift1[:], bank[:, 0:16].rearrange("p (k j) -> p k j", j=2))
                    nc.vector.scalar_tensor_tensor(scale1[:], bank[:, 16:32].rearrange("p (k j) -> p k j", j=2), 1.0,
                                                   cols[:, 0:8].rearrange("p (k o) -> p k o", o=1).to_broadcast([P, NK, 2]), ALU.add, ALU.mult).then_inc(G.freed(st), 1)
                    dve.wait_ge(*G.drained(st))
                elif kind == "norm_s":
                    g = st[1]
                    nt = NTC if g == 0 else 4
                    dve.wait_ge(x_ss, (2, 6, 10)[g])
                    nc.vector.tensor_scalar(ss[:, 16 + 4 * g:16 + 4 * g + nt], ss[:, 4 * g:4 * g + nt], EPS, None, ALU.add).then_inc(x_ms, 1)
                    dve.wait_ge(x_rs, g + 1)
                    for t in range(nt):
                        ins = nc.vector.tensor_scalar(xbuf[g][:, t, :], xbuf[g][:, t, :], rs[:, 4 * g + t:4 * g + t + 1], None, ALU.mult)
                    ins.then_inc(x_normed, 1)
                elif kind == "norm_x":
                    g = st[1]
                    for k in range(0, NK, 2):
                        bank = take(G, st + (k,))
                        dst = hcT[:, k, :] if g == 0 else hT[:, k, (g - 1) * HALF:g * HALF]
                        w = TC if g == 0 else HALF
                        j = 1 if g == 0 else 0
                        nc.vector.tensor_scalar(dst, bank[:, 0:w], scale1[:, k, j:j + 1], shift1[:, k, j:j + 1],
                                                ALU.mult, ALU.add).then_inc(G.freed(st + (k,)), 1)
                elif kind == "prepare":
                    _, h, part = st
                    B = hb[h % 2]
                    F4 = B["F"].rearrange("p (c a t) -> p c a t", c=NT, a=2)
                    if part < 2:
                        a = part
                        dve.wait_ge(*G.drained(("z", h, ("ff", "fb")[a], 2)))
                        mul, add = gate_mul[:, 4 * a + h:4 * a + h + 1], gate_add[:, 4 * a + h:4 * a + h + 1]
                        kk = (B["X2"], B["X1"])[a][:, :, a, :]
                        nc.vector.tensor_scalar(Fc[:, 0, a, :], Fc[:, 0, a, :], mul, add, ALU.mult, ALU.add)
                        nc.vector.tensor_scalar(Kc[:, a, :], Kc[:, a, :], mul, None, ALU.mult).then_inc(kc_ready, 1)
                        nc.vector.tensor_scalar(F4[:, :, a, :], F4[:, :, a, :], mul, add, ALU.mult, ALU.add)
                        step(nc.vector.tensor_scalar(kk, kk, mul, None, ALU.mult))
                        if a:
                            nc.vector.tensor_tensor(U.rearrange("p (c t) -> p c t", c=NT), B["X2"][:, :, 0, :],
                                                    B["X1"][:, :, 1, :], ALU.add)
                        continue
                    if h == 0:
                        dve.wait_ge(d_mask, 16)
                        step(nc.vector.tensor_copy(masks[:], mask_raw))
                    dve.wait_ge(*G.drained(("z", h, "q", 1)))
                    nc.vector.tensor_tensor(B["X1"][:, :, 0, :], B["A"], F4[:, :, 0, :], ALU.mult)
                    nc.vector.tensor_tensor(B["X2"][:, :, 1, :], B["A"], F4[:, :, 1, :], ALU.mult).then_inc(x_ready, 1)
                elif kind == "level" and st[2]:
                    _, h, l = st
                    B = hb[h % 2]
                    m = 1 << (l - 1)
                    if l == 1:
                        dve.wait_ge(L.freed(("level", h, 0, 1)), 2 * (h + 1))
                    else:
                        dve.wait_ge(x_ready, x_at(h, l - 1))
                    for j in range(2):
                        bank = take(L, st + (j,))
                        nc.vector.copy_predicated(B["A"][:, 4 * j:4 * j + 4, :], masks[:, l - 1:l, :].to_broadcast([P, 4, P]),
                                                  bank[:].rearrange("p (c t) -> p c t", c=4)).then_inc(L.freed(st + (j,)), 1)
                    nb = 2 * NT * P // (2 * m)
                    src, dst = (B["F"], U) if l % 2 else (U, B["F"])
                    if l == LEVELS:
                        dst = totals
                    pair = src[:, 0:2 * nb].rearrange("p (b two) -> p b two", two=2)
                    X1 = B["X1"].rearrange("p c a t -> p (c a t)").rearrange("p (b two m) -> p b two m", two=2, m=m)
                    X2 = B["X2"].rearrange("p c a t -> p (c a t)").rearrange("p (b two m) -> p b two m", two=2, m=m)
                    nc.vector.tensor_tensor(dst[:, 0:nb], pair[:, :, 0], pair[:, :, 1], ALU.mult)
                    nc.vector.tensor_tensor(X1[:, :, 1, :], X1[:, :, 1, :], pair[:, :, 0:1].to_broadcast([P, nb, m]), ALU.mult)
                    nc.vector.tensor_tensor(X2[:, :, 0, :], X2[:, :, 0, :], pair[:, :, 1:2].to_broadcast([P, nb, m]),
                                            ALU.mult).then_inc(x_ready, 1)
                elif kind == "kv":
                    h = st[1]
                    B = hb[h % 2]
                    tot = totals[:].rearrange("p (c a) -> p c a", a=2)
                    dve.wait_ge(x_ready, x_at(h, LEVELS))
                    dve.wait_ge(*S2.drained(("ctx_state", h)))
                    for half in range(2):
                        banks2 = [take(S2, st + (2 * half + a,)) for a in range(2)]
                        for i in range(4 - half):
                            for a in range(2):
                                ch = 4 * half + i if a == 0 else 7 - 4 * half - i
                                nx = ch + 1 if a == 0 else ch - 1
                                ins = nc.vector.scalar_tensor_tensor(S[:, a, nx, :], S[:, a, ch, :], tot[:, ch, a:a + 1],
                                                                     banks2[a][:, i * P:(i + 1) * P], ALU.mult, ALU.add)
                            step(ins)
                        for a in range(2):
                            dve.sem_inc(S2.freed(st + (2 * half + a,)), 1)
                    dve.sem_inc(s_ready, 1)
                elif kind == "out":
                    h = st[1]
                    dve.wait_ge(*S2.drained(("out", h, 1)))
                    step(nc.vector.tensor_reduce(ss[:, 32:40], o_sq, AX.X, ALU.add))
                    nc.vector.tensor_scalar(ss[:, 40:48], ss[:, 32:40], EPS, None, ALU.add).then_inc(o_ms, 1)
                    dve.wait_ge(o_rs, h + 1)
                    dve.wait_ge(o_gated, h + 1)
                    nc.vector.tensor_tensor(o_sb[:], o_sb[:], rs[:, 32:40].rearrange("p (c o) -> p c o", o=1).to_broadcast([P, NT, HD]),
                                            ALU.mult).then_inc(o_ready, 1)
                elif kind == "fold":
                    dve.wait_ge(*S2.filled(("out", H - 1, 1)))
                    dve.wait_ge(*G.drained(("zb", NT - 1)))
                    nc.vector.tensor_tensor(zfold[0], zb[:, 0:4, :], zb[:, 4:8, :], ALU.add).then_inc(fold_done, 1)
                    nc.vector.tensor_tensor(zfold[1], zb[:, 0:4, :], zb[:, 4:8, :], ALU.subtract).then_inc(fold_done, 1)
                elif kind == "vv_norm":
                    for j in range(4):
                        dve.wait_ge(vv_sq_ready, j + 1)
                        sq = big[:, 1024 * (j % 2):1024 * (j % 2 + 1)].rearrange("p (c t) -> p c t", t=P)
                        nc.vector.tensor_reduce(ss[:, 8 * j:8 * j + 8], sq, AX.X, ALU.add).then_inc(v_sq, 1)
                    dve.wait_ge(v_sq, 4)
                    nc.vector.tensor_scalar(ss[:, 0:32], ss[:, 0:32], EPS, None, ALU.add).then_inc(v_ms, 1)
                    dve.wait_ge(v_rs, 1)
                    v4 = vg.rearrange("p t (g n) -> p (t g) n", g=4)
                    step(nc.vector.tensor_tensor(v4, v4, rs[:, 0:32].rearrange("p (c o) -> p c o", o=1).to_broadcast([P, 32, P]), ALU.mult))
                    dve.wait_ge(d_late, 32)
                    nc.vector.tensor_tensor(vg, vg, snorm.rearrange("p (o n) -> p o n", o=1).to_broadcast([P, NT, 4 * P]), ALU.mult).then_inc(vv_done, 1)
                elif kind == "dft2":
                    _, g, par = st
                    i = 2 * g + par
                    dve.wait_ge(*G.drained(st))
                    b = pq[i % 2]
                    if par == 0:
                        nc.vector.tensor_tensor(obT[:, g, 2:HALF:2], b[:, 1:256], b[:, 257:512], ALU.subtract)
                        nc.vector.tensor_tensor(obT[:, g, T - 2:HALF:-2], b[:, 1:256], b[:, 257:512], ALU.add)
                        nc.vector.tensor_copy(obT[:, g, 0:HALF + 1:HALF], b[:, 0:257:256]).then_inc(ob_done, 1)
                    else:
                        nc.vector.tensor_tensor(obT[:, g, 1:HALF:2], b[:, 0:256], b[:, 256:512], ALU.subtract)
                        nc.vector.tensor_tensor(obT[:, g, T - 1:HALF:-2], b[:, 0:256], b[:, 256:512], ALU.add).then_inc(ob_done, 1)
                elif kind == "mix":
                    _, g, j = st
                    bank = take(G, st)
                    uu = ug[:, 4 * j:4 * j + 4, g * P:(g + 1) * P]
                    nc.vector.scalar_tensor_tensor(uu, bank[:].rearrange("p (t n) -> p t n", t=4), cols[:, 8 + g:9 + g], uu,
                                                   ALU.add, ALU.mult).then_inc(G.freed(st), 1)
                elif kind == "h_split":
                    k = st[1]
                    dve.wait_ge(h_hi_done, k + 1)
                    nc.vector.tensor_tensor(h_lo[:, k, :], hT[:, k, :], h_hi[:, k, :].bitcast(F32), ALU.subtract).then_inc(h_lo_done, 1)
                elif kind == "o_split":
                    _, b, g = st
                    dve.wait_ge(o_hi_done, 4 * (0, 2, 1)[b] + g + 1)
                    nc.vector.tensor_tensor(o_lo[b][:, g, :], (oaT, obT, ocT)[b][:, g, :], o_hi[:, g, :].bitcast(F32),
                                            ALU.subtract).then_inc(o_lo_done, 1)
                elif kind == "merge":
                    q = st[1]
                    b, jj = MERGE[q]
                    if q == 0:
                        for i in range(4):
                            split_unit(i)
                    split_unit(3 * q + 4)
                    split_unit(3 * q + 5)
                    for j in range(2):
                        key = ("branch", q, j)
                        bank = take(G, key)
                        dve.wait_ge(*G.drained(("gate", q, j)))
                        if b == 0:
                            nc.vector.tensor_tensor(mT[:, jj, j * HALF:(j + 1) * HALF], bank[:], sig[j], ALU.mult).then_inc(G.freed(key), 1)
                        else:
                            if q > NK:
                                dve.wait_ge(merged_done, 2 * (q - NK) - 1 + j)
                            nc.vector.tensor_tensor(gated[j], bank[:], sig[j], ALU.mult).then_inc(G.freed(key), 1)
                    split_unit(3 * q + 6)
                elif kind == "ada_sum":
                    part = st[1]
                    dve.wait_ge(d_ada, 16 * (part + 1))
                    acc = rows[:, part // 4, part // 2 % 2 * HALF:(part // 2 % 2 + 1) * HALF]
                    for k in range(4):
                        cs = csilu[:, 0, 4 * (part % 2) + k:4 * (part % 2) + k + 1]
                        if k == 0 and part % 2 == 0:
                            step(nc.vector.tensor_scalar(acc, ada_part[:, 0, :], cs, None, ALU.mult))
                        else:
                            step(nc.vector.scalar_tensor_tensor(acc, ada_part[:, k, :], cs, acc, ALU.mult, ALU.add))
                    dve.sem_inc(ada_added, 1)
                    if part % 2:
                        dve.sem_inc(ada_summed, 1)
                elif kind == "ada_rows":
                    nn = st[1]
                    seg, j = nn // 2, nn % 2
                    bank = take(G, st)
                    dve.wait_ge(d_rows, 32 * (nn + 1))
                    dst = rows[:, seg, j * HALF:(j + 1) * HALF]
                    step(nc.vector.tensor_tensor(dst, bank[:], ada_bias, ALU.add))
                    dve.sem_inc(G.freed(st), 1)
                    if seg == 1:
                        dve.sem_inc(rows_done, 1)
                    elif seg == 2:
                        nc.vector.scalar_tensor_tensor(dst, dst, 1.0, norm_row, ALU.add, ALU.mult).then_inc(rows_done, 1)
                    else:
                        nc.vector.tensor_tensor(dst, dst, norm_row, ALU.mult).then_inc(rows_done, 1)
                elif kind == "out_split":
                    u = st[1]
                    dve.wait_ge(out_hi_done, u + 1)
                    cut = (slice(None), u // 2, slice(u % 2 * 4, u % 2 * 4 + 4))
                    nc.vector.tensor_tensor(out_lo[cut], out_raw[u], out_hi[cut].bitcast(F32), ALU.subtract).then_inc(out_lo_done, 1)
                elif kind == "m_split":
                    t = st[1]
                    dve.wait_ge(mt_hi_done, t + 1)
                    nc.vector.tensor_tensor(mt_lo[:, t % 2], mT[:, :, t * P:(t + 1) * P], mt_hi[:, t % 2].bitcast(F32),
                                            ALU.subtract).then_inc(mt_lo_done, 1)
                elif kind == "y_norm":
                    t = st[1]
                    y = ybuf[t % 2]
                    dve.wait_ge(y_ss, t + 1)
                    nc.vector.tensor_scalar(ss[:, 16 + t:17 + t], ss[:, t:t + 1], EPS, None, ALU.add).then_inc(y_ms, 1)
                    dve.wait_ge(rows_done, 8)
                    dve.wait_ge(y_rs, t + 1)
                    nc.vector.scalar_tensor_tensor(y, y, rs[:, t:t + 1], rows[:, 0, :], ALU.mult, ALU.mult).then_inc(yg, 1)
                    dve.wait_ge(d_xre[t % 2], 16 * (t // 2 + 1))
                    dve.wait_ge(yg, t + 1)
                    nc.vector.tensor_tensor(x1[:, t, :], y, xre[t % 2], ALU.add).then_inc(x1_done, 1)
                    dve.wait_ge(x1_ss, t + 1)
                    nc.vector.tensor_scalar(ss[:, 24 + t:25 + t], ss[:, 8 + t:9 + t], EPS, None, ALU.add).then_inc(x1_ms, 1)
                    dve.wait_ge(x1_rs, t + 1)
                    step(nc.vector.scalar_tensor_tensor(y, x1[:, t, :], rs[:, 8 + t:9 + t], rows[:, 2, :], ALU.mult, ALU.mult))
                    nc.vector.tensor_tensor(y, y, rows[:, 1, :], ALU.add).then_inc(h2_done, 1)
                elif kind == "h2_turn":
                    t = st[1]
                    bank = take(G, st + (0,))
                    nc.vector.tensor_copy(h2T[:, 0:4, t * P:(t + 1) * P], bank[:].rearrange("p (k t) -> p k t", k=4)).then_inc(G.freed(st + (0,)), 1)
                elif kind == "router":
                    bank = take(G, st + (0,))
                    logits = bank[:, 0:NT * NE].rearrange("p (t e) -> p t e", e=NE)
                    step(nc.vector.tensor_reduce(pmax[:], logits, AX.X, ALU.max))
                    step(nc.vector.tensor_tensor(prob, logits, pmax[:].rearrange("p (t o) -> p t o", o=1).to_broadcast([P, NT, NE]), ALU.subtract))
                    dve.sem_inc(G.freed(st + (0,)), 1)
                    dve.sem_inc(r_sub, 1)
                    dve.wait_ge(r_exp, 1)
                    step(nc.vector.tensor_reduce(psumm[:], prob, AX.X, ALU.add))
                    step(nc.vector.reciprocal(psumm[:], psumm[:]))
                    nc.vector.tensor_tensor(prob, prob, psumm[:].rearrange("p (t o) -> p t o", o=1).to_broadcast([P, NT, NE]),
                                            ALU.mult).then_inc(r_prob, 1)
                elif kind == "router_turn":
                    for j in range(2):
                        bank = take(G, st + (j,))
                        nc.vector.tensor_copy(aff[:, j * HALF:(j + 1) * HALF], bank[0:NE, :]).then_inc(G.freed(st + (j,)), 1)
                    dve.wait_ge(*G.drained(st + (1,)))
                elif kind == "choose":
                    a, b = aff, aff2
                    for r in range(CAP // 8):
                        v8, i8 = topv[:, 8 * r:8 * r + 8], topi[:, 8 * r:8 * r + 8]
                        step(nc.vector.max(v8, a))
                        nc.vector.max_index(i8, v8, a)
                        step(nc.vector.match_replace(b, v8, a, -1.0))
                        a, b = b, a
                    nc.vector.tensor_copy(topf, topi).then_inc(chosen, 1)
                elif kind == "choose_turn":
                    nc.vector.tensor_copy(gates[:], take(G, st + (0,))[:, 0:NE]).then_inc(G.freed(st + (0,)), 1)
                    nc.vector.tensor_copy(idx[:], take(G, st + (1,))[:, 0:NE]).then_inc(G.freed(st + (1,)), 1)

            dve.wait_ge(G.sems["dve"], G.count["dve"])

            def split(e, u):
                if u in BY_POOL:
                    return
                dve.wait_ge(hi_done, e * UNITS + (u + 1))
                nc.vector.tensor_tensor(wlo[u % PAIRS], raw[u % RAW], whi[u % PAIRS].bitcast(F32), ALU.subtract).then_inc(lo_dve, 1)

            def gathered(n, j):
                dve.wait_ge(tx_hi, n * 2 + (j + 1))
                nc.vector.tensor_tensor(xe_lo[:, 4 * j:4 * j + 4, :], banks[4][:].rearrange("p (k t) -> p k t", k=4),
                                        xe_hi[:, 4 * j:4 * j + 4, :].bitcast(F32), ALU.subtract).then_inc(tx_lo, 1)

            def hidden(e, j):
                dve.wait_ge(th_hi, e * 2 + (j + 1))
                nc.vector.tensor_tensor(ht_lo[:, 4 * j:4 * j + 4, :], banks[6][:].rearrange("p (k t) -> p k t", k=4),
                                        ht_hi[:, 4 * j:4 * j + 4, :].bitcast(F32), ALU.subtract).then_inc(th_lo, 1)

            def gate_b(e, j):
                dve.wait_ge(a_drained, e * 2 + (j + 1))
                dve.wait_ge(used, e * UNITS + (4 * j + 4))
                nc.vector.tensor_tensor(hid[:, j * HALF:(j + 1) * HALF], banks[2 * j + 1][:], sa[j], ALU.mult).then_inc(b_drained, 1)

            def expert(e, before):
                if before is not None:
                    gate_b(before, 1)
                    split(e, 0)
                    split(e, 1)
                    gathered(e, 0)
                    hidden(before, 1)
                    split(e, 2)
                    gathered(e, 1)
                    split(e, 3)
                    split(e, 4)
                    split(e, 5)
                for u in range(6, 9):
                    split(e, u)
                gate_b(e, 0)
                split(e, 9)
                split(e, 10)
                hidden(e, 0)
                split(e, 11)

            gathered(0, 0)
            gathered(0, 1)
            dve.wait_ge(*lo_done(0, PAIRS - 1))
            expert(0, None)
            with dve.Fori(0, NE - 1) as i:
                expert(i + 1, i)
            gate_b(NE - 1, 1)
            hidden(NE - 1, 1)
            for t in range(NT):
                dve.wait_ge(f_ss, t + 1)
                nc.vector.tensor_scalar(ss[:, 24 + t:25 + t], ss[:, 16 + t:17 + t], EPS, None, ALU.add).then_inc(f_ms, 1)
                dve.wait_ge(f_rs, t + 1)
                nc.vector.scalar_tensor_tensor(fin[t], fin[t], rs[:, 16 + t:17 + t], rows[:, 3, :], ALU.mult, ALU.mult).then_inc(f_scaled, 1)
                if t % 2:
                    dve.wait_ge(f_scaled, t + 1)
                    dve.wait_ge(x1_back, 16)
                    nc.vector.tensor_tensor(fin[t], fin[t], x1_again[:, t, :], ALU.add).then_inc(f_out[1], 1)

        @block.gpsimd
        def _(pool):
            def root(dst, src, w):
                return nc.gpsimd.tensor_tensor(dst, src, half_pow[:, 0:w], ALU.pow)

            nc.gpsimd.memset(ident[:], 0.0).then_inc(ident_ready, 1)
            nc.gpsimd.memset(half_pow[:], -0.5).then_inc(pow_ready, 1)
            pool.wait_ge(ident_ready, 1)
            nc.gpsimd.affine_select(out=ident[:], in_=ident[:], compare_op=ALU.not_equal, fill=1.0, base=0,
                                    pattern=[[-1, P]], channel_multiplier=1).then_inc(ident_ready, 1)
            pool.wait_ge(pow_ready, 1)
            n = [0]
            for st in STEPS:
                kind = st[0]
                if kind == "norm_s":
                    g = st[1]
                    nt = NTC if g == 0 else 4
                    pool.wait_ge(x_ms, g + 1)
                    root(rs[:, 4 * g:4 * g + nt], ss[:, 16 + 4 * g:16 + 4 * g + nt], nt).then_inc(x_rs, 1)
                elif kind == "ga":
                    t = st[1]
                    if t == 0:
                        pool.wait_ge(d_row, 16)
                    pool.wait_ge(*G.drained(st))
                    g4 = Gt[:, t, :].rearrange("p (h n) -> p h n", h=H)
                    nc.gpsimd.tensor_tensor(g4, g4, gnorm[:].rearrange("p (o n) -> p o n", o=1).to_broadcast([P, H, HD]), ALU.mult).then_inc(ga_gated, 1)
                elif kind == "prepare" and st[2] == 1:
                    h = st[1]
                    pool.wait_ge(kc_ready, 2 * (h + 1))
                    for l in range(8):
                        m = 1 << l
                        nb = TC // (2 * m)
                        src, dst = Fc[:, l % 2], Fc[:, 1 - l % 2]
                        pair = src[:, :, 0:2 * nb].rearrange("p a (b two) -> p a b two", two=2)
                        kf = Kc[:, 0, :].rearrange("p (b two m) -> p b two m", two=2, m=m)
                        kb = Kc[:, 1, :].rearrange("p (b two m) -> p b two m", two=2, m=m)
                        nc.gpsimd.tensor_tensor(kf[:, :, 0, :], kf[:, :, 0, :], pair[:, 0, :, 1:2].to_broadcast([P, nb, m]), ALU.mult)
                        ins = nc.gpsimd.tensor_tensor(kb[:, :, 1, :], kb[:, :, 1, :], pair[:, 1, :, 0:1].to_broadcast([P, nb, m]), ALU.mult)
                        if l < 7:
                            ins = nc.gpsimd.tensor_tensor(dst[:, :, 0:nb], pair[:, :, :, 0], pair[:, :, :, 1], ALU.mult)
                            ins.then_inc(pstep, 1)
                            n[0] += 1
                            pool.wait_ge(pstep, n[0])
                        else:
                            ins.then_inc(ctx_done, 1)
                elif kind == "out":
                    h = st[1]
                    pool.wait_ge(o_ms, h + 1)
                    root(rs[:, 32:40], ss[:, 40:48], 8).then_inc(o_rs, 1)
                    if h == 0:
                        pool.wait_ge(ga_gated, NT)
                    pool.wait_ge(*S2.drained(("out", h, 1)))
                    nc.gpsimd.tensor_tensor(o_sb[:], o_sb[:], Gt[:, :, h * HD:(h + 1) * HD], ALU.mult).then_inc(o_gated, 1)
                elif kind == "vv_norm":
                    pool.wait_ge(v_ms, 1)
                    root(rs[:, 0:32], ss[:, 0:32], 32).then_inc(v_rs, 1)
                elif kind == "merge" and st[1] >= NK:
                    q = st[1]
                    for j in range(2):
                        pool.wait_ge(*G.drained(("branch", q, j)))
                        mm = mT[:, MERGE[q][1], j * HALF:(j + 1) * HALF]
                        nc.gpsimd.tensor_tensor(mm, mm, gated[j], ALU.add).then_inc(merged_done, 1)
                elif kind == "mix" and st[1:] == (0, 0):
                    nc.gpsimd.memset(ones[:], 1.0).then_inc(ones_ready, 1)
                elif kind == "y_norm":
                    t = st[1]
                    pool.wait_ge(y_ms, t + 1)
                    root(rs[:, t:t + 1], ss[:, 16 + t:17 + t], 1).then_inc(y_rs, 1)
                    pool.wait_ge(x1_ms, t + 1)
                    root(rs[:, 8 + t:9 + t], ss[:, 24 + t:25 + t], 1).then_inc(x1_rs, 1)

            for u in range(PAIRS):
                pool.wait_ge(hi_done, u + 1)
                nc.gpsimd.tensor_tensor(wlo[u], raw[u % RAW], whi[u].bitcast(F32), ALU.subtract).then_inc(lo_done(0, u)[0], 1)
            pool.wait_ge(G.sems["dve"], G.count["dve"])
            for j in range(2):
                pool.wait_ge(d_h2[j], 8 * NT)
            pool.wait_ge(d_zero, 16 * NT)
            pool.sem_inc(added, 1)

            def wait(semaphore, value):
                pool.wait_ge(semaphore, value)
                pool.sem_inc(tick, 1)

            def gather(n):
                if not isinstance(n, int) or n:
                    wait(tx_full, n * 2)
                nc.gpsimd.tensor_copy(icur[:, :], idx[:, bass.ds(n, 1)]).then_inc(cur_done, 1)
                wait(cur_done, n + 1)
                pool.indirect_dma_start(xg, None, h2_dram[:, :], bass.IndirectOffsetOnAxis(ap=icur[:, 0:1], axis=0),
                                        bounds_check=T - 1).then_inc(xg_full, 16)

            def gate_of(e):
                nc.gpsimd.tensor_copy(icur2[:, :], idx[:, bass.ds(e, 1)])
                nc.gpsimd.tensor_copy(gcur[:, :], gates[:, bass.ds(e, 1)]).then_inc(cur_g, 1)

            def scatter(e):
                wait(cur_g, e + 1)
                wait(y_drained, e * 2 + 4)
                pool.indirect_dma_start(moe_dram[:, :], bass.IndirectOffsetOnAxis(ap=icur2[:, 0:1], axis=0), yb, None,
                                        compute_op=ALU.add, bounds_check=T - 1).then_inc(sc_done, 16)

            def scattered(e):
                wait(sc_done, e * 16 + 16)
                pool.sem_inc(added, 1)

            def split(e, u):
                wait(hi_done, e * UNITS + (u + 1))
                nc.gpsimd.tensor_tensor(wlo[u % PAIRS], raw[u % RAW], whi[u % PAIRS].bitcast(F32), ALU.subtract).then_inc(lo_pool, 1)

            def expert(e, before, last=False):
                for i, u in enumerate(BY_POOL):
                    if before is not None or u >= PAIRS:
                        split(e, u)
                    if i == 0 and not last:
                        gather(e + 1)
                    if i == 1 and before is not None:
                        scatter(before)
                    if i == 2:
                        if before is not None:
                            scattered(before)
                        gate_of(e)

            gather(0)
            expert(0, None)
            with pool.Fori(0, NE - 2) as e:
                expert(e + 1, e)
            expert(NE - 1, NE - 2, last=True)
            scatter(NE - 1)
            scattered(NE - 1)
            for t in range(NT):
                pool.wait_ge(f_ms, t + 1)
                root(rs[:, 16 + t:17 + t], ss[:, 24 + t:25 + t], 1).then_inc(f_rs, 1)
                if t % 2:
                    pool.wait_ge(f_scaled, t)
                    pool.wait_ge(x1_back, 16)
                    nc.gpsimd.tensor_tensor(fin[t - 1], fin[t - 1], x1_again[:, t - 1, :], ALU.add).then_inc(f_out[0], 1)


_INS = ["x", "c", "ctx", "c_ctx", "ada_w", "ada_b", "norm_w", "w_in", "hgrn_lb_raw", "hgrn_gnorm_w", "sgu_w", "sgu_b",
        "sgu_norm_w", "w_branch", "w_out", "router_w", "exp_w13", "exp_w2"]


def kernel(**inputs):
    import concourse.bacc as bacc
    from concourse.bass_utils import run_bass_kernel_spmd

    nc = bacc.Bacc("TRN2", target_bir_lowering=False, num_devices=1)
    arrays, args = {}, []
    tokens, channels = dft_tables()
    extra = dict(token_dft=tokens, channel_dft=channels, level_masks=level_masks())
    for name in _INS + list(extra):
        a = np.ascontiguousarray(inputs[name] if name in inputs else extra[name])
        arrays[f"in_{name}"] = a
        args.append(nc.dram_tensor(f"in_{name}", a.shape, mybir.dt.from_np(a.dtype), kind="ExternalInput").ap())
    out = nc.dram_tensor("out", (1, T, D), F32, kind="ExternalOutput").ap()
    h2 = nc.dram_tensor("h2", (T, D), F32, kind="Internal").ap()
    moe = nc.dram_tensor("moe", (T, D), F32, kind="Internal").ap()
    x1 = nc.dram_tensor("x1", (T, D), F32, kind="Internal").ap()
    build(nc, *args, out, h2, moe, x1)
    r = run_bass_kernel_spmd(nc, [arrays], core_ids=[0])
    return r.results[0]["out"]
```

```python
import math
from contextlib import ExitStack

import numpy as np

import concourse.bass as bass
from concourse import mybir

ALU = mybir.AluOpType
ACT = mybir.ActivationFunctionType
AX = mybir.AxisListType
F32 = mybir.dt.float32
F32R = mybir.dt.float32r
U32 = mybir.dt.uint32
U8 = mybir.dt.uint8

P = 128
D = 1024
T = 1024
TC = 256
H = 4
HD = 128
AW = H * HD
NE = 16
CAP = 2 * T // NE
NK = D // P
NT = T // P
NTC = TC // P
HALF = 512
EPS = 1e-6
FLOOR = 1e-20
LEVELS = 7
COL = dict(q=0, ff=AW, fb=2 * AW, i=3 * AW, ga=4 * AW, zb=5 * AW, u=6 * AW, v=7 * AW, gate=8 * AW)
SLOTS = 4
BLK = NK * HALF
UNIT = 4 * HALF
UNITS = 12
RAW = 6
PAIRS = 6
BY_POOL = (1, 4, 7, 10)
MERGE = [(b, j) for b in range(3) for j in range(NK)]
PART = 4 * P
MERGE_UNITS = 3 * len(MERGE)
RING = 4
Z_RAW, Z_PAIRS = 2, 3
ADA_AT = {NK - 1 + i: i for i in range(16)}


def dft_tables():
    t = np.arange(T // 2)[:, None].astype(np.float64)
    even, odd = np.arange(0, T // 2 + 1, 2), np.arange(1, T // 2, 2)
    w = 2 * np.pi / T
    parts = [np.cos(w * ((t * even) % T)), np.sin(w * ((t * even[1:-1]) % T)),
             np.cos(w * ((t * odd) % T)), np.sin(w * ((t * odd) % T))]
    tokens = np.concatenate(parts, 1)
    d = np.arange(HD)[:, None] * np.arange(HD)[None, :] % HD * (2 * np.pi / HD)
    s = 1.0 / math.sqrt(T * HD)
    channels = np.concatenate([np.cos(d) * s, np.sin(d) * s], 1)
    return tokens.astype(np.float32), channels.astype(np.float32)


def level_masks():
    s, t = np.arange(P)[:, None], np.arange(P)[None, :]
    out = [(s // (2 * m) == t // (2 * m)) & (s // m != t // m) for m in (1 << l for l in range(LEVELS))]
    return np.stack(out, 1).astype(np.float32)


class Psum:

    def __init__(self, banks, full, drained):
        self.banks, self.full, self.sems = banks, full, drained
        self.keys, self.count, self.n = {}, {e: 0 for e in drained}, 0
        self.jobs = []

    def plan(self, key, consumer):
        assert key not in self.keys, key
        self.count[consumer] += 1
        self.keys[key] = self.n
        self.jobs.append((consumer, self.count[consumer]))
        self.n += 1

    def bank(self, key):
        return self.banks[self.keys[key] % len(self.banks)]

    def reuses(self, key):
        return self.keys[key] >= len(self.banks)

    def last_drained(self, key):
        consumer, count = self.jobs[self.keys[key] - len(self.banks)]
        return self.sems[consumer], count

    def filled(self, key):
        return self.full, self.keys[key] + 1

    def freed(self, key):
        return self.sems[self.jobs[self.keys[key]][0]]

    def drained(self, key):
        consumer, count = self.jobs[self.keys[key]]
        return self.sems[consumer], count


def schedule():
    steps = [("small",)]
    steps += [("ada_cols", n) for n in range(4)] + [("ada_turn",)]
    steps += [("norm_s", 0), ("norm_s", 1), ("norm_x", 0), ("norm_s", 2), ("norm_x", 1),
              ("h_split", 1), ("norm_x", 2), ("h_split", 2), ("h_split", 0)]

    def z_units(h):
        return [("z", w, h, kh) for w in ("ff", "fb", "q", "i") for kh in range(2)]

    steps += [("z", "i", 0, 0), ("z", "i", 0, 1)] + z_units(0)[:2] + [("v_turn", 0)] + z_units(0)[2:6]
    steps += [("prepare", 0, part) for part in range(3)]
    for h in range(H):
        fill = z_units(h + 1) if h + 1 < H else [("z", "u", g, kh) for g in range(4) for kh in range(2)]
        gate = [("z", "ga", h - 1, kh) for kh in range(2)] if h else []
        steps += [("level", h, 0)] + ([("v_turn", h)] if h else []) + [("level", h, 1), fill[0]]
        steps += [("ctx_turn", h), ("level", h, 2), fill[1], ("ctx_state", h)] + gate[:1]
        if h + 1 < H:
            steps += [("prepare", h + 1, 0)]
        steps += [("level", h, 3)] + gate[1:]
        steps += [("level", h, 4), fill[2]] + ([("o_turn", h - 1)] if h else [])
        steps += [("level", h, 5), fill[3], ("level", h, 6), fill[4], ("level", h, 7), fill[5], ("k_turn", h)]
        if h + 1 < H:
            steps += [("prepare", h + 1, 1)]
        steps += [fill[6], ("kv", h), fill[7]]
        if h + 1 < H:
            steps += [("prepare", h + 1, 2)]
        steps += [("out", h)]
    steps += [("z", "ga", H - 1, kh) for kh in range(2)]
    steps += [("o_turn", H - 1)] + [("wide", "zb", k) for k in range(NK)] + [("fold",)]
    steps += [("wide", "v", k) for k in range(NK)] + [("vv_norm",)]
    steps += [("dft", g, par) for g in range(4) for par in range(2)]
    for g in range(4):
        steps += [("dft2", g, 0), ("dft2", g, 1), ("o_split", 0, g)]
    steps += [("mix", g, j) for g in range(4) for j in range(2)]
    for q, (b, j) in enumerate(MERGE):
        if j == 0 and q:
            steps += [("o_split", b, g) for g in range(4)]
        if q == len(MERGE) - 1:
            steps += [("out_split", 0)]
        steps += [("merge", q)]
        if ADA_AT.get(q - 1, 0) % 2:
            steps += [("ada_rows", ADA_AT[q - 1] // 2)]
        if q in ADA_AT:
            steps += [("ada_sum", ADA_AT[q])]
    steps += [("out_split", 1), ("m_split", 0), ("out_split", 2), ("m_split", 1), ("out_split", 3)]
    for t in range(NT):
        steps += [("y", t)] + ([("m_split", t + 2)] if t + 2 < NT else []) + [("y_norm", t)]
        steps += [("h2_turn", t - 1)] if t else []
        steps += [("logits", t - 2)] if t > 1 else []
    steps += [("h2_turn", NT - 1), ("logits", NT - 2), ("logits", NT - 1), ("router",), ("router_turn",), ("choose",), ("choose_turn",)]
    return steps


def build(nc, x, c, ctx_in, c_ctx, ada_w, ada_b, norm_w, w_in, hgrn_lb_raw, hgrn_gnorm_w, sgu_w, sgu_b,
          sgu_norm_w, w_branch, w_out, router_w, exp_w13, exp_w2, token_dft, channel_dft, masks_in, out,
          h2_dram, moe_dram, x1_dram):
    STEPS = schedule()
    UNITS_Z = [st for st in STEPS if st[0] in ("z", "wide")]
    z_index = {st: i for i, st in enumerate(UNITS_Z)}
    with ExitStack() as stack:
        def sb(name, shape, dt=F32):
            return stack.enter_context(nc.sbuf_tensor(name, shape, dt))

        def sem(name):
            return stack.enter_context(nc.semaphore(name))

        space = -(-nc.sbuf_base // 32) * 32
        sb("fence", [P, 49152])
        AT_H, AT_W, AT_V, AT_OA, AT_A, AT_B = 0, 8192, 20480, 28672, 32768, 40960

        def place(name, at, n, dt=F32):
            return nc.alloc_sbuf_tensor_at(name, [P, n], dt, offset=space + 4 * at)

        r_h = place("r_h", AT_H, NK * T)
        r_w = place("r_w", AT_W, 3 * BLK)
        r_v = place("r_v", AT_V, 8192)
        r_oa = place("r_oa", AT_OA, H * T)
        r_a = place("r_a", AT_A, 8192)
        r_b = place("r_b", AT_B, 8192)

        at_c = -(-nc.sbuf_base // 32) * 32
        r_c = sb("r_c", [P, NK * TC])
        hT = r_h[:].rearrange("p (k t) -> p k t", k=NK)
        hcT = r_c[:].rearrange("p (k t) -> p k t", k=NK)
        wslot = [r[:, s * BLK:(s + 1) * BLK].rearrange("p (k n) -> p k n", k=NK) for r in (r_w, r_v) for s in range(2)]
        V = [r_v[:, 1024 * i:1024 * (i + 1)].rearrange("p (t n) -> p t n", t=NT) for i in range(2)]
        oaT = r_oa[:].rearrange("p (h t) -> p h t", h=H)
        U = r_b[:, 7168:8192]
        totals = sb("totals", [P, 2 * NT])
        hb = []
        for r in (r_a, r_b):
            hb.append(dict(X1=r[:, 0:2048].rearrange("p (c a t) -> p c a t", c=NT, a=2),
                           X2=r[:, 2048:4096].rearrange("p (c a t) -> p c a t", c=NT, a=2),
                           F=r[:, 4096:6144],
                           A=r[:, 6144:7168].rearrange("p (c t) -> p c t", c=NT)))
        xbuf = [r_a[:, 0:4096].rearrange("p (t n) -> p t n", t=4), r_b[:, 0:4096].rearrange("p (t n) -> p t n", t=4),
                r_a[:, 4096:8192].rearrange("p (t n) -> p t n", t=4)]
        adar = r_oa[0:2, 0:2048]
        adab = r_oa[0:2, 2048:4096]
        zb = r_b[:, 4096:8192].rearrange("p (t n) -> p t n", t=NT)
        tdft = r_v[:, 0:4096].rearrange("p (t n) -> p t n", t=4)
        zfold = [r_b[:, 0:2048].rearrange("p (t n) -> p t n", t=4),
                 r_b[:, 2048:4096].rearrange("p (t n) -> p t n", t=4)]
        AB = r_v[:, 4096:8192].rearrange("p (g e n) -> p g e n", g=4, e=2)
        obT = r_a[:, 4096:8192].rearrange("p (g t) -> p g t", g=4)
        vg = r_b[:, 4096:8192].rearrange("p (t n) -> p t n", t=NT)
        bias_row = r_v[:, 0:HALF].rearrange("p (g q) -> p g q", g=4)
        biased = [r_v[:, HALF * (1 + j):HALF * (2 + j)].rearrange("p (t n) -> p t n", t=4) for j in range(2)]
        ocT = r_a[:, 0:4096].rearrange("p (g t) -> p g t", g=4)
        uT = ocT
        mT = r_b[:].rearrange("p (k t) -> p k t", k=NK)
        rows = r_oa[:].rearrange("p (r n) -> p r n", r=4)
        x1 = r_a[:].rearrange("p (t n) -> p t n", t=NT)
        h2T = mT
        ybuf = [r_v[:, 6144 + 1024 * i:7168 + 1024 * i] for i in range(2)]
        xre = [r_v[:, 4096 + 1024 * i:5120 + 1024 * i] for i in range(2)]
        h_hi = place("h_hi", AT_W, NK * T, F32R)[:].rearrange("p (k t) -> p k t", k=NK)
        h_lo = place("h_lo", AT_H, NK * T, F32R)[:].rearrange("p (k t) -> p k t", k=NK)
        hc_hi = place("hc_hi", AT_V + 2048, NK * TC, F32R)[:].rearrange("p (k t) -> p k t", k=NK)
        hc_lo = nc.alloc_sbuf_tensor_at("hc_lo", [P, NK * TC], F32R, offset=at_c)[:].rearrange("p (k t) -> p k t", k=NK)
        raw_z = [r_v[:, 4096 + u * PART:4096 + (u + 1) * PART].rearrange("p (k n) -> p k n", k=4) for u in range(Z_RAW)]
        wz = place("wz", AT_V + 4096 + Z_RAW * PART, 2 * Z_PAIRS * PART, F32R)
        wz_hi = [wz[:, 2 * u * PART:(2 * u + 1) * PART].rearrange("p (k n) -> p k n", k=4) for u in range(Z_PAIRS)]
        wz_lo = [wz[:, (2 * u + 1) * PART:(2 * u + 2) * PART].rearrange("p (k n) -> p k n", k=4) for u in range(Z_PAIRS)]
        o_hi = place("o_hi", AT_W + 2 * BLK, H * T, F32R)[:].rearrange("p (k t) -> p k t", k=H)
        o_lo = [place(f"o_lo{b}", at, H * T, F32R)[:].rearrange("p (k t) -> p k t", k=H)
                for b, at in enumerate((AT_OA, AT_A + 4096, AT_A))]
        raw_m = [r_v[:, 6144 + u * PART:6144 + (u + 1) * PART].rearrange("p (k n) -> p k n", k=4) for u in range(RING)]
        wm = place("wm", AT_V + 2048, 2 * RING * PART, F32R)
        wm_hi = [wm[:, 2 * u * PART:(2 * u + 1) * PART].rearrange("p (k n) -> p k n", k=4) for u in range(RING)]
        wm_lo = [wm[:, (2 * u + 1) * PART:(2 * u + 2) * PART].rearrange("p (k n) -> p k n", k=4) for u in range(RING)]
        out_raw = [x.rearrange("p (k n) -> p k n", k=4) for x in (
            r_a[:, 4096:6144], r_a[:, 6144:8192], r_c[:], r_w[:, 2 * BLK:2 * BLK + 2048])]
        out_hi = place("out_hi", AT_W, 2 * BLK, F32R)[:].rearrange("p (n k c) -> p n k c", n=2, k=NK)
        out_lo = place("out_lo", AT_H, 2 * BLK, F32R)[:].rearrange("p (n k c) -> p n k c", n=2, k=NK)
        mt_hi = place("mt_hi", AT_V, 2 * D, F32R)[:].rearrange("p (s k t) -> p s k t", s=2, k=NK)
        mt_lo = place("mt_lo", AT_V + 2 * D, 2 * D, F32R)[:].rearrange("p (s k t) -> p s k t", s=2, k=NK)

        ident = sb("ident", [P, P])
        half_pow = sb("half_pow", [P, 32])
        small = sb("small", [16, P])
        cols = sb("cols", [P, 16])
        gate_add = sb("gate_add", [P, 8])
        gate_mul = sb("gate_mul", [P, 8])
        lb = sb("lb", [P, 4, 8])
        craw = sb("craw", [P, 2, NK])
        csilu = sb("csilu", [P, 2, NK])
        scale1 = sb("scale1", [P, NK, 2])
        shift1 = sb("shift1", [P, NK, 2])
        ss = sb("ss", [P, 48])
        rs = sb("rs", [P, 48])
        masks = sb("masks", [P, LEVELS, P], U8)
        gnorm = sb("gnorm", [P, 1])
        ones = sb("ones", [P, P])
        Vc = r_oa[:, 3072:3072 + NTC * HD].rearrange("p (t n) -> p t n", t=NTC)
        Fc = r_oa[:, 2048:3072].rearrange("p (i a t) -> p i a t", i=2, a=2)
        Kc = r_a[:, 7168:7680].rearrange("p (a t) -> p a t", a=2)
        big = r_w[:, 2 * BLK:3 * BLK]
        KT = big[:, 0:2048].rearrange("p (a c k) -> p a c k", a=2, c=NT)
        S = big[:, 2048:4096].rearrange("p (a c k) -> p a c k", a=2, c=NT)
        KcT = big[:, 0:512].rearrange("p (c k) -> p c k", c=4)
        o_sb = sb("o_sb", [P, NT, HD])
        o_sq = big[:, 1024:2048].rearrange("p (c t) -> p c t", c=NT)
        zero = big[:, 1024:2048]
        mask_raw = big[:, 0:LEVELS * P].rearrange("p (l t) -> p l t", t=P)
        wsraw = o_sb[:, 0:4, :]
        wsT = o_sb[:, 4:8, :]
        pq = [r_c[:, 512 * i:512 * (i + 1)] for i in range(2)]
        snorm = r_c[:, 1024:1536]
        cdft = r_c[:, 1536:1792]
        sig = [r_v[:, 512 * i:512 + 512 * i] for i in range(2)]
        gated = [r_v[:, 1024 + 512 * i:1536 + 512 * i] for i in range(2)]
        ada_part = r_c[:].rearrange("p (k n) -> p k n", k=4)
        flat = o_sb[:].rearrange("p a b -> p (a b)")
        ada_bias, norm_row = flat[:, 0:HALF], flat[:, HALF:]
        rw = ones[:].rearrange("p (k e) -> p k e", e=NE)
        prob = r_v[:, 2816:2944].rearrange("p (t e) -> p t e", e=NE)
        pmax = sb("pmax", [P, NT])
        psumm = sb("psumm", [P, NT])
        aff, aff2 = r_v[0:NE, 0:1024], r_v[0:NE, 1024:2048]
        topv, topf = r_v[0:NE, 2048:2048 + CAP], r_v[0:NE, 2048 + CAP:2048 + 2 * CAP]
        topi = r_v[0:NE, 2048 + 2 * CAP:2048 + 3 * CAP].bitcast(U32)
        gates = sb("gates", [P, NE])
        idx = sb("idx", [P, NE], U32)
        raw = [r_w[:, u * UNIT:(u + 1) * UNIT].rearrange("p (k n) -> p k n", k=4) for u in range(RAW)]
        def pairs(name, at, n):
            t = place(name, at, n * UNIT, F32R)
            return [t[:, u * UNIT:(u + 1) * UNIT].rearrange("p (k n) -> p k n", k=4) for u in range(n)]

        whi = pairs("w_hi0", AT_H, 4) + pairs("w_hi1", AT_A, 2)
        wlo = pairs("w_lo0", AT_B, 4) + pairs("w_lo1", AT_A + 4096, 2)
        x1_again = r_w[:, 0:NT * D].rearrange("p (t n) -> p t n", t=NT)
        xg = r_v[:, 0:1024]
        hid = r_v[:, 1024:2048]
        sa = [r_v[:, 2048 + 512 * i:2560 + 512 * i] for i in range(2)]
        yb = r_v[:, 3072:4096]
        m_x = place("m_x", AT_V + 4096, 2048, F32R)
        m_t = place("m_t", AT_V + 6144, 2048, F32R)
        xe_hi, xe_lo = (m_x[:, 1024 * i:1024 * (i + 1)].rearrange("p (k t) -> p k t", k=NK) for i in range(2))
        ht_hi, ht_lo = (m_t[:, 1024 * i:1024 * (i + 1)].rearrange("p (k t) -> p k t", k=NK) for i in range(2))
        gcur = sb("gcur", [P, 1])
        icur = sb("icur", [P, 1], U32)
        icur2 = sb("icur2", [P, 1], U32)
        fin = [r_b[:, 1024 * i:1024 * (i + 1)] for i in range(8)]

        banks = [stack.enter_context(nc.psum_tensor(f"bank{i}", [P, 512], F32)) for i in range(8)]
        G = Psum(banks[0:4], sem("g_full"), dict(act=sem("g_drained_act"), dve=sem("g_drained_dve")))
        L = Psum(banks[4:6], sem("l_full"), dict(act=sem("l_drained_act"), dve=sem("l_drained_dve")))
        S2 = Psum(banks[6:8], sem("s_full"), dict(act=sem("s_drained_act"), dve=sem("s_drained_dve")))

        def wide_stream(t):
            return G if t < 4 else L if t < 6 else S2

        for st in STEPS:
            k = st[0]
            if k in ("small", "ada_cols", "ada_turn"):
                G.plan(st, "dve")
            elif k == "norm_x":
                for kk in range(NK):
                    G.plan(st + (kk,), "act" if kk % 2 else "dve")
            elif k == "z":
                if st[3] == 0:
                    for j in range(3 if st[1] in ("i", "ff", "fb") else 2):
                        G.plan(("zj",) + st[1:3] + (j,), "act")
            elif k == "level":
                for j in range(2):
                    L.plan(st + (j,), "dve" if st[2] else "act")
            elif k in ("ctx_turn", "ctx_state"):
                S2.plan(st, "act")
            elif k == "k_turn":
                for j in range(4):
                    S2.plan(st + (j,), "act")
            elif k == "kv":
                for j in range(4):
                    S2.plan(st + (j,), "dve")
            elif k == "out":
                for j in range(2):
                    S2.plan(st + (j,), "act")
            elif k == "o_turn":
                for j in range(2):
                    S2.plan(st + (j,), "dve")
            elif k in ("dft", "dft2"):
                G.plan(st, "act")
            elif k == "v_turn":
                for j in range(3):
                    G.plan(st + (j,), "act")
            elif k == "wide":
                if st[2] == 0:
                    for t in range(NT):
                        wide_stream(t).plan(("wj", st[1], t), "act")
            elif k in ("mix", "ada_rows"):
                G.plan(st, "dve")
            elif k == "merge":
                for j in range(2):
                    G.plan(("gate",) + st[1:] + (j,), "act")
                for j in range(2):
                    G.plan(("branch",) + st[1:] + (j,), "dve")
            elif k == "y":
                for n in range(2):
                    G.plan(st + (n,), "act")
            elif k == "h2_turn":
                for j in range(2):
                    G.plan(st + (j,), "act" if j else "dve")
            elif k in ("router_turn", "choose_turn"):
                for j in range(2):
                    G.plan(st + (j,), "dve")
        w_full = [sem(f"w_full{s}") for s in range(SLOTS)]

        d_small, d_mod, d_row, d_late, d_mask, d_tab, d_ws = (sem(n) for n in ("d_small", "d_mod", "d_row", "d_late", "d_mask", "d_tab", "d_ws"))
        d_x = [sem(f"d_x{g}") for g in range(3)]
        d_xre = [sem("d_xre0"), sem("d_xre1")]
        d_h2, d_zero = [sem("d_h2_0"), sem("d_h2_1")], sem("d_zero")
        ident_ready, pow_ready, zero_ready = sem("ident_ready"), sem("pow_ready"), sem("zero_ready")
        csilu_ready = sem("csilu_ready")
        lb_max, lb_ready = sem("lb_max"), sem("lb_ready")
        x_ss, x_ms, x_rs, x_normed = sem("x_ss"), sem("x_ms"), sem("x_rs"), sem("x_normed")
        z_full = [sem(f"z_full{s}") for s in range(Z_RAW)]
        z_hi_done, z_lo_done, z_used = sem("z_hi_done"), sem("z_lo_done"), sem("z_used")
        x_ready = sem("x_ready")
        kc_ready = sem("kc_ready")
        ctx_done = sem("ctx_done")
        s_ready = sem("s_ready")
        o_ms, o_rs, o_ready = (sem(n) for n in ("o_ms", "o_rs", "o_ready"))
        fold_done, vv_done = sem("fold_done"), sem("vv_done")
        v_sq, v_ms, v_rs = sem("v_sq"), sem("v_ms"), sem("v_rs")
        ws_t, vv_sq_ready, ob_done = sem("ws_t"), sem("vv_sq_ready"), sem("ob_done")
        merged_done = sem("merged_done")
        rows_done = sem("rows_done")
        h_hi_done, h_lo_done, o_hi_done, o_lo_done = sem("h_hi_done"), sem("h_lo_done"), sem("o_hi_done"), sem("o_lo_done")
        m_full = [sem(f"m_full{s}") for s in range(RING)]
        m_hi_done, m_lo_done, m_used = sem("m_hi_done"), sem("m_lo_done"), sem("m_used")
        d_ada, d_rows, ones_ready, ada_summed, ada_added = (sem(n) for n in ("d_ada", "d_rows", "ones_ready", "ada_summed", "ada_added"))
        d_out_w = [sem(f"d_out_w{s}") for s in range(4)]
        out_hi_done, out_lo_done, mt_hi_done, mt_lo_done = (sem(n) for n in ("out_hi_done", "out_lo_done", "mt_hi_done", "mt_lo_done"))
        y_ss, y_ms, y_rs, x1_done, x1_ss, x1_ms, x1_rs, h2_done = (sem(n) for n in (
            "y_ss", "y_ms", "y_rs", "x1_done", "x1_ss", "x1_ms", "x1_rs", "h2_done"))
        yg = sem("yg")
        r_sub, r_exp, r_prob, chosen = (sem(n) for n in ("r_sub", "r_exp", "r_prob", "chosen"))
        vstep, pstep, tick = sem("dve_step"), sem("pool_step"), sem("pool_tick")
        added = sem("added")
        raw_full = [sem(f"raw_full{s}") for s in range(RAW)]
        hi_done, used = sem("hi_done"), sem("used")
        lo_dve, lo_pool = sem("lo_dve"), sem("lo_pool")
        x1_stored, x1_back = sem("x1_stored"), sem("x1_back")
        a_drained, b_drained = sem("a_drained"), sem("b_drained")
        tx_full, tx_hi, tx_lo, th_full, th_hi, th_lo = (sem(n) for n in ("tx_full", "tx_hi", "tx_lo", "th_full", "th_hi", "th_lo"))
        y_drained = sem("y_drained")
        cur_done, xg_full, sc_done, cur_g = sem("cur_done"), sem("xg_full"), sem("sc_done"), sem("cur_g")
        f_ss, f_ms, f_rs, f_scaled, d_out = (sem(n) for n in ("f_ss", "f_ms", "f_rs", "f_scaled", "d_out"))
        d_bias, logits_done = sem("d_bias"), sem("logits_done")
        f_out = [sem("f_out_pool"), sem("f_out_dve")]
        d_fins = [sem(f"d_fin{t}") for t in range(NT)]

        def lo_done(e, u):
            before = sum(v in BY_POOL for v in range(u))
            if u in BY_POOL:
                return lo_pool, e * len(BY_POOL) + (before + 1)
            return lo_dve, e * (UNITS - len(BY_POOL)) + (u - before + 1)

        def x_at(h, l, j):
            return 2 * (8 * h + l) + j + 1

        def split_parts(g):
            if g == 0:
                return [(hcT[:, k:k + 4, :], hc_hi[:, k:k + 4, :], hc_lo[:, k:k + 4, :]) for k in (0, 4)]
            cut = slice((g - 1) * HALF, g * HALF)
            return [(hT[:, k:k + 2, cut], h_hi[:, k:k + 2, cut], h_lo[:, k:k + 2, cut]) for k in range(0, NK, 2)]

        def z_jobs(st):
            return [("zj",) + st[1:3] + (j,) for j in range(3 if st[1] in ("i", "ff", "fb") else 2)]

        def z_unit_used(i):
            def within(st):
                return st[3] == 0 if st[0] == "z" else st[2] < NK - 1

            st = UNITS_Z[i]
            if within(st):
                return z_used, sum(within(u) for u in UNITS_Z[:i + 1])
            return G.filled(z_jobs(st)[-1]) if st[0] == "z" else S2.filled(("wj", st[1], NT - 1))

        def wide_waits(eng, name):
            for t in (3, 5, 7):
                eng.wait_ge(*wide_stream(t).drained(("wj", name, t)))

        def merge_unit(i):
            b, j = MERGE[i // 3]
            if i % 3 < 2:
                c0, r0 = COL["gate"] + b * D + j * P, i % 3 * HALF
                src = w_in[0, r0:r0 + HALF, c0:c0 + P]
            else:
                src = w_branch[0, b, :, j * P:(j + 1) * P]
            return src.rearrange("(k p) n -> p k n", p=P)

        def unit_used(i):
            if i % 3 == 0:
                return m_used, i // 3 + 1
            return G.filled((("gate", "branch")[i % 3 - 1], i // 3, 1))

        block = stack.enter_context(nc.Block())

        @block.sync
        def _(sp):
            sp.dma_start(small[0:8, :], norm_w[0, 0, :].rearrange("(r n) -> r n", r=8)).then_inc(d_small, 16)
            sp.dma_start(small[8:16, :], hgrn_lb_raw.rearrange("a d (h n) -> (a d h) n", h=H)).then_inc(d_small, 16)
            sp.dma_start(craw[:, 0, :], c[0].rearrange("(p k) -> p k", k=NK)).then_inc(d_mod, 16)
            sp.dma_start(craw[:, 1, :], c_ctx.rearrange("(p k) -> p k", k=NK)).then_inc(d_mod, 16)
            sp.dma_start(adab[:, :], ada_b[0:1, 0:2048].to_broadcast([2, 2048])).then_inc(d_mod, 16)
            for n in range(SLOTS):
                sp.dma_start(wslot[n], ada_w[0, :, n * HALF:(n + 1) * HALF].rearrange(
                    "(p k) n -> p k n", k=NK)).then_inc(w_full[n], 16)
            for t in range(NTC):
                sp.dma_start(xbuf[0][:, t, :], ctx_in[0, t * P:(t + 1) * P, :]).then_inc(d_x[0], 16)
            for g in (1, 2):
                for t in range(4):
                    i = 4 * (g - 1) + t
                    sp.dma_start(xbuf[g][:, t, :], x[0, i * P:(i + 1) * P, :]).then_inc(d_x[g], 16)
            sp.dma_start(mask_raw, masks_in).then_inc(d_mask, 16)
            sp.dma_start(gnorm[:], hgrn_gnorm_w.rearrange("o n -> n o")).then_inc(d_row, 16)
            for i, st in enumerate(UNITS_Z):
                if i >= Z_RAW:
                    sp.wait_ge(z_lo_done, i - Z_RAW + 1)
                else:
                    sp.wait_ge(*G.filled(("ada_cols", SLOTS - 1)))
                if st[0] == "z":
                    _, name, h, kh = st
                    c0 = COL[name] + h * HD
                    src = w_in[0, kh * HALF:(kh + 1) * HALF, c0:c0 + HD].rearrange("(k p) n -> p k n", p=P)
                else:
                    _, name, k = st
                    src = w_in[0, k * P:(k + 1) * P, COL[name]:COL[name] + HALF].rearrange("p (k n) -> p k n", k=4)
                sp.dma_start(raw_z[i % Z_RAW], src).then_inc(z_full[i % Z_RAW], 16)
                t = i - 4
                if 0 <= t < NT:
                    sp.wait_ge(zero_ready, 1)
                    sp.dma_start(moe_dram[t * P:(t + 1) * P, :], zero).then_inc(d_zero, 16)
                if st == ("wide", "v", 1):
                    sp.wait_ge(*S2.filled(("out", H - 1, 1)))
                    sp.dma_start(snorm, sgu_norm_w.rearrange("a g n -> a (g n)").to_broadcast([P, 4 * P])).then_inc(d_late, 16)
                    sp.dma_start(cdft, channel_dft).then_inc(d_late, 16)
                    sp.dma_start(tdft, token_dft.rearrange("(t p) n -> p t n", p=P)).then_inc(d_tab, 16)
            sp.wait_ge(o_ready, 4)
            sp.wait_ge(*S2.filled(("o_turn", H - 1, 1)))
            sp.dma_start(wsraw, sgu_w[0].rearrange("g p q -> p g q")).then_inc(d_ws, 16)
            sp.wait_ge(*G.filled(("dft", 3, 1)))
            sp.dma_start(bias_row, sgu_b.rearrange("a g q -> a (g q)").to_broadcast([P, HALF]).rearrange("p (g q) -> p g q", g=4)).then_inc(d_bias, 16)
            sp.wait_ge(*G.filled(("dft2", 3, 1)))
            for i in range(MERGE_UNITS):
                if i >= RING:
                    sp.wait_ge(m_lo_done, i - RING + 1)
                sp.dma_start(raw_m[i % RING], merge_unit(i)).then_inc(m_full[i % RING], 16)
                if i % 3 or i // 3 - 1 not in ADA_AT:
                    continue
                part = ADA_AT[i // 3 - 1]
                if part:
                    sp.wait_ge(ada_added, part)
                else:
                    sp.wait_ge(ob_done, 8)
                n, kh = part // 2, part % 2
                c0 = 2048 + n * HALF
                src = ada_w[0, :, c0:c0 + HALF].rearrange("(p k) n -> p k n", k=NK)
                sp.dma_start(ada_part, src[:, 4 * kh:4 * kh + 4, :]).then_inc(d_ada, 16)
                if kh:
                    if n:
                        sp.wait_ge(rows_done, n)
                    nw, r0 = (1, 1, 2, 3)[n // 2], n % 2 * HALF
                    sp.dma_start(ada_bias, ada_b[0:1, c0:c0 + HALF].to_broadcast([P, HALF])).then_inc(d_rows, 16)
                    sp.dma_start(norm_row, norm_w[0, nw:nw + 1, r0:r0 + HALF].to_broadcast([P, HALF])).then_inc(d_rows, 16)
            for u in range(4):
                if u == 0:
                    sp.wait_ge(*G.filled(("branch", 2 * NK - 1, 1)))
                elif u == 2:
                    sp.wait_ge(ada_added, 16)
                elif u == 3:
                    sp.wait_ge(*G.filled(("branch", len(MERGE) - 1, 1)))
                n, kh = u // 2, u % 2
                sp.dma_start(out_raw[u], w_out[0, kh * HALF:(kh + 1) * HALF, n * HALF:(n + 1) * HALF].rearrange(
                    "(k p) n -> p k n", p=P)).then_inc(d_out_w[u], 16)
            sp.wait_ge(*G.filled(("ada_rows", 7)))
            sp.dma_start(rw, router_w[0].rearrange("(k p) e -> p k e", p=P)).then_inc(d_row, 16)
            for t in range(NT):
                if t >= 2:
                    sp.wait_ge(x1_done, t - 1)
                sp.dma_start(xre[t % 2], x[0, t * P:(t + 1) * P, :]).then_inc(d_xre[t % 2], 16)
                if t >= 1:
                    sp.wait_ge(h2_done, t)
                    sp.dma_start(x1_dram[(t - 1) * P:t * P, :], x1[:, t - 1, :]).then_inc(x1_stored, 16)
                    sp.dma_start(h2_dram[(t - 1) * P:t * P, :], ybuf[(t - 1) % 2]).then_inc(d_h2[(t - 1) % 2], 16)
            sp.wait_ge(h2_done, NT)
            sp.dma_start(x1_dram[(NT - 1) * P:NT * P, :], x1[:, NT - 1, :]).then_inc(x1_stored, 16)
            sp.dma_start(h2_dram[(NT - 1) * P:NT * P, :], ybuf[(NT - 1) % 2]).then_inc(d_h2[(NT - 1) % 2], 16)

            def expert_unit(e, u):
                if u < 8:
                    c0 = (u // 2 % 2) * D + (u // 4) * HALF
                    src, k0 = exp_w13[0, e, :, c0:c0 + HALF], u % 2 * 4
                else:
                    c0 = u % 2 * HALF
                    src, k0 = exp_w2[0, e, :, c0:c0 + HALF], (u - 8) // 2 * 4
                sp.dma_start(raw[u % RAW], src[k0 * P:(k0 + 4) * P, :].rearrange("(k p) n -> p k n", p=P)).then_inc(raw_full[u % RAW], 16)

            sp.wait_ge(*G.filled(("y", NT - 1, 1)))
            for u in range(UNITS):
                if u >= RAW:
                    sp.wait_ge(*lo_done(0, u - RAW))
                expert_unit(0, u)
            with sp.Fori(0, NE - 1) as e:
                for u in range(UNITS):
                    sp.wait_ge(*(lo_done(e, u + UNITS - RAW) if u < RAW else lo_done(e + 1, u - RAW)))
                    expert_unit(e + 1, u)
            for u in range(UNITS - RAW, UNITS):
                sp.wait_ge(*lo_done(NE - 1, u))
            sp.wait_ge(x1_stored, 16 * NT)
            sp.dma_start(x1_again, x1_dram.rearrange("(t p) n -> p t n", p=P)).then_inc(x1_back, 16)
            sp.wait_ge(sc_done, 16 * NE)
            for t in range(NT):
                sp.dma_start(fin[t], moe_dram[t * P:(t + 1) * P, :]).then_inc(d_fins[t], 16)
            for t in range(NT):
                sp.wait_ge(f_out[t % 2], t // 2 + 1)
                sp.dma_start(out[0, t * P:(t + 1) * P, :], fin[t]).then_inc(d_out, 16)
            sp.wait_ge(d_out, 16 * NT)
            sp.wait_ge(d_zero, 16 * NT)
            for j in range(2):
                sp.wait_ge(d_h2[j], 8 * NT)

        @block.tensor
        def _(pe):
            def claim(stream, key):
                if stream.reuses(key):
                    pe.wait_ge(*stream.last_drained(key))
                return stream.bank(key)

            def turn(dst, src, n=P):
                return nc.tensor.transpose(dst, src, ident[0:n, 0:n])

            pe.wait_ge(ident_ready, 2)
            for st in STEPS:
                kind = st[0]
                if kind == "small":
                    bank = claim(G, st)
                    pe.wait_ge(d_small, 32)
                    turn(bank[:, 0:16], small[:], 16).then_inc(G.full, 1)
                elif kind == "ada_cols":
                    w = wslot[st[1]]
                    pe.wait_ge(w_full[st[1]], 16)
                    bank = claim(G, st)
                    pe.wait_ge(csilu_ready, 2)
                    for k in range(NK):
                        mm = nc.tensor.matmul(bank[0:2, :], csilu[:, :, k], w[:, k, :], start=(k == 0), stop=(k == NK - 1))
                    mm.then_inc(G.full, 1)
                elif kind == "ada_turn":
                    bank = claim(G, st)
                    pe.wait_ge(*G.drained(("ada_cols", 3)))
                    for m in range(16):
                        mm = turn(bank[:, 2 * m:2 * m + 2], adar[:, m * P:(m + 1) * P], 2)
                    mm.then_inc(G.full, 1)
                elif kind == "norm_x":
                    g = st[1]
                    nt = NTC if g == 0 else 4
                    pe.wait_ge(x_normed, g + 1)
                    for k in range(NK):
                        bank = claim(G, st + (k,))
                        for t in range(nt):
                            mm = turn(bank[:, t * P:(t + 1) * P], xbuf[g][:, t, k * P:(k + 1) * P])
                        mm.then_inc(G.full, 1)
                elif kind == "z":
                    _, name, h, kh = st
                    u = z_index[st] % Z_PAIRS
                    pe.wait_ge(z_lo_done, z_index[st] + 1)
                    for j, key in enumerate(z_jobs(st)):
                        bank = G.bank(key) if kh else claim(G, key)
                        if z_index[st] == 0:
                            pe.wait_ge(h_lo_done, (4, 8, 10)[j])
                        xh, xl = (h_hi, h_lo) if j < 2 else (hc_hi, hc_lo)
                        base, width = (j * HALF, HALF) if j < 2 else (0, TC)
                        cut = slice(base, base + width)
                        for k in range(4):
                            kx = 4 * kh + k
                            w_hi, w_lo = wz_hi[u][:, k, :], wz_lo[u][:, k, :]
                            nc.tensor.matmul(bank[:, 0:width], w_hi, xh[:, kx, cut], start=(kx == 0), stop=False)
                            nc.tensor.matmul(bank[:, 0:width], w_hi, xl[:, kx, cut], start=False, stop=False)
                            mm = nc.tensor.matmul(bank[:, 0:width], w_lo, xh[:, kx, cut], start=False, stop=(kx == NK - 1))
                        if kh:
                            mm.then_inc(G.full, 1)
                    if not kh:
                        mm.then_inc(z_used, 1)
                elif kind == "v_turn":
                    h = st[1]
                    for j in range(3):
                        bank = claim(G, st + (j,))
                        pe.wait_ge(*G.drained(("zj", "i", h, j)))
                        src, t0, n = (V[h % 2], 4 * j, 4) if j < 2 else (Vc, 0, NTC)
                        for t in range(n):
                            mm = turn(bank[:, t * P:(t + 1) * P], src[:, t0 + t, :])
                        mm.then_inc(G.full, 1)
                elif kind == "wide":
                    _, name, k = st
                    u = z_index[st] % Z_PAIRS
                    pe.wait_ge(z_lo_done, z_index[st] + 1)
                    b_hi, b_lo = (x[u].rearrange("p k n -> p (k n)") for x in (wz_hi, wz_lo))
                    for t in range(NT):
                        stream, key = wide_stream(t), ("wj", name, t)
                        bank = stream.bank(key) if k else claim(stream, key)
                        a_hi, a_lo = h_hi[:, k, t * P:(t + 1) * P], h_lo[:, k, t * P:(t + 1) * P]
                        nc.tensor.matmul(bank[:], a_hi, b_hi, start=(k == 0), stop=False)
                        nc.tensor.matmul(bank[:], a_hi, b_lo, start=False, stop=False)
                        mm = nc.tensor.matmul(bank[:], a_lo, b_hi, start=False, stop=(k == NK - 1))
                        if k == NK - 1:
                            mm.then_inc(stream.full, 1)
                    if k < NK - 1:
                        mm.then_inc(z_used, 1)
                elif kind == "level":
                    _, h, l = st
                    B = hb[h % 2]
                    for j in range(2):
                        pe.wait_ge(x_ready, x_at(h, max(l - 1, 0), j))
                        bank = claim(L, st + (j,))
                        for cc in range(4):
                            ch = 4 * j + cc
                            if l == 0:
                                mm = nc.tensor.matmul(bank[:, cc * P:(cc + 1) * P], U[:, ch * P:(ch + 1) * P],
                                                      B["A"][:, ch, :], start=True, stop=True)
                                continue
                            m = 1 << (l - 1)
                            o = bank[:, cc * P:(cc + 1) * P].rearrange("p (b two m) -> p b two m", two=2, m=m)
                            qf = B["X1"][:, ch, 0, :].rearrange("p (b two m) -> p b two m", two=2, m=m)
                            qb = B["X2"][:, ch, 1, :].rearrange("p (b two m) -> p b two m", two=2, m=m)
                            nc.tensor.matmul(o[:, :, 1, :], B["X2"][:, ch, 0, :], qf[:, :, 1, :], start=True, stop=True)
                            mm = nc.tensor.matmul(o[:, :, 0, :], B["X1"][:, ch, 1, :], qb[:, :, 0, :], start=True, stop=True)
                        mm.then_inc(L.full, 1)
                elif kind == "ctx_turn":
                    bank = claim(S2, st)
                    pe.wait_ge(ctx_done, st[1] + 1)
                    for a in range(2):
                        for t in range(NTC):
                            mm = turn(bank[:, (2 * a + t) * P:(2 * a + t + 1) * P], Kc[:, a, t * P:(t + 1) * P])
                    mm.then_inc(S2.full, 1)
                elif kind == "ctx_state":
                    h = st[1]
                    bank = claim(S2, st)
                    pe.wait_ge(*S2.drained(("ctx_turn", h)))
                    for a in range(2):
                        for t in range(NTC):
                            mm = nc.tensor.matmul(bank[:, a * P:(a + 1) * P], KcT[:, 2 * a + t, :],
                                                  Vc[:, t, :], start=(t == 0), stop=(t == NTC - 1))
                    mm.then_inc(S2.full, 1)
                elif kind == "k_turn":
                    h = st[1]
                    B = hb[h % 2]
                    pe.wait_ge(x_ready, x_at(h, LEVELS, 1))
                    for j in range(4):
                        bank = claim(S2, st + (j,))
                        src = B["X2"] if j < 2 else B["X1"]
                        for cc in range(4):
                            mm = turn(bank[:, cc * P:(cc + 1) * P], src[:, 4 * (j % 2) + cc, j // 2, :])
                        mm.then_inc(S2.full, 1)
                elif kind == "kv":
                    h = st[1]
                    for j in range(4):
                        bank = claim(S2, st + (j,))
                        if j == 0:
                            pe.wait_ge(*S2.drained(("k_turn", h, 3)))
                        a = j % 2
                        for i in range(4 if j < 2 else 3):
                            ch = 4 * (j // 2) + i if a == 0 else 7 - 4 * (j // 2) - i
                            mm = nc.tensor.matmul(bank[:, i * P:(i + 1) * P], KT[:, a, ch, :],
                                                  V[h % 2][:, ch, :], start=True, stop=True)
                        mm.then_inc(S2.full, 1)
                elif kind == "out":
                    h = st[1]
                    B = hb[h % 2]
                    pe.wait_ge(s_ready, h + 1)
                    for j in range(2):
                        bank = claim(S2, st + (j,))
                        for cc in range(4):
                            ch = 4 * j + cc
                            o = bank[:, cc * P:(cc + 1) * P]
                            nc.tensor.matmul(o, B["A"][:, ch, :], V[h % 2][:, ch, :], start=True, stop=False)
                            nc.tensor.matmul(o, B["X1"][:, ch, 0, :], S[:, 0, ch, :], start=False, stop=False)
                            mm = nc.tensor.matmul(o, B["X2"][:, ch, 1, :], S[:, 1, ch, :], start=False, stop=True)
                        mm.then_inc(S2.full, 1)
                elif kind == "o_turn":
                    h = st[1]
                    pe.wait_ge(o_ready, h + 1)
                    for j in range(2):
                        bank = claim(S2, st + (j,))
                        for cc in range(4):
                            mm = turn(bank[:, cc * P:(cc + 1) * P], o_sb[:, 4 * j + cc, :])
                        mm.then_inc(S2.full, 1)
                elif kind == "dft":
                    _, g, par = st
                    bank = claim(G, st)
                    if (g, par) == (0, 0):
                        pe.wait_ge(fold_done, 2)
                        pe.wait_ge(d_tab, 16)
                    for t in range(4):
                        mm = nc.tensor.matmul(bank[:], zfold[par][:, t, g * P:(g + 1) * P],
                                              tdft[:, t, par * HALF:(par + 1) * HALF], start=(t == 0), stop=(t == 3))
                    mm.then_inc(G.full, 1)
                elif kind == "dft2":
                    _, g, par = st
                    bank = claim(G, st)
                    pe.wait_ge(*G.drained(("dft", g, par)))
                    n = 257 - par
                    pe.wait_ge(d_late, 32)
                    nc.tensor.matmul(bank[:, 0:n], cdft[:, 0:HD], AB[:, g, par, 0:n], start=True, stop=True)
                    nc.tensor.matmul(bank[:, n:HALF], cdft[:, HD:], AB[:, g, par, n:HALF], start=True,
                                     stop=True).then_inc(G.full, 1)
                elif kind == "mix":
                    _, g, j = st
                    if (g, j) == (0, 0):
                        pe.wait_ge(d_ws, 16)
                        pe.wait_ge(*L.drained(("wj", "v", 4)))
                        for gg in range(4):
                            mm = turn(banks[4][:, gg * P:(gg + 1) * P], wsraw[:, gg, :])
                        mm.then_inc(ws_t, 1)
                        pe.wait_ge(vv_done, 1)
                        pe.wait_ge(ws_t, 2)
                    bank = claim(G, st)
                    for t in range(4):
                        mm = nc.tensor.matmul(bank[:, t * P:(t + 1) * P], vg[:, 4 * j + t, g * P:(g + 1) * P], wsT[:, g, :],
                                              start=True, stop=True)
                    mm.then_inc(G.full, 1)
                elif kind == "merge":
                    q = st[1]
                    b = MERGE[q][0]
                    for part in range(3):
                        i = 3 * q + part
                        if part == 2 and MERGE[q][1] == 0:
                            pe.wait_ge(o_lo_done, 4 * (q // NK + 1))
                        pe.wait_ge(m_lo_done, i + 1)
                        for j in range(2):
                            key = ("branch" if part == 2 else "gate", q, j)
                            bank = G.bank(key) if part == 1 else claim(G, key)
                            xh, xl = (h_hi, h_lo) if part < 2 else (o_hi, o_lo[b])
                            for k in range(4):
                                kx = 4 * part + k if part < 2 else k
                                first, last = part != 1 and k == 0, part and k == 3
                                cut = slice(j * HALF, (j + 1) * HALF)
                                wh, wl = wm_hi[i % RING][:, k, :], wm_lo[i % RING][:, k, :]
                                nc.tensor.matmul(bank[:], wh, xh[:, kx, cut], start=first, stop=False)
                                nc.tensor.matmul(bank[:], wh, xl[:, kx, cut], start=False, stop=False)
                                mm = nc.tensor.matmul(bank[:], wl, xh[:, kx, cut], start=False, stop=bool(last))
                            if part:
                                mm.then_inc(G.full, 1)
                            elif j:
                                mm.then_inc(m_used, 1)
                elif kind == "ada_rows":
                    n = st[1]
                    bank = claim(G, st)
                    pe.wait_ge(ones_ready, 1)
                    pe.wait_ge(ada_summed, n + 1)
                    nc.tensor.matmul(bank[:], ones[:], rows[:, n // 2, n % 2 * HALF:(n % 2 + 1) * HALF],
                                     start=True, stop=True).then_inc(G.full, 1)
                elif kind == "y":
                    t = st[1]
                    pe.wait_ge(mt_lo_done, t + 1)
                    for n in range(2):
                        bank = claim(G, st + (n,))
                        for k in range(NK):
                            if t == 0 and k % 4 == 0:
                                pe.wait_ge(out_lo_done, 2 * n + k // 4 + 1)
                            hi, lo = mt_hi[:, t % 2, k, :], mt_lo[:, t % 2, k, :]
                            nc.tensor.matmul(bank[:], hi, out_hi[:, n, k, :], start=(k == 0), stop=False)
                            nc.tensor.matmul(bank[:], hi, out_lo[:, n, k, :], start=False, stop=False)
                            mm = nc.tensor.matmul(bank[:], lo, out_hi[:, n, k, :], start=False, stop=(k == NK - 1))
                        mm.then_inc(G.full, 1)
                elif kind == "h2_turn":
                    t = st[1]
                    pe.wait_ge(h2_done, t + 1)
                    for j in range(2):
                        bank = claim(G, st + (j,))
                        for k in range(4):
                            mm = turn(bank[:, k * P:(k + 1) * P], ybuf[t % 2][:, (4 * j + k) * P:(4 * j + k + 1) * P])
                        mm.then_inc(G.full, 1)
                elif kind == "logits":
                    t = st[1]
                    for j in range(2):
                        pe.wait_ge(*G.drained(("h2_turn", t, j)))
                    if t == 0:
                        pe.wait_ge(d_row, 32)
                    for k in range(NK):
                        mm = nc.tensor.matmul(banks[4][:, t * NE:(t + 1) * NE], h2T[:, k, t * P:(t + 1) * P], rw[:, k, :],
                                              start=(k == 0), stop=(k == NK - 1))
                    mm.then_inc(logits_done, 1)
                elif kind == "router_turn":
                    pe.wait_ge(r_prob, 1)
                    for j in range(2):
                        bank = claim(G, st + (j,))
                        for t in range(4):
                            mm = turn(bank[0:NE, t * P:(t + 1) * P], prob[:, 4 * j + t, :])
                        mm.then_inc(G.full, 1)
                elif kind == "choose_turn":
                    pe.wait_ge(chosen, 1)
                    for j, src in enumerate((topv, topf)):
                        bank = claim(G, st + (j,))
                        turn(bank[:, 0:NE], src, NE).then_inc(G.full, 1)

            pe.wait_ge(*S2.drained(("o_turn", H - 1, 1)))

            def turn_gathered(n, j):
                if j == 0:
                    pe.wait_ge(xg_full, n * 16 + 16)
                else:
                    pe.wait_ge(tx_hi, n * 2 + 1)
                    pe.wait_ge(tx_lo, n * 2 + 1)
                for k in range(4):
                    mm = turn(banks[4][:, k * P:(k + 1) * P], xg[:, (4 * j + k) * P:(4 * j + k + 1) * P])
                mm.then_inc(tx_full, 1)

            def turn_hidden(e, j):
                pe.wait_ge(b_drained, e * 2 + (j + 1))
                if j:
                    pe.wait_ge(th_hi, e * 2 + 1)
                    pe.wait_ge(th_lo, e * 2 + 1)
                for k in range(4):
                    mm = turn(banks[6][:, k * P:(k + 1) * P], hid[:, (4 * j + k) * P:(4 * j + k + 1) * P])
                mm.then_inc(th_full, 1)

            def unit(e, u):
                if u < 8:
                    bank, k0, stop_at, hi, lo = banks[u // 2], u % 2 * 4, 1, xe_hi, xe_lo
                    if u < 2:
                        pe.wait_ge(tx_hi, e * 2 + (u + 1))
                        pe.wait_ge(tx_lo, e * 2 + (u + 1))
                else:
                    bank, k0, hi, lo = banks[7 if u % 2 == 0 else 5], (u - 8) // 2 * 4, ht_hi, ht_lo
                    if u in (8, 10):
                        pe.wait_ge(th_hi, e * 2 + (u // 2 - 3))
                        pe.wait_ge(th_lo, e * 2 + (u // 2 - 3))
                    if u in (8, 9):
                        pe.wait_ge(y_drained, e * 2 + 2)
                pe.wait_ge(*lo_done(e, u))
                for k in range(4):
                    first, last = k0 == 0 and k == 0, k0 == 4 and k == 3
                    nc.tensor.matmul(bank[:], hi[:, k0 + k, :], whi[u % PAIRS][:, k, :], start=first, stop=False)
                    nc.tensor.matmul(bank[:], hi[:, k0 + k, :], wlo[u % PAIRS][:, k, :], start=False, stop=False)
                    mm = nc.tensor.matmul(bank[:], lo[:, k0 + k, :], whi[u % PAIRS][:, k, :], start=False, stop=last)
                mm.then_inc(used, 1)

            def expert(e, last):
                for u in range(6):
                    unit(e, u)
                turn_hidden(e, 0)
                for u in (6, 7, 8):
                    unit(e, u)
                if not last:
                    turn_gathered(e + 1, 0)
                turn_hidden(e, 1)
                unit(e, 9)
                if not last:
                    turn_gathered(e + 1, 1)
                unit(e, 10)
                unit(e, 11)

            turn_gathered(0, 0)
            turn_gathered(0, 1)
            with pe.Fori(0, NE - 1) as e:
                expert(e, False)
            expert(NE - 1, True)

        @block.scalar
        def _(act):
            def take(stream, key):
                act.wait_ge(*stream.filled(key))
                return stream.bank(key)

            def split_z(i):
                if i < len(UNITS_Z):
                    act.wait_ge(z_full[i % Z_RAW], 16 * (i // Z_RAW + 1))
                    if i >= Z_PAIRS:
                        act.wait_ge(*z_unit_used(i - Z_PAIRS))
                    nc.scalar.copy(wz_hi[i % Z_PAIRS], raw_z[i % Z_RAW]).then_inc(z_hi_done, 1)

            def split_unit(i):
                if i < MERGE_UNITS:
                    act.wait_ge(m_full[i % RING], 16 * (i // RING + 1))
                    if i >= RING:
                        act.wait_ge(*unit_used(i - RING))
                    nc.scalar.copy(wm_hi[i % RING], raw_m[i % RING]).then_inc(m_hi_done, 1)

            act.wait_ge(d_mod, 48)
            for j in range(2):
                nc.scalar.activation(csilu[:, j, :], craw[:, j, :], ACT.Silu).then_inc(csilu_ready, 1)
            for st in STEPS:
                kind = st[0]
                if kind == "small":
                    act.wait_ge(lb_max, 1)
                    nc.scalar.activation(lb[:, 1, :], lb[:, 0, :], ACT.Exp).then_inc(lb_ready, 1)
                elif kind == "norm_s":
                    g = st[1]
                    nt = NTC if g == 0 else 4
                    act.wait_ge(d_x[g], 16 * nt)
                    for t in range(nt):
                        nc.scalar.activation(o_sb[:].rearrange("p a b -> p (a b)"), xbuf[g][:, t, :], ACT.Square,
                                             scale=1.0 / math.sqrt(D), accum_out=ss[:, 4 * g + t:4 * g + t + 1]).then_inc(x_ss, 1)
                        act.wait_ge(x_ss, (0, 2, 6)[g] + t + 1)
                elif kind == "norm_x":
                    g = st[1]
                    act.wait_ge(*G.drained(("ada_turn",)))
                    for k in range(1, NK, 2):
                        bank = take(G, st + (k,))
                        dst = hcT[:, k, :] if g == 0 else hT[:, k, (g - 1) * HALF:g * HALF]
                        w = TC if g == 0 else HALF
                        j = 1 if g == 0 else 0
                        nc.scalar.activation(dst, bank[:, 0:w], ACT.Identity, bias=shift1[:, k, j:j + 1],
                                             scale=scale1[:, k, j:j + 1]).then_inc(G.freed(st + (k,)), 1)
                elif kind == "z":
                    _, name, h, kh = st
                    if z_index[st] == 0:
                        split_z(0)
                        split_z(1)
                    split_z(z_index[st] + 2)
                    if kh == 0:
                        continue
                    B = hb[h % 2]
                    for j, key in enumerate(z_jobs(st)):
                        bank = take(G, key)
                        if j < 2:
                            src, cut = bank[:].rearrange("p (c t) -> p c t", c=4), slice(4 * j, 4 * j + 4)
                        else:
                            src, cut = bank[:, 0:TC].rearrange("p (c t) -> p c t", c=2), slice(0, 2)
                        if name == "i":
                            nc.scalar.copy((V[h % 2] if j < 2 else Vc)[:, cut, :], src).then_inc(G.freed(key), 1)
                        elif name == "q":
                            nc.scalar.activation(B["A"][:, cut, :], src, ACT.Silu).then_inc(G.freed(key), 1)
                        elif name == "ga":
                            nc.scalar.activation(oaT[:, h, j * HALF:(j + 1) * HALF], bank[:], ACT.Silu).then_inc(G.freed(key), 1)
                        elif name == "u":
                            nc.scalar.activation(uT[:, h, j * HALF:(j + 1) * HALF], bank[:], ACT.Gelu).then_inc(G.freed(key), 1)
                        else:
                            a = 0 if name == "ff" else 1
                            if j < 2:
                                f = B["F"].rearrange("p (c a t) -> p c a t", c=NT, a=2)[:, cut, a, :]
                                kk = (B["X2"], B["X1"])[a][:, cut, a, :]
                            else:
                                src, f, kk = bank[:, 0:TC], Fc[:, 0, a, :], Kc[:, a, :]
                                if h:
                                    act.wait_ge(*S2.filled(("ctx_turn", h - 1)))
                            nc.scalar.activation(f, src, ACT.Sigmoid)
                            nc.scalar.activation(kk, src, ACT.Sigmoid, scale=-1.0).then_inc(G.freed(key), 1)
                elif kind == "v_turn":
                    h = st[1]
                    for j in range(3):
                        bank = take(G, st + (j,))
                        dst = V[h % 2][:, 4 * j:4 * j + 4, :] if j < 2 else Vc
                        nc.scalar.copy(dst, bank[:, 0:HALF if j < 2 else TC].rearrange("p (c t) -> p c t", t=P)).then_inc(G.freed(st + (j,)), 1)
                elif kind == "wide":
                    _, name, k = st
                    split_z(z_index[st] + 2)
                    if k == NK - 1:
                        if name == "v":
                            act.wait_ge(fold_done, 2)
                        for t in range(NT):
                            stream, key = wide_stream(t), ("wj", name, t)
                            bank = take(stream, key)
                            if name == "v":
                                nc.scalar.activation(vg[:, t, :], bank[:], ACT.Gelu).then_inc(stream.freed(key), 1)
                            else:
                                nc.scalar.copy(zb[:, t, :], bank[:]).then_inc(stream.freed(key), 1)
                elif kind == "level" and st[2] == 0:
                    for j in range(2):
                        bank = take(L, st + (j,))
                        nc.scalar.copy(hb[st[1] % 2]["A"][:, 4 * j:4 * j + 4, :],
                                       bank[:].rearrange("p (c t) -> p c t", c=4)).then_inc(L.freed(st + (j,)), 1)
                elif kind == "ctx_turn":
                    bank = take(S2, st)
                    nc.scalar.copy(KcT, bank[:].rearrange("p (c t) -> p c t", c=4)).then_inc(S2.freed(st), 1)
                elif kind == "ctx_state":
                    h = st[1]
                    bank = take(S2, st)
                    nc.scalar.copy(S[:, 0, 0, :], bank[:, 0:P])
                    nc.scalar.copy(S[:, 1, NT - 1, :], bank[:, P:2 * P]).then_inc(S2.freed(st), 1)
                elif kind == "k_turn":
                    if st[1] == 0:
                        act.wait_ge(d_zero, 16 * NT)
                    for j in range(4):
                        bank = take(S2, st + (j,))
                        nc.scalar.copy(KT[:, j // 2, 4 * (j % 2):4 * (j % 2) + 4, :],
                                       bank[:].rearrange("p (c t) -> p c t", c=4)).then_inc(S2.freed(st + (j,)), 1)
                elif kind == "out":
                    h = st[1]
                    for j in range(2):
                        bank = take(S2, st + (j,))
                        src = bank[:].rearrange("p (c t) -> p c t", c=4)
                        if j == 0 and h:
                            act.wait_ge(*S2.filled(("o_turn", h - 1, 1)))
                        nc.scalar.copy(o_sb[:, 4 * j:4 * j + 4, :], src)
                        nc.scalar.activation(o_sq[:, 4 * j:4 * j + 4, :], src, ACT.Square,
                                             scale=1.0 / math.sqrt(HD)).then_inc(S2.freed(st + (j,)), 1)
                elif kind == "vv_norm":
                    wide_waits(act, "v")
                    for j in range(4):
                        if j >= 2:
                            act.wait_ge(v_sq, j - 1)
                        sq = big[:, 1024 * (j % 2):1024 * (j % 2 + 1)].rearrange("p (t n) -> p t n", t=2)
                        nc.scalar.activation(sq, vg[:, 2 * j:2 * j + 2, :], ACT.Square,
                                             scale=1.0 / math.sqrt(P)).then_inc(vv_sq_ready, 1)
                elif kind == "dft":
                    _, g, par = st
                    bank = take(G, st)
                    nc.scalar.copy(AB[:, g, par, :], bank[:]).then_inc(G.freed(st), 1)
                elif kind == "dft2":
                    _, g, par = st
                    n = 2 * g + par
                    bank = take(G, st)
                    if n >= 2:
                        act.wait_ge(ob_done, n - 1)
                    nc.scalar.copy(pq[n % 2], bank[:]).then_inc(G.freed(st), 1)
                elif kind == "mix" and st[1:] == (0, 0):
                    act.wait_ge(ws_t, 1)
                    nc.scalar.copy(wsT, banks[4][:].rearrange("p (c t) -> p c t", c=4)).then_inc(ws_t, 1)
                elif kind == "h_split":
                    for kk in range(2):
                        act.wait_ge(*G.drained(("norm_x", st[1], NK - 2 + kk)))
                    for src, hi, _ in split_parts(st[1]):
                        nc.scalar.copy(hi, src).then_inc(h_hi_done, 1)
                elif kind == "o_split":
                    _, b, g = st
                    if b == 0 and g == 0:
                        act.wait_ge(v_sq, 4)
                        act.wait_ge(*S2.drained(("o_turn", H - 1, 1)))
                    elif g == 0:
                        act.wait_ge(*G.filled(("branch", b * NK - 1, 1)))
                        if b == 1:
                            act.wait_ge(ob_done, 8)
                        else:
                            act.wait_ge(*G.drained(("mix", 3, 1)))
                    nc.scalar.copy(o_hi[:, g, :], (oaT, obT, ocT)[b][:, g, :]).then_inc(o_hi_done, 1)
                elif kind == "merge":
                    q = st[1]
                    if q == 0:
                        act.wait_ge(*G.drained(("mix", 3, 1)))
                        for i in range(4):
                            split_unit(i)
                    split_unit(3 * q + 4)
                    for j in range(2):
                        key = ("gate", q, j)
                        bank = take(G, key)
                        if q:
                            act.wait_ge(*G.drained(("branch", q - 1, j)))
                        nc.scalar.activation(sig[j], bank[:], ACT.Sigmoid).then_inc(G.freed(key), 1)
                    split_unit(3 * q + 5)
                    split_unit(3 * q + 6)
                elif kind == "out_split":
                    u = st[1]
                    act.wait_ge(d_out_w[u], 16)
                    if u == 0:
                        act.wait_ge(*G.filled(("gate", len(MERGE) - 1, 1)))
                    nc.scalar.copy(out_hi[:, u // 2, u % 2 * 4:u % 2 * 4 + 4, :], out_raw[u]).then_inc(out_hi_done, 1)
                elif kind == "m_split":
                    t = st[1]
                    if t == 0:
                        act.wait_ge(merged_done, 4 * NK)
                        act.wait_ge(*G.filled(("branch", len(MERGE) - 1, 1)))
                    elif t >= 2:
                        act.wait_ge(*G.filled(("y", t - 2, 1)))
                    nc.scalar.copy(mt_hi[:, t % 2], mT[:, :, t * P:(t + 1) * P]).then_inc(mt_hi_done, 1)
                elif kind == "y_norm":
                    t = st[1]
                    for n in range(2):
                        key = ("y", t, n)
                        bank = take(G, key)
                        if t >= 2 and n == 0:
                            act.wait_ge(d_h2[t % 2], 16 * (t // 2))
                            act.wait_ge(*G.filled(("h2_turn", t - 2, 1)))
                        nc.scalar.copy(ybuf[t % 2][:, n * HALF:(n + 1) * HALF], bank[:]).then_inc(G.freed(key), 1)
                    act.wait_ge(*G.drained(("y", t, 1)))
                    nc.scalar.activation(flat, ybuf[t % 2], ACT.Square, scale=1.0 / math.sqrt(D),
                                         accum_out=ss[:, t:t + 1]).then_inc(y_ss, 1)
                    act.wait_ge(x1_done, t + 1)
                    act.wait_ge(y_ss, t + 1)
                    nc.scalar.activation(flat, x1[:, t, :], ACT.Square, scale=1.0 / math.sqrt(D),
                                         accum_out=ss[:, 8 + t:9 + t]).then_inc(x1_ss, 1)
                    act.wait_ge(x1_ss, t + 1)
                elif kind == "h2_turn":
                    t = st[1]
                    bank = take(G, st + (1,))
                    nc.scalar.copy(h2T[:, 4:8, t * P:(t + 1) * P], bank[:].rearrange("p (k t) -> p k t", k=4)).then_inc(G.freed(st + (1,)), 1)
                elif kind == "router":
                    act.wait_ge(r_sub, 1)
                    nc.scalar.activation(prob, prob, ACT.Exp).then_inc(r_exp, 1)


            def split(e, u):
                act.wait_ge(raw_full[u % RAW], e * (16 * UNITS // RAW) + 16 * (u // RAW + 1))
                if not (isinstance(e, int) and e == 0 and u < PAIRS):
                    act.wait_ge(used, e * UNITS + (u - PAIRS + 1))
                nc.scalar.copy(whi[u % PAIRS], raw[u % RAW]).then_inc(hi_done, 1)

            def gathered(n, j):
                act.wait_ge(tx_full, n * 2 + (j + 1))
                nc.scalar.copy(xe_hi[:, 4 * j:4 * j + 4, :], banks[4][:].rearrange("p (k t) -> p k t", k=4)).then_inc(tx_hi, 1)

            def hidden(e, j):
                act.wait_ge(th_full, e * 2 + (j + 1))
                nc.scalar.copy(ht_hi[:, 4 * j:4 * j + 4, :], banks[6][:].rearrange("p (k t) -> p k t", k=4)).then_inc(th_hi, 1)

            def silu_a(e, j):
                act.wait_ge(used, e * UNITS + (4 * j + 2))
                nc.scalar.activation(sa[j], banks[2 * j][:], ACT.Silu).then_inc(a_drained, 1)

            def result(e, j):
                if j == 0:
                    act.wait_ge(cur_g, e + 1)
                    act.wait_ge(added, e + 1)
                act.wait_ge(used, e * UNITS + (11 + j))
                nc.scalar.activation(yb[:, j * HALF:(j + 1) * HALF], banks[7 - 2 * j][:], ACT.Identity,
                                     scale=gcur[:, 0:1]).then_inc(y_drained, 1)

            def expert(e, before):
                if before is not None:
                    split(e, 0)
                    split(e, 1)
                    gathered(e, 0)
                    hidden(before, 1)
                    split(e, 2)
                    gathered(e, 1)
                    split(e, 3)
                    split(e, 4)
                    result(before, 0)
                    split(e, 5)
                    result(before, 1)
                split(e, 6)
                silu_a(e, 0)
                for u in (7, 8, 9, 10):
                    split(e, u)
                silu_a(e, 1)
                hidden(e, 0)
                split(e, 11)

            act.wait_ge(x1_stored, 16 * NT)
            for u in range(PAIRS):
                split(0, u)
            act.wait_ge(G.sems["act"], G.count["act"])
            act.wait_ge(G.sems["dve"], G.count["dve"])
            act.sem_inc(y_drained, 2)
            gathered(0, 0)
            gathered(0, 1)
            expert(0, None)
            with act.Fori(0, NE - 1) as i:
                expert(i + 1, i)
            hidden(NE - 1, 1)
            result(NE - 1, 0)
            result(NE - 1, 1)
            for t in range(NT):
                act.wait_ge(d_fins[t], 16)
                nc.scalar.activation(o_sb[:].rearrange("p a b -> p (a b)"), fin[t], ACT.Square, scale=1.0 / math.sqrt(D),
                                     accum_out=ss[:, 16 + t:17 + t]).then_inc(f_ss, 1)
                act.wait_ge(f_ss, t + 1)

        @block.vector
        def _(dve):
            def take(stream, key):
                dve.wait_ge(*stream.filled(key))
                return stream.bank(key)

            n = [0]

            def step(ins):
                ins.then_inc(vstep, 1)
                n[0] += 1
                dve.wait_ge(vstep, n[0])

            def split_z(i):
                if i < len(UNITS_Z):
                    dve.wait_ge(z_hi_done, i + 1)
                    nc.vector.tensor_tensor(wz_lo[i % Z_PAIRS], raw_z[i % Z_RAW], wz_hi[i % Z_PAIRS].bitcast(F32),
                                            ALU.subtract).then_inc(z_lo_done, 1)

            def split_unit(i):
                if i < MERGE_UNITS:
                    dve.wait_ge(m_hi_done, i + 1)
                    nc.vector.tensor_tensor(wm_lo[i % RING], raw_m[i % RING], wm_hi[i % RING].bitcast(F32),
                                            ALU.subtract).then_inc(m_lo_done, 1)

            nc.vector.memset(zero, 0.0).then_inc(zero_ready, 1)
            for st in STEPS:
                kind = st[0]
                if kind == "small":
                    step(nc.vector.tensor_copy(cols[:], take(G, st)[:, 0:16]))
                    nc.vector.tensor_copy(lb[:, 3, :], cols[:, 8:16]).then_inc(G.freed(st), 1)
                    dve.wait_ge(G.sems["dve"], 1)
                    nc.vector.tensor_tensor(lb[:, 0, :], lb[:, 3, :], lb[:, 3, :], ALU.subtract).then_inc(lb_max, 1)
                    dve.wait_ge(lb_ready, 1)
                    step(nc.vector.reciprocal(lb[:, 2, :], lb[:, 1, :]))
                    step(nc.vector.tensor_tensor(lb[:, 2, :], lb[:, 2, :], lb[:, 1, :], ALU.mult))
                    step(nc.vector.tensor_tensor(lb[:, 0, :], lb[:, 2, :], lb[:, 2, :], ALU.subtract))
                    nc.vector.tensor_scalar(gate_add[:], lb[:, 0, :], FLOOR, None, ALU.max)
                    step(nc.vector.tensor_scalar(gate_mul[:], lb[:, 0, :], -1.0, 1.0, ALU.mult, ALU.add))
                elif kind == "ada_cols":
                    nn = st[1]
                    bank = take(G, st)
                    dve.wait_ge(d_mod, 48)
                    nc.vector.tensor_tensor(adar[:, nn * HALF:(nn + 1) * HALF], bank[0:2, :],
                                            adab[:, nn * HALF:(nn + 1) * HALF], ALU.add).then_inc(G.freed(st), 1)
                elif kind == "ada_turn":
                    bank = take(G, st)
                    nc.vector.tensor_copy(shift1[:], bank[:, 0:16].rearrange("p (k j) -> p k j", j=2))
                    nc.vector.scalar_tensor_tensor(scale1[:], bank[:, 16:32].rearrange("p (k j) -> p k j", j=2), 1.0,
                                                   cols[:, 0:8].rearrange("p (k o) -> p k o", o=1).to_broadcast([P, NK, 2]), ALU.add, ALU.mult).then_inc(G.freed(st), 1)
                    dve.wait_ge(*G.drained(st))
                elif kind == "norm_s":
                    g = st[1]
                    nt = NTC if g == 0 else 4
                    dve.wait_ge(x_ss, (2, 6, 10)[g])
                    nc.vector.tensor_scalar(ss[:, 16 + 4 * g:16 + 4 * g + nt], ss[:, 4 * g:4 * g + nt], EPS, None, ALU.add).then_inc(x_ms, 1)
                    dve.wait_ge(x_rs, g + 1)
                    for t in range(nt):
                        ins = nc.vector.tensor_scalar(xbuf[g][:, t, :], xbuf[g][:, t, :], rs[:, 4 * g + t:4 * g + t + 1], None, ALU.mult)
                    ins.then_inc(x_normed, 1)
                elif kind == "norm_x":
                    g = st[1]
                    for k in range(0, NK, 2):
                        bank = take(G, st + (k,))
                        dst = hcT[:, k, :] if g == 0 else hT[:, k, (g - 1) * HALF:g * HALF]
                        w = TC if g == 0 else HALF
                        j = 1 if g == 0 else 0
                        nc.vector.tensor_scalar(dst, bank[:, 0:w], scale1[:, k, j:j + 1], shift1[:, k, j:j + 1],
                                                ALU.mult, ALU.add).then_inc(G.freed(st + (k,)), 1)
                elif kind == "prepare":
                    _, h, part = st
                    B = hb[h % 2]
                    F4 = B["F"].rearrange("p (c a t) -> p c a t", c=NT, a=2)
                    if part < 2:
                        a = part
                        dve.wait_ge(*G.drained(("zj", ("ff", "fb")[a], h, 2)))
                        mul, add = gate_mul[:, 4 * a + h:4 * a + h + 1], gate_add[:, 4 * a + h:4 * a + h + 1]
                        kk = (B["X2"], B["X1"])[a][:, :, a, :]
                        nc.vector.tensor_scalar(Fc[:, 0, a, :], Fc[:, 0, a, :], mul, add, ALU.mult, ALU.add)
                        nc.vector.tensor_scalar(Kc[:, a, :], Kc[:, a, :], mul, None, ALU.mult).then_inc(kc_ready, 1)
                        nc.vector.tensor_scalar(F4[:, :, a, :], F4[:, :, a, :], mul, add, ALU.mult, ALU.add)
                        step(nc.vector.tensor_scalar(kk, kk, mul, None, ALU.mult))
                        if a:
                            nc.vector.tensor_tensor(U.rearrange("p (c t) -> p c t", c=NT), B["X2"][:, :, 0, :],
                                                    B["X1"][:, :, 1, :], ALU.add)
                        continue
                    if h == 0:
                        dve.wait_ge(d_mask, 16)
                        step(nc.vector.tensor_copy(masks[:], mask_raw))
                    dve.wait_ge(*G.drained(("zj", "q", h, 1)))
                    nc.vector.tensor_tensor(B["X1"][:, :, 0, :], B["A"], F4[:, :, 0, :], ALU.mult)
                    for j in range(2):
                        cut = slice(4 * j, 4 * j + 4)
                        nc.vector.tensor_tensor(B["X2"][:, cut, 1, :], B["A"][:, cut, :], F4[:, cut, 1, :], ALU.mult).then_inc(x_ready, 1)
                elif kind == "level" and st[2]:
                    _, h, l = st
                    B = hb[h % 2]
                    m = 1 << (l - 1)
                    if l == 1:
                        dve.wait_ge(L.freed(("level", h, 0, 1)), 2 * (h + 1))
                    else:
                        dve.wait_ge(x_ready, x_at(h, l - 1, 1))
                        dve.wait_ge(*L.drained(("level", h, l - 1, 1)))

                    nb = NT * P // (2 * m)
                    src, dst = (B["F"], U) if l % 2 else (U, B["F"])
                    if l == LEVELS:
                        dst = totals
                    for j in range(2):
                        bank = take(L, st + (j,))
                        nc.vector.copy_predicated(B["A"][:, 4 * j:4 * j + 4, :], masks[:, l - 1:l, :].to_broadcast([P, 4, P]),
                                                  bank[:].rearrange("p (c t) -> p c t", c=4)).then_inc(L.freed(st + (j,)), 1)
                        cut = slice(4 * j, 4 * j + 4)
                        pair = src[:, 2 * nb * j:2 * nb * (j + 1)].rearrange("p (b two) -> p b two", two=2)
                        X1 = B["X1"][:, cut].rearrange("p c a t -> p (c a t)").rearrange("p (b two m) -> p b two m", two=2, m=m)
                        X2 = B["X2"][:, cut].rearrange("p c a t -> p (c a t)").rearrange("p (b two m) -> p b two m", two=2, m=m)
                        nc.vector.tensor_tensor(dst[:, nb * j:nb * (j + 1)], pair[:, :, 0], pair[:, :, 1], ALU.mult)
                        nc.vector.tensor_tensor(X1[:, :, 1, :], X1[:, :, 1, :], pair[:, :, 0:1].to_broadcast([P, nb, m]), ALU.mult)
                        nc.vector.tensor_tensor(X2[:, :, 0, :], X2[:, :, 0, :], pair[:, :, 1:2].to_broadcast([P, nb, m]),
                                                ALU.mult).then_inc(x_ready, 1)
                elif kind == "kv":
                    h = st[1]
                    B = hb[h % 2]
                    tot = totals[:].rearrange("p (c a) -> p c a", a=2)
                    dve.wait_ge(x_ready, x_at(h, LEVELS, 1))
                    dve.wait_ge(*S2.drained(("ctx_state", h)))
                    for half in range(2):
                        banks2 = [take(S2, st + (2 * half + a,)) for a in range(2)]
                        for i in range(4 - half):
                            for a in range(2):
                                ch = 4 * half + i if a == 0 else 7 - 4 * half - i
                                nx = ch + 1 if a == 0 else ch - 1
                                ins = nc.vector.scalar_tensor_tensor(S[:, a, nx, :], S[:, a, ch, :], tot[:, ch, a:a + 1],
                                                                     banks2[a][:, i * P:(i + 1) * P], ALU.mult, ALU.add)
                            step(ins)
                        for a in range(2):
                            dve.sem_inc(S2.freed(st + (2 * half + a,)), 1)
                    dve.sem_inc(s_ready, 1)
                elif kind == "out":
                    h = st[1]
                    dve.wait_ge(*S2.drained(("out", h, 1)))
                    step(nc.vector.tensor_reduce(ss[:, 32:40], o_sq, AX.X, ALU.add))
                    nc.vector.tensor_scalar(ss[:, 40:48], ss[:, 32:40], EPS, None, ALU.add).then_inc(o_ms, 1)
                    dve.wait_ge(o_rs, h + 1)
                    nc.vector.tensor_tensor(o_sb[:], o_sb[:], rs[:, 32:40].rearrange("p (c o) -> p c o", o=1).to_broadcast([P, NT, HD]),
                                            ALU.mult).then_inc(o_ready, 1)
                elif kind == "fold":
                    dve.wait_ge(*S2.filled(("out", H - 1, 1)))
                    wide_waits(dve, "zb")
                    nc.vector.tensor_tensor(zfold[0], zb[:, 0:4, :], zb[:, 4:8, :], ALU.add).then_inc(fold_done, 1)
                    nc.vector.tensor_tensor(zfold[1], zb[:, 0:4, :], zb[:, 4:8, :], ALU.subtract).then_inc(fold_done, 1)
                elif kind == "vv_norm":
                    for j in range(4):
                        dve.wait_ge(vv_sq_ready, j + 1)
                        sq = big[:, 1024 * (j % 2):1024 * (j % 2 + 1)].rearrange("p (c t) -> p c t", t=P)
                        nc.vector.tensor_reduce(ss[:, 8 * j:8 * j + 8], sq, AX.X, ALU.add).then_inc(v_sq, 1)
                    dve.wait_ge(v_sq, 4)
                    nc.vector.tensor_scalar(ss[:, 0:32], ss[:, 0:32], EPS, None, ALU.add).then_inc(v_ms, 1)
                    dve.wait_ge(v_rs, 1)
                    v4 = vg.rearrange("p t (g n) -> p (t g) n", g=4)
                    step(nc.vector.tensor_tensor(v4, v4, rs[:, 0:32].rearrange("p (c o) -> p c o", o=1).to_broadcast([P, 32, P]), ALU.mult))
                    dve.wait_ge(d_late, 32)
                    nc.vector.tensor_tensor(vg, vg, snorm.rearrange("p (o n) -> p o n", o=1).to_broadcast([P, NT, 4 * P]), ALU.mult).then_inc(vv_done, 1)
                elif kind == "dft2":
                    _, g, par = st
                    i = 2 * g + par
                    dve.wait_ge(*G.drained(st))
                    b = pq[i % 2]
                    if par == 0:
                        nc.vector.tensor_tensor(obT[:, g, 2:HALF:2], b[:, 1:256], b[:, 257:512], ALU.subtract)
                        nc.vector.tensor_tensor(obT[:, g, T - 2:HALF:-2], b[:, 1:256], b[:, 257:512], ALU.add)
                        nc.vector.tensor_copy(obT[:, g, 0:HALF + 1:HALF], b[:, 0:257:256]).then_inc(ob_done, 1)
                    else:
                        nc.vector.tensor_tensor(obT[:, g, 1:HALF:2], b[:, 0:256], b[:, 256:512], ALU.subtract)
                        nc.vector.tensor_tensor(obT[:, g, T - 1:HALF:-2], b[:, 0:256], b[:, 256:512], ALU.add).then_inc(ob_done, 1)
                elif kind == "mix":
                    _, g, j = st
                    bank = take(G, st)
                    if (g, j) == (0, 0):
                        dve.wait_ge(d_bias, 16)
                    step(nc.vector.tensor_tensor(biased[j], bank[:].rearrange("p (t n) -> p t n", t=4),
                                                 bias_row[:, g:g + 1, :].to_broadcast([P, 4, P]), ALU.add))
                    uu = uT[:, g, j * HALF:(j + 1) * HALF].rearrange("p (t n) -> p t n", t=4)
                    nc.vector.tensor_tensor(uu, biased[j], uu, ALU.mult).then_inc(G.freed(st), 1)
                elif kind == "h_split":
                    for i, (src, hi, lo) in enumerate(split_parts(st[1])):
                        dve.wait_ge(h_hi_done, (8, 0, 4)[st[1]] + i + 1)
                        nc.vector.tensor_tensor(lo, src, hi.bitcast(F32), ALU.subtract).then_inc(h_lo_done, 1)
                elif kind in ("z", "wide"):
                    if z_index[st] == 0:
                        split_z(0)
                        split_z(1)
                    split_z(z_index[st] + 2)
                elif kind == "o_turn":
                    h = st[1]
                    if h == 0:
                        dve.wait_ge(d_row, 16)
                    dve.wait_ge(*G.drained(("zj", "ga", h, 1)))
                    for j in range(2):
                        bank = take(S2, st + (j,))
                        o = oaT[:, h, j * HALF:(j + 1) * HALF]
                        nc.vector.scalar_tensor_tensor(o, bank[:], gnorm[:, 0:1], o, ALU.mult, ALU.mult).then_inc(S2.freed(st + (j,)), 1)
                elif kind == "o_split":
                    _, b, g = st
                    dve.wait_ge(o_hi_done, 4 * b + g + 1)
                    nc.vector.tensor_tensor(o_lo[b][:, g, :], (oaT, obT, ocT)[b][:, g, :], o_hi[:, g, :].bitcast(F32),
                                            ALU.subtract).then_inc(o_lo_done, 1)
                elif kind == "merge":
                    q = st[1]
                    b, jj = MERGE[q]
                    if q == 0:
                        for i in range(4):
                            split_unit(i)
                    split_unit(3 * q + 4)
                    split_unit(3 * q + 5)
                    for j in range(2):
                        key = ("branch", q, j)
                        bank = take(G, key)
                        dve.wait_ge(*G.drained(("gate", q, j)))
                        if b == 0:
                            nc.vector.tensor_tensor(mT[:, jj, j * HALF:(j + 1) * HALF], bank[:], sig[j], ALU.mult).then_inc(G.freed(key), 1)
                        else:
                            if q > NK:
                                dve.wait_ge(merged_done, 2 * (q - NK) - 1 + j)
                            nc.vector.tensor_tensor(gated[j], bank[:], sig[j], ALU.mult).then_inc(G.freed(key), 1)
                    split_unit(3 * q + 6)
                elif kind == "ada_sum":
                    part = st[1]
                    dve.wait_ge(d_ada, 16 * (part + 1))
                    acc = rows[:, part // 4, part // 2 % 2 * HALF:(part // 2 % 2 + 1) * HALF]
                    for k in range(4):
                        cs = csilu[:, 0, 4 * (part % 2) + k:4 * (part % 2) + k + 1]
                        if k == 0 and part % 2 == 0:
                            step(nc.vector.tensor_scalar(acc, ada_part[:, 0, :], cs, None, ALU.mult))
                        else:
                            step(nc.vector.scalar_tensor_tensor(acc, ada_part[:, k, :], cs, acc, ALU.mult, ALU.add))
                    dve.sem_inc(ada_added, 1)
                    if part % 2:
                        dve.sem_inc(ada_summed, 1)
                elif kind == "ada_rows":
                    nn = st[1]
                    seg, j = nn // 2, nn % 2
                    bank = take(G, st)
                    dve.wait_ge(d_rows, 32 * (nn + 1))
                    dst = rows[:, seg, j * HALF:(j + 1) * HALF]
                    step(nc.vector.tensor_tensor(dst, bank[:], ada_bias, ALU.add))
                    dve.sem_inc(G.freed(st), 1)
                    if seg == 1:
                        dve.sem_inc(rows_done, 1)
                    elif seg == 2:
                        nc.vector.scalar_tensor_tensor(dst, dst, 1.0, norm_row, ALU.add, ALU.mult).then_inc(rows_done, 1)
                    else:
                        nc.vector.tensor_tensor(dst, dst, norm_row, ALU.mult).then_inc(rows_done, 1)
                elif kind == "out_split":
                    u = st[1]
                    dve.wait_ge(out_hi_done, u + 1)
                    cut = (slice(None), u // 2, slice(u % 2 * 4, u % 2 * 4 + 4))
                    nc.vector.tensor_tensor(out_lo[cut], out_raw[u], out_hi[cut].bitcast(F32), ALU.subtract).then_inc(out_lo_done, 1)
                elif kind == "m_split":
                    t = st[1]
                    dve.wait_ge(mt_hi_done, t + 1)
                    nc.vector.tensor_tensor(mt_lo[:, t % 2], mT[:, :, t * P:(t + 1) * P], mt_hi[:, t % 2].bitcast(F32),
                                            ALU.subtract).then_inc(mt_lo_done, 1)
                elif kind == "y_norm":
                    t = st[1]
                    y = ybuf[t % 2]
                    dve.wait_ge(y_ss, t + 1)
                    nc.vector.tensor_scalar(ss[:, 16 + t:17 + t], ss[:, t:t + 1], EPS, None, ALU.add).then_inc(y_ms, 1)
                    dve.wait_ge(rows_done, 8)
                    dve.wait_ge(y_rs, t + 1)
                    nc.vector.scalar_tensor_tensor(y, y, rs[:, t:t + 1], rows[:, 0, :], ALU.mult, ALU.mult).then_inc(yg, 1)
                    dve.wait_ge(d_xre[t % 2], 16 * (t // 2 + 1))
                    dve.wait_ge(yg, t + 1)
                    nc.vector.tensor_tensor(x1[:, t, :], y, xre[t % 2], ALU.add).then_inc(x1_done, 1)
                    dve.wait_ge(x1_ss, t + 1)
                    nc.vector.tensor_scalar(ss[:, 24 + t:25 + t], ss[:, 8 + t:9 + t], EPS, None, ALU.add).then_inc(x1_ms, 1)
                    dve.wait_ge(x1_rs, t + 1)
                    step(nc.vector.scalar_tensor_tensor(y, x1[:, t, :], rs[:, 8 + t:9 + t], rows[:, 2, :], ALU.mult, ALU.mult))
                    nc.vector.tensor_tensor(y, y, rows[:, 1, :], ALU.add).then_inc(h2_done, 1)
                elif kind == "h2_turn":
                    t = st[1]
                    bank = take(G, st + (0,))
                    nc.vector.tensor_copy(h2T[:, 0:4, t * P:(t + 1) * P], bank[:].rearrange("p (k t) -> p k t", k=4)).then_inc(G.freed(st + (0,)), 1)
                elif kind == "router":
                    dve.wait_ge(logits_done, NT)
                    logits = banks[4][:, 0:NT * NE].rearrange("p (t e) -> p t e", e=NE)
                    step(nc.vector.tensor_reduce(pmax[:], logits, AX.X, ALU.max))
                    step(nc.vector.tensor_tensor(prob, logits, pmax[:].rearrange("p (t o) -> p t o", o=1).to_broadcast([P, NT, NE]), ALU.subtract))
                    dve.sem_inc(r_sub, 1)
                    dve.wait_ge(r_exp, 1)
                    step(nc.vector.tensor_reduce(psumm[:], prob, AX.X, ALU.add))
                    step(nc.vector.reciprocal(psumm[:], psumm[:]))
                    nc.vector.tensor_tensor(prob, prob, psumm[:].rearrange("p (t o) -> p t o", o=1).to_broadcast([P, NT, NE]),
                                            ALU.mult).then_inc(r_prob, 1)
                elif kind == "router_turn":
                    for j in range(2):
                        bank = take(G, st + (j,))
                        nc.vector.tensor_copy(aff[:, j * HALF:(j + 1) * HALF], bank[0:NE, :]).then_inc(G.freed(st + (j,)), 1)
                    dve.wait_ge(*G.drained(st + (1,)))
                elif kind == "choose":
                    a, b = aff, aff2
                    for r in range(CAP // 8):
                        v8, i8 = topv[:, 8 * r:8 * r + 8], topi[:, 8 * r:8 * r + 8]
                        step(nc.vector.max(v8, a))
                        nc.vector.max_index(i8, v8, a)
                        step(nc.vector.match_replace(b, v8, a, -1.0))
                        a, b = b, a
                    nc.vector.tensor_copy(topf, topi).then_inc(chosen, 1)
                elif kind == "choose_turn":
                    nc.vector.tensor_copy(gates[:], take(G, st + (0,))[:, 0:NE]).then_inc(G.freed(st + (0,)), 1)
                    nc.vector.tensor_copy(idx[:], take(G, st + (1,))[:, 0:NE]).then_inc(G.freed(st + (1,)), 1)

            dve.wait_ge(G.sems["dve"], G.count["dve"])

            def split(e, u):
                if u in BY_POOL:
                    return
                dve.wait_ge(hi_done, e * UNITS + (u + 1))
                nc.vector.tensor_tensor(wlo[u % PAIRS], raw[u % RAW], whi[u % PAIRS].bitcast(F32), ALU.subtract).then_inc(lo_dve, 1)

            def gathered(n, j):
                dve.wait_ge(tx_hi, n * 2 + (j + 1))
                nc.vector.tensor_tensor(xe_lo[:, 4 * j:4 * j + 4, :], banks[4][:].rearrange("p (k t) -> p k t", k=4),
                                        xe_hi[:, 4 * j:4 * j + 4, :].bitcast(F32), ALU.subtract).then_inc(tx_lo, 1)

            def hidden(e, j):
                dve.wait_ge(th_hi, e * 2 + (j + 1))
                nc.vector.tensor_tensor(ht_lo[:, 4 * j:4 * j + 4, :], banks[6][:].rearrange("p (k t) -> p k t", k=4),
                                        ht_hi[:, 4 * j:4 * j + 4, :].bitcast(F32), ALU.subtract).then_inc(th_lo, 1)

            def gate_b(e, j):
                dve.wait_ge(a_drained, e * 2 + (j + 1))
                dve.wait_ge(used, e * UNITS + (4 * j + 4))
                nc.vector.tensor_tensor(hid[:, j * HALF:(j + 1) * HALF], banks[2 * j + 1][:], sa[j], ALU.mult).then_inc(b_drained, 1)

            def expert(e, before):
                if before is not None:
                    gate_b(before, 1)
                    split(e, 0)
                    split(e, 1)
                    gathered(e, 0)
                    hidden(before, 1)
                    split(e, 2)
                    gathered(e, 1)
                    split(e, 3)
                    split(e, 4)
                    split(e, 5)
                for u in range(6, 9):
                    split(e, u)
                gate_b(e, 0)
                split(e, 9)
                split(e, 10)
                hidden(e, 0)
                split(e, 11)

            gathered(0, 0)
            gathered(0, 1)
            dve.wait_ge(*lo_done(0, PAIRS - 1))
            expert(0, None)
            with dve.Fori(0, NE - 1) as i:
                expert(i + 1, i)
            gate_b(NE - 1, 1)
            hidden(NE - 1, 1)
            for t in range(NT):
                dve.wait_ge(f_ss, t + 1)
                nc.vector.tensor_scalar(ss[:, 24 + t:25 + t], ss[:, 16 + t:17 + t], EPS, None, ALU.add).then_inc(f_ms, 1)
                dve.wait_ge(f_rs, t + 1)
                nc.vector.scalar_tensor_tensor(fin[t], fin[t], rs[:, 16 + t:17 + t], rows[:, 3, :], ALU.mult, ALU.mult).then_inc(f_scaled, 1)
                if t % 2:
                    dve.wait_ge(f_scaled, t + 1)
                    dve.wait_ge(x1_back, 16)
                    nc.vector.tensor_tensor(fin[t], fin[t], x1_again[:, t, :], ALU.add).then_inc(f_out[1], 1)

        @block.gpsimd
        def _(pool):
            def root(dst, src, w):
                return nc.gpsimd.tensor_tensor(dst, src, half_pow[:, 0:w], ALU.pow)

            nc.gpsimd.memset(ident[:], 0.0).then_inc(ident_ready, 1)
            nc.gpsimd.memset(half_pow[:], -0.5).then_inc(pow_ready, 1)
            pool.wait_ge(ident_ready, 1)
            nc.gpsimd.affine_select(out=ident[:], in_=ident[:], compare_op=ALU.not_equal, fill=1.0, base=0,
                                    pattern=[[-1, P]], channel_multiplier=1).then_inc(ident_ready, 1)
            pool.wait_ge(pow_ready, 1)
            n = [0]
            for st in STEPS:
                kind = st[0]
                if kind == "norm_s":
                    g = st[1]
                    nt = NTC if g == 0 else 4
                    pool.wait_ge(x_ms, g + 1)
                    root(rs[:, 4 * g:4 * g + nt], ss[:, 16 + 4 * g:16 + 4 * g + nt], nt).then_inc(x_rs, 1)
                elif kind == "prepare" and st[2] == 1:
                    h = st[1]
                    pool.wait_ge(kc_ready, 2 * (h + 1))
                    for l in range(8):
                        m = 1 << l
                        nb = TC // (2 * m)
                        src, dst = Fc[:, l % 2], Fc[:, 1 - l % 2]
                        pair = src[:, :, 0:2 * nb].rearrange("p a (b two) -> p a b two", two=2)
                        kf = Kc[:, 0, :].rearrange("p (b two m) -> p b two m", two=2, m=m)
                        kb = Kc[:, 1, :].rearrange("p (b two m) -> p b two m", two=2, m=m)
                        nc.gpsimd.tensor_tensor(kf[:, :, 0, :], kf[:, :, 0, :], pair[:, 0, :, 1:2].to_broadcast([P, nb, m]), ALU.mult)
                        ins = nc.gpsimd.tensor_tensor(kb[:, :, 1, :], kb[:, :, 1, :], pair[:, 1, :, 0:1].to_broadcast([P, nb, m]), ALU.mult)
                        if l < 7:
                            ins = nc.gpsimd.tensor_tensor(dst[:, :, 0:nb], pair[:, :, :, 0], pair[:, :, :, 1], ALU.mult)
                            ins.then_inc(pstep, 1)
                            n[0] += 1
                            pool.wait_ge(pstep, n[0])
                        else:
                            ins.then_inc(ctx_done, 1)
                elif kind == "out":
                    h = st[1]
                    pool.wait_ge(o_ms, h + 1)
                    root(rs[:, 32:40], ss[:, 40:48], 8).then_inc(o_rs, 1)
                elif kind == "vv_norm":
                    pool.wait_ge(v_ms, 1)
                    root(rs[:, 0:32], ss[:, 0:32], 32).then_inc(v_rs, 1)
                elif kind == "merge" and st[1] >= NK:
                    q = st[1]
                    for j in range(2):
                        pool.wait_ge(*G.drained(("branch", q, j)))
                        mm = mT[:, MERGE[q][1], j * HALF:(j + 1) * HALF]
                        nc.gpsimd.tensor_tensor(mm, mm, gated[j], ALU.add).then_inc(merged_done, 1)
                elif kind == "mix" and st[1:] == (0, 0):
                    nc.gpsimd.memset(ones[:], 1.0).then_inc(ones_ready, 1)
                elif kind == "y_norm":
                    t = st[1]
                    pool.wait_ge(y_ms, t + 1)
                    root(rs[:, t:t + 1], ss[:, 16 + t:17 + t], 1).then_inc(y_rs, 1)
                    pool.wait_ge(x1_ms, t + 1)
                    root(rs[:, 8 + t:9 + t], ss[:, 24 + t:25 + t], 1).then_inc(x1_rs, 1)

            for u in range(PAIRS):
                pool.wait_ge(hi_done, u + 1)
                nc.gpsimd.tensor_tensor(wlo[u], raw[u % RAW], whi[u].bitcast(F32), ALU.subtract).then_inc(lo_done(0, u)[0], 1)
            pool.wait_ge(G.sems["dve"], G.count["dve"])
            for j in range(2):
                pool.wait_ge(d_h2[j], 8 * NT)
            pool.wait_ge(d_zero, 16 * NT)
            pool.sem_inc(added, 1)

            def wait(semaphore, value):
                pool.wait_ge(semaphore, value)
                pool.sem_inc(tick, 1)

            def gather(n):
                if not isinstance(n, int) or n:
                    wait(tx_full, n * 2)
                nc.gpsimd.tensor_copy(icur[:, :], idx[:, bass.ds(n, 1)]).then_inc(cur_done, 1)
                wait(cur_done, n + 1)
                pool.indirect_dma_start(xg, None, h2_dram[:, :], bass.IndirectOffsetOnAxis(ap=icur[:, 0:1], axis=0),
                                        bounds_check=T - 1).then_inc(xg_full, 16)

            def gate_of(e):
                nc.gpsimd.tensor_copy(icur2[:, :], idx[:, bass.ds(e, 1)])
                nc.gpsimd.tensor_copy(gcur[:, :], gates[:, bass.ds(e, 1)]).then_inc(cur_g, 1)

            def scatter(e):
                wait(cur_g, e + 1)
                wait(y_drained, e * 2 + 4)
                pool.indirect_dma_start(moe_dram[:, :], bass.IndirectOffsetOnAxis(ap=icur2[:, 0:1], axis=0), yb, None,
                                        compute_op=ALU.add, bounds_check=T - 1).then_inc(sc_done, 16)

            def scattered(e):
                wait(sc_done, e * 16 + 16)
                pool.sem_inc(added, 1)

            def split(e, u):
                wait(hi_done, e * UNITS + (u + 1))
                nc.gpsimd.tensor_tensor(wlo[u % PAIRS], raw[u % RAW], whi[u % PAIRS].bitcast(F32), ALU.subtract).then_inc(lo_pool, 1)

            def expert(e, before, last=False):
                for i, u in enumerate(BY_POOL):
                    if before is not None or u >= PAIRS:
                        split(e, u)
                    if i == 0 and not last:
                        gather(e + 1)
                    if i == 1 and before is not None:
                        scatter(before)
                    if i == 2:
                        if before is not None:
                            scattered(before)
                        gate_of(e)

            gather(0)
            expert(0, None)
            with pool.Fori(0, NE - 2) as e:
                expert(e + 1, e)
            expert(NE - 1, NE - 2, last=True)
            scatter(NE - 1)
            scattered(NE - 1)
            for t in range(NT):
                pool.wait_ge(f_ms, t + 1)
                root(rs[:, 16 + t:17 + t], ss[:, 24 + t:25 + t], 1).then_inc(f_rs, 1)
                if t % 2:
                    pool.wait_ge(f_scaled, t)
                    pool.wait_ge(x1_back, 16)
                    nc.gpsimd.tensor_tensor(fin[t - 1], fin[t - 1], x1_again[:, t - 1, :], ALU.add).then_inc(f_out[0], 1)


_INS = ["x", "c", "ctx", "c_ctx", "ada_w", "ada_b", "norm_w", "w_in", "hgrn_lb_raw", "hgrn_gnorm_w", "sgu_w", "sgu_b",
        "sgu_norm_w", "w_branch", "w_out", "router_w", "exp_w13", "exp_w2"]


def kernel(**inputs):
    import concourse.bacc as bacc
    from concourse.bass_utils import run_bass_kernel_spmd

    nc = bacc.Bacc("TRN2", target_bir_lowering=False, num_devices=1)
    arrays, args = {}, []
    tokens, channels = dft_tables()
    extra = dict(token_dft=tokens, channel_dft=channels, level_masks=level_masks())
    for name in _INS + list(extra):
        a = np.ascontiguousarray(inputs[name] if name in inputs else extra[name])
        arrays[f"in_{name}"] = a
        args.append(nc.dram_tensor(f"in_{name}", a.shape, mybir.dt.from_np(a.dtype), kind="ExternalInput").ap())
    out = nc.dram_tensor("out", (1, T, D), F32, kind="ExternalOutput").ap()
    h2 = nc.dram_tensor("h2", (T, D), F32, kind="Internal").ap()
    moe = nc.dram_tensor("moe", (T, D), F32, kind="Internal").ap()
    x1 = nc.dram_tensor("x1", (T, D), F32, kind="Internal").ap()
    build(nc, *args, out, h2, moe, x1)
    r = run_bass_kernel_spmd(nc, [arrays], core_ids=[0])
    return r.results[0]["out"]
```
